# Optimizing a Trainium2 kernel written in Bass

```python
import math
import jax
import jax.numpy as jnp
from jax import lax
import numpy as np

D_MODEL = 1024
BATCH = 1
SEQ = 512
DEPTH = 2

N_HEADS = 16
HEAD_DIM = 64
A_HEADS = 8
B_HEADS = 8
MOBA_BLOCK = 256
MOBA_TOPK = 3
MOBA_Q_CHUNK = 64
IDX_HEADS = 16
IDX_DIM = 64
DSA_TOPK_MAX = 256
DSA_Q_CHUNK = 128
DILATED_PATTERNS = ((128, 1), (512, 4), (2048, 16))
REL_BUCKETS = 32
REL_MAX_DIST = 128
D_FF = 2816
CONV_WIDTH = 3
RMS_EPS = 1e-6


def rmsnorm(x, g):
    x32 = x.astype(jnp.float32)
    y = x32 * lax.rsqrt(jnp.mean(x32 * x32, axis=-1, keepdims=True) + RMS_EPS)
    return (y * g.astype(jnp.float32)).astype(x.dtype)

def t5_bucket(dist):
    n = jnp.maximum(dist, 0)
    max_exact = REL_BUCKETS // 2
    nf = jnp.maximum(n, max_exact).astype(jnp.float32)
    large = max_exact + (jnp.log(nf / max_exact) / math.log(REL_MAX_DIST / max_exact)
                         * (REL_BUCKETS - max_exact)).astype(jnp.int32)
    large = jnp.minimum(large, REL_BUCKETS - 1)
    return jnp.where(n < max_exact, n, large)

def split_cols(a, sizes):
    out, off = [], 0
    for s in sizes:
        out.append(a[..., off:off + s])
        off += s
    return out

def moba_attention(q, k, v, table_hk):
    B, H, S, Dh = q.shape
    nb = -(-S // MOBA_BLOCK)
    pad = nb * MOBA_BLOCK - S
    kb = jnp.pad(k, ((0, 0), (0, 0), (0, pad), (0, 0))).reshape(B, H, nb, MOBA_BLOCK, Dh)
    vb = jnp.pad(v, ((0, 0), (0, 0), (0, pad), (0, 0))).reshape(B, H, nb, MOBA_BLOCK, Dh)
    kmean = jnp.mean(kb.astype(jnp.float32), axis=3).astype(k.dtype)
    n_sel = min(MOBA_TOPK, nb - 1)
    scale = Dh ** -0.5
    nq = S // MOBA_Q_CHUNK
    qc = jnp.moveaxis(q.reshape(B, H, nq, MOBA_Q_CHUNK, Dh), 2, 0)
    bi = jnp.arange(B)[:, None, None, None]
    hi = jnp.arange(H)[None, :, None, None]
    offs = jnp.arange(MOBA_BLOCK)
    blk_ids = jnp.arange(nb)

    def chunk(args):
        qi, c = args
        q0 = c * MOBA_Q_CHUNK
        t = q0 + jnp.arange(MOBA_Q_CHUNK)
        own = q0 // MOBA_BLOCK
        k_own = lax.dynamic_index_in_dim(kb, own, axis=2, keepdims=False)
        v_own = lax.dynamic_index_in_dim(vb, own, axis=2, keepdims=False)
        d_own = t[:, None] - (own * MOBA_BLOCK + offs)[None, :]
        l_own = jnp.einsum('bhqd,bhkd->bhqk', qi, k_own).astype(jnp.float32) * scale
        l_own = jnp.where(d_own >= 0, l_own + table_hk[:, t5_bucket(d_own)], -jnp.inf)
        if n_sel == 0:
            p = jax.nn.softmax(l_own, axis=-1).astype(v.dtype)
            return jnp.einsum('bhqk,bhkd->bhqd', p, v_own)
        gate = jnp.einsum('bhqd,bhnd->bhqn', qi, kmean).astype(jnp.float32)
        gate = jnp.where(blk_ids < own, gate, -jnp.inf)
        _, sel = lax.top_k(gate, n_sel)
        k_sel = kb[bi, hi, sel]
        v_sel = vb[bi, hi, sel]
        d_sel = t[None, None, :, None, None] - (sel[..., None] * MOBA_BLOCK + offs)
        l_sel = jnp.einsum('bhqd,bhqnkd->bhqnk', qi, k_sel).astype(jnp.float32) * scale
        l_sel = l_sel + table_hk[hi[..., None], t5_bucket(d_sel)]
        l_sel = jnp.where((sel < own)[..., None], l_sel, -jnp.inf)
        n_k = n_sel * MOBA_BLOCK
        logits = jnp.concatenate([l_sel.reshape(B, H, MOBA_Q_CHUNK, n_k), l_own], axis=-1)
        p = jax.nn.softmax(logits, axis=-1).astype(v.dtype)
        p_sel = p[..., :n_k].reshape(B, H, MOBA_Q_CHUNK, n_sel, MOBA_BLOCK)
        p_own = p[..., n_k:]
        return (jnp.einsum('bhqnk,bhqnkd->bhqd', p_sel, v_sel)
                + jnp.einsum('bhqk,bhkd->bhqd', p_own, v_own))

    out = lax.map(chunk, (qc, jnp.arange(nq, dtype=jnp.int32)))
    return jnp.moveaxis(out, 0, 2).reshape(B, H, S, Dh)

def dsa_attention(q, k, v, q_idx, k_idx, w_idx, table_hk):
    B, S, H, Dh = q.shape
    n_keep = min(DSA_TOPK_MAX, S // 4)
    nq = S // DSA_Q_CHUNK
    scale = Dh ** -0.5
    key_pos = jnp.arange(S)
    bi = jnp.arange(B)[:, None, None]

    def chunkify(a):
        return jnp.moveaxis(a.reshape((B, nq, DSA_Q_CHUNK) + a.shape[2:]), 1, 0)

    def chunk(args):
        qi, qii, wi, c = args
        t = c * DSA_Q_CHUNK + jnp.arange(DSA_Q_CHUNK)
        rel = jax.nn.relu(jnp.einsum('bqhd,bsd->bqhs', qii, k_idx) * (IDX_DIM ** -0.5))
        score = jnp.einsum('bqhs,bqh->bqs', rel, wi).astype(jnp.float32)
        score = jnp.where(key_pos[None, :] <= t[:, None], score, -jnp.inf)
        _, sel = lax.top_k(score, n_keep)
        k_sel = k[bi, sel]
        v_sel = v[bi, sel]
        d = t[None, :, None] - sel
        logits = jnp.einsum('bqhd,bqkhd->bhqk', qi, k_sel).astype(jnp.float32) * scale
        logits = logits + jnp.moveaxis(table_hk[:, t5_bucket(d)], 0, 1)
        logits = jnp.where((d >= 0)[:, None], logits, -jnp.inf)
        p = jax.nn.softmax(logits, axis=-1).astype(v.dtype)
        return jnp.einsum('bhqk,bqkhd->bqhd', p, v_sel)

    out = lax.map(chunk, (chunkify(q), chunkify(q_idx), chunkify(w_idx),
                          jnp.arange(nq, dtype=jnp.int32)))
    return jnp.moveaxis(out, 0, 1).reshape(B, S, H, Dh)

def dilated_branch(q, k, v, table_hk, window, dilation):
    B, H, S, Dh = q.shape
    w_sub = window // dilation
    bb = w_sub
    n = S // dilation
    nbk = -(-n // bb)
    npad = nbk * bb
    scale = Dh ** -0.5

    def to_sub(a):
        a = jnp.swapaxes(a.reshape(B, H, n, dilation, Dh), 2, 3)
        return jnp.pad(a, ((0, 0), (0, 0), (0, 0), (0, npad - n), (0, 0)))

    def band(a):
        ap = jnp.pad(a, ((0, 0), (0, 0), (0, 0), (bb, 0), (0, 0)))
        prev = ap[:, :, :, :npad].reshape(B, H, dilation, nbk, bb, Dh)
        cur = a.reshape(B, H, dilation, nbk, bb, Dh)
        return jnp.concatenate([prev, cur], axis=4)

    qs = to_sub(q).reshape(B, H, dilation, nbk, bb, Dh)
    kband = band(to_sub(k))
    vband = band(to_sub(v))
    logits = jnp.einsum('bhrnqd,bhrnkd->bhrnqk', qs, kband).astype(jnp.float32) * scale
    a_i = jnp.arange(bb)
    m_i = jnp.arange(2 * bb)
    di = a_i[:, None] + bb - m_i[None, :]
    band_ok = (di >= 0) & (di <= w_sub)
    j_idx = jnp.arange(nbk)[:, None] * bb - bb + m_i[None, :]
    mask = band_ok[None] & (j_idx >= 0)[:, None, :]
    bias = table_hk[:, t5_bucket(di * dilation)][:, None, None]
    logits = jnp.where(mask, logits + bias, -jnp.inf)
    mx = jnp.max(logits, axis=-1, keepdims=True)
    e = jnp.exp(logits - mx)
    den = jnp.sum(e, axis=-1, keepdims=True)
    o = jnp.einsum('bhrnqk,bhrnkd->bhrnqd', (e / den).astype(v.dtype), vband)
    lse = (mx + jnp.log(den))[..., 0]
    o = jnp.swapaxes(o.reshape(B, H, dilation, npad, Dh)[:, :, :, :n], 2, 3).reshape(B, H, S, Dh)
    lse = jnp.swapaxes(lse.reshape(B, H, dilation, npad)[:, :, :, :n], 2, 3).reshape(B, H, S)
    return o, lse

def dilated_mixture(q, k, v, table_hk):
    outs, lses = [], []
    for window, dilation in DILATED_PATTERNS:
        o, l = dilated_branch(q, k, v, table_hk, window, dilation)
        outs.append(o)
        lses.append(l)
    alpha = jax.nn.softmax(jnp.stack(lses, axis=0), axis=0)
    return jnp.einsum('pbhs,pbhsd->bhsd', alpha.astype(v.dtype), jnp.stack(outs, axis=0))

def conv_ffn(h, w_up, conv_w, conv_b, w_down):
    S = h.shape[1]
    u = h @ w_up
    up = jnp.pad(u, ((0, 0), (CONV_WIDTH - 1, 0), (0, 0)))
    c = conv_b
    for j in range(CONV_WIDTH):
        c = c + conv_w[j] * up[:, j:j + S]
    val, gate = jnp.split(c, 2, axis=-1)
    return (jax.nn.silu(gate) * val) @ w_down

def first_inputs(seed: int = 0) -> dict:
    key = jax.random.key(seed)
    ks = jax.random.split(key, 13)
    n_even = (DEPTH + 1) // 2
    n_odd = DEPTH // 2
    even_in = 3 * A_HEADS * HEAD_DIM + 3 * B_HEADS * HEAD_DIM + IDX_HEADS * IDX_DIM + IDX_DIM + IDX_HEADS
    odd_in = 3 * N_HEADS * HEAD_DIM
    mix = N_HEADS * HEAD_DIM

    def nrm(k, shape, s):
        return jax.random.normal(k, shape, jnp.float32) * s

    return {
        'x': nrm(ks[0], (BATCH, SEQ, D_MODEL), 1.0),
        'w_in_even': nrm(ks[1], (n_even, D_MODEL, even_in), D_MODEL ** -0.5),
        'idx_k_norm': 1.0 + nrm(ks[2], (n_even, IDX_DIM), 0.02),
        'w_in_odd': nrm(ks[3], (n_odd, D_MODEL, odd_in), D_MODEL ** -0.5),
        'w_o': nrm(ks[4], (DEPTH, mix, D_MODEL), mix ** -0.5),
        'rel_bias': nrm(ks[5], (REL_BUCKETS, N_HEADS), 0.2),
        'attn_norm': 1.0 + nrm(ks[6], (DEPTH, D_MODEL), 0.02),
        'ffn_norm': 1.0 + nrm(ks[7], (DEPTH, D_MODEL), 0.02),
        'w_up': nrm(ks[8], (DEPTH, D_MODEL, 2 * D_FF), D_MODEL ** -0.5),
        'conv_w': nrm(ks[9], (DEPTH, CONV_WIDTH, 2 * D_FF), CONV_WIDTH ** -0.5),
        'conv_b': nrm(ks[10], (DEPTH, 2 * D_FF), 0.02),
        'w_down': nrm(ks[11], (DEPTH, D_FF, D_MODEL), D_FF ** -0.5),
        'final_norm': 1.0 + nrm(ks[12], (D_MODEL,), 0.02),
    }

def first_block(x, w_in_even, idx_k_norm, w_in_odd, w_o, rel_bias, attn_norm, ffn_norm,
              w_up, conv_w, conv_b, w_down, final_norm):
    B, S, _ = x.shape
    mix = N_HEADS * HEAD_DIM
    sizes_even = [A_HEADS * HEAD_DIM] * 3 + [B_HEADS * HEAD_DIM] * 3 + [IDX_HEADS * IDX_DIM, IDX_DIM, IDX_HEADS]
    sizes_odd = [N_HEADS * HEAD_DIM] * 3
    table_a = rel_bias[:, :A_HEADS].T
    table_b = rel_bias[:, A_HEADS:A_HEADS + B_HEADS].T
    table_c = rel_bias.T
    for layer in range(DEPTH):
        h = rmsnorm(x, attn_norm[layer])
        if layer % 2 == 0:
            j = layer // 2
            qa, ka, va, qb, kb, vb, qi, ki, wi = split_cols(h @ w_in_even[j], sizes_even)
            qa, ka, va = (jnp.swapaxes(a.reshape(B, S, A_HEADS, HEAD_DIM), 1, 2) for a in (qa, ka, va))
            o_a = jnp.swapaxes(moba_attention(qa, ka, va, table_a), 1, 2)
            qb, kb, vb = (a.reshape(B, S, B_HEADS, HEAD_DIM) for a in (qb, kb, vb))
            o_b = dsa_attention(qb, kb, vb,
                                qi.reshape(B, S, IDX_HEADS, IDX_DIM),
                                rmsnorm(ki, idx_k_norm[j]),
                                wi * (IDX_HEADS ** -0.5),
                                table_b)
            mixed = jnp.concatenate([o_a, o_b], axis=2).reshape(B, S, mix)
        else:
            j = layer // 2
            qc, kc, vc = (jnp.swapaxes(a.reshape(B, S, N_HEADS, HEAD_DIM), 1, 2)
                          for a in split_cols(h @ w_in_odd[j], sizes_odd))
            o_c = dilated_mixture(qc, kc, vc, table_c)
            mixed = jnp.swapaxes(o_c, 1, 2).reshape(B, S, mix)
        x = x + mixed @ w_o[layer]
        h = rmsnorm(x, ffn_norm[layer])
        x = x + conv_ffn(h, w_up[layer], conv_w[layer], conv_b[layer], w_down[layer])
    return rmsnorm(x, final_norm)


DEPTH_2 = 1

CTX_LEN = 256
GRID_W = 64
BRANCH_WIDTH = 512
N_BRANCH = 3
A_KV_HEADS = 2
WINDOW = 128
B_KV_HEADS = 2
C_HEADS = 4
C_DK = 128
C_DV = 128
CHUNK = 64
BLOCK = 128
CONV_W = 3
ROPE_THETA = 10000.0
AXIS_ROPE_DIM = HEAD_DIM // 2
N_MOD = 6
EPS = 1e-6
NEG_BIG = -1e30
PROJ_SIZES = (A_HEADS * HEAD_DIM, A_KV_HEADS * HEAD_DIM, A_KV_HEADS * HEAD_DIM,
              B_HEADS * HEAD_DIM, B_KV_HEADS * HEAD_DIM, B_KV_HEADS * HEAD_DIM,
              C_HEADS * C_DK, C_HEADS * C_DK, C_HEADS * C_DK, C_HEADS * C_DV, C_HEADS * C_DV,
              N_BRANCH * D_MODEL)
PROJ_WIDTH = sum(PROJ_SIZES)


def rms_norm(t, g):
    tf = t.astype(jnp.float32)
    y = tf * lax.rsqrt(jnp.mean(tf * tf, axis=-1, keepdims=True) + EPS)
    return (y * g.astype(jnp.float32)).astype(t.dtype)

def axial_rope(n):
    rows = n // GRID_W
    row = jnp.repeat(jnp.arange(rows), GRID_W).astype(jnp.float32)
    col = jnp.tile(jnp.arange(GRID_W), rows).astype(jnp.float32)
    inv = ROPE_THETA ** (-jnp.arange(0, AXIS_ROPE_DIM, 2, dtype=jnp.float32) / AXIS_ROPE_DIM)
    ang = jnp.concatenate([row[:, None] * inv, col[:, None] * inv], axis=-1)
    return jnp.cos(ang), jnp.sin(ang)

def apply_rope(t, cos, sin):
    t1, t2 = t[..., 0::2], t[..., 1::2]
    c = cos[None, :, None, :].astype(t.dtype)
    s = sin[None, :, None, :].astype(t.dtype)
    return jnp.stack([t1 * c - t2 * s, t1 * s + t2 * c], axis=-1).reshape(t.shape)

def features(h, w_in, qn, kn, rope):
    B_, L, _ = h.shape
    split_at = np.cumsum(PROJ_SIZES)[:-1].tolist()
    aq, ak, av, bq, bk, bv, cq, cf, cb, ci, cg, gates = jnp.split(h @ w_in, split_at, axis=-1)
    heads = lambda t, n: t.reshape(B_, L, n, HEAD_DIM)
    aq, ak, av = heads(aq, A_HEADS), heads(ak, A_KV_HEADS), heads(av, A_KV_HEADS)
    bq = rms_norm(heads(bq, B_HEADS), qn)
    bk = rms_norm(heads(bk, B_KV_HEADS), kn)
    bv = heads(bv, B_KV_HEADS)
    if rope is not None:
        cos, sin = rope
        aq, ak, bq, bk = [apply_rope(t, cos, sin) for t in (aq, ak, bq, bk)]
    return aq, ak, av, bq, bk, bv, cq, cf, cb, ci, cg, gates

def dense_attn(q, k, v, sink=None):
    B_, Lq, HQ, hd = q.shape
    KV = k.shape[2]
    G = HQ // KV
    s = jnp.einsum('bqkgd,bjkd->bkgqj', q.reshape(B_, Lq, KV, G, hd), k).astype(jnp.float32) * hd ** -0.5
    if sink is not None:
        s_sink = jnp.broadcast_to(sink.astype(jnp.float32).reshape(1, KV, G, 1, 1), s.shape[:-1] + (1,))
        s = jnp.concatenate([s, s_sink], axis=-1)
    p = jax.nn.softmax(s, axis=-1)[..., :k.shape[1]].astype(v.dtype)
    return jnp.einsum('bkgqj,bjkd->bqkgd', p, v).reshape(B_, Lq, HQ * hd)

def window_attn(q, k, v, ck, cv, sink):
    B_, S, HQ, hd = q.shape
    KV = k.shape[2]
    G = HQ // KV
    nb = S // BLOCK
    n_ctx = ck.shape[1]
    qb = q.reshape(B_, nb, BLOCK, KV, G, hd)

    def band(t):
        tp = jnp.pad(t, ((0, 0), (BLOCK, BLOCK), (0, 0), (0, 0))).reshape(B_, nb + 2, BLOCK, KV, hd)
        return jnp.concatenate([tp[:, :-2], tp[:, 1:-1], tp[:, 2:]], axis=2)

    kb, vb = band(k), band(v)
    scale = hd ** -0.5
    s_loc = jnp.einsum('bnqkgd,bnjkd->bkgnqj', qb, kb).astype(jnp.float32) * scale
    blk = jnp.arange(nb)[:, None, None]
    qpos = blk * BLOCK + jnp.arange(BLOCK)[None, :, None]
    kpos = (blk - 1) * BLOCK + jnp.arange(3 * BLOCK)[None, None, :]
    valid = (jnp.abs(kpos - qpos) <= WINDOW) & (kpos >= 0) & (kpos < S)
    s_loc = jnp.where(valid, s_loc, NEG_BIG)
    s_ctx = jnp.einsum('bnqkgd,bjkd->bkgnqj', qb, ck).astype(jnp.float32) * scale
    s_sink = jnp.broadcast_to(sink.astype(jnp.float32).reshape(1, KV, G, 1, 1, 1), s_ctx.shape[:-1] + (1,))
    p = jax.nn.softmax(jnp.concatenate([s_ctx, s_loc, s_sink], axis=-1), axis=-1).astype(v.dtype)
    o = (jnp.einsum('bkgnqj,bjkd->bnqkgd', p[..., :n_ctx], cv)
         + jnp.einsum('bkgnqj,bnjkd->bnqkgd', p[..., n_ctx:n_ctx + 3 * BLOCK], vb))
    return o.reshape(B_, S, HQ * hd)

def global_attn(q, k, v, ck, cv):
    B_, S, HQ, hd = q.shape
    nb = S // BLOCK
    k_all = jnp.concatenate([ck, k], axis=1)
    v_all = jnp.concatenate([cv, v], axis=1)
    qb = jnp.moveaxis(q.reshape(B_, nb, BLOCK, HQ, hd), 1, 0)
    o = lax.map(lambda qblk: dense_attn(qblk, k_all, v_all), qb)
    return jnp.moveaxis(o, 0, 1).reshape(B_, S, HQ * hd)

def layer_lower_bounds(raw):
    p = jax.nn.softmax(raw.astype(jnp.float32), axis=0)
    return jnp.clip(jnp.cumsum(p, axis=0) - p[0], 0.0, 1.0)

def hgrn_forget(z, lb):
    log_f = jax.nn.log_sigmoid(z) + jnp.log1p(lb * jnp.exp(-z))
    k = (1.0 - lb) * jax.nn.sigmoid(-z)
    return k, log_f

def gla_chunk_scan(q, k, v, log_f, s0):
    B_, L, H, _ = q.shape
    nc = L // CHUNK
    to_chunks = lambda t: t.reshape(B_, nc, CHUNK, H, t.shape[-1]).transpose(1, 0, 3, 2, 4)
    tri = jnp.tril(jnp.ones((CHUNK, CHUNK), dtype=bool))[:, :, None]

    def step(s, inp):
        qi, ki, vi, fi = inp
        a = jnp.cumsum(fi, axis=2)
        o_inter = jnp.einsum('bhtd,bhde->bhte', qi * jnp.exp(a), s)
        diff = a[:, :, :, None, :] - a[:, :, None, :, :]
        decay = jnp.exp(jnp.where(tri, diff, NEG_BIG))
        scores = jnp.einsum('bhtd,bhjd,bhtjd->bhtj', qi, ki, decay)
        o_intra = jnp.einsum('bhtj,bhje->bhte', scores, vi)
        a_last = a[:, :, -1, :]
        s_new = (jnp.exp(a_last)[..., None] * s
                 + jnp.einsum('bhjd,bhje->bhde', ki * jnp.exp(a_last[:, :, None, :] - a), vi))
        return s_new, o_inter + o_intra

    s_fin, o = lax.scan(step, s0, (to_chunks(q), to_chunks(k), to_chunks(v), to_chunks(log_f)))
    return o.transpose(1, 0, 3, 2, 4).reshape(B_, L, H, v.shape[-1]), s_fin

def hgrn2_bidir(cq, cf, cb, ci, cg, lb_f, lb_b, gn, s0_f, s0_b):
    B_, L = cq.shape[:2]
    q = jax.nn.silu(cq.astype(jnp.float32)).reshape(B_, L, C_HEADS, C_DK)
    v = ci.astype(jnp.float32).reshape(B_, L, C_HEADS, C_DV)
    k_f, lf_f = hgrn_forget(cf.astype(jnp.float32).reshape(B_, L, C_HEADS, C_DK), lb_f.reshape(C_HEADS, C_DK))
    k_b, lf_b = hgrn_forget(cb.astype(jnp.float32).reshape(B_, L, C_HEADS, C_DK), lb_b.reshape(C_HEADS, C_DK))
    rev = lambda t: jnp.flip(t, axis=1)
    o_f, s_f = gla_chunk_scan(q, k_f, v, lf_f, s0_f)
    o_b, s_b = gla_chunk_scan(rev(q), rev(k_b), rev(v), rev(lf_b), s0_b)
    o = rms_norm(o_f + rev(o_b), gn) * jax.nn.silu(cg.astype(jnp.float32)).reshape(B_, L, C_HEADS, C_DV)
    return o.reshape(B_, L, C_HEADS * C_DV).astype(cq.dtype), s_f, s_b

def merge_branches(ya, yb, yc, gates, w_branch, w_out):
    B_, L = ya.shape[:2]
    ys = jnp.stack([ya, yb, yc], axis=2)
    up = jnp.einsum('blnw,nwd->blnd', ys, w_branch)
    g = jax.nn.sigmoid(gates.reshape(B_, L, N_BRANCH, -1))
    return jnp.sum(g * up, axis=2) @ w_out

def dwconv(u, w, b):
    y = lax.conv_general_dilated(u, w[:, None, :], window_strides=(1,),
                                 padding=((CONV_W // 2, CONV_W // 2),),
                                 dimension_numbers=('NWC', 'WIO', 'NWC'),
                                 feature_group_count=u.shape[-1])
    return y + b

def conv_ffn_2(h, w_up, w_dw, b_dw, w_down):
    a, g = jnp.split(dwconv(h @ w_up, w_dw, b_dw), 2, axis=-1)
    return (a * jax.nn.silu(g)) @ w_down

def second_inputs(seed: int = 0) -> dict:
    key = jax.random.key(seed)
    ks = jax.random.split(key, 22)
    nrm = lambda k, shape, s: jax.random.normal(k, shape, jnp.float32) * s
    L = DEPTH_2
    return {
        'x': nrm(ks[0], (BATCH, SEQ, D_MODEL), 1.0),
        'c': nrm(ks[1], (BATCH, D_MODEL), 1.0),
        'ctx': nrm(ks[2], (BATCH, CTX_LEN, D_MODEL), 1.0),
        'c_ctx': nrm(ks[3], (D_MODEL,), 1.0),
        'w_mod': nrm(ks[4], (L, D_MODEL, N_MOD * D_MODEL), 0.5 * D_MODEL ** -0.5),
        'b_mod': nrm(ks[5], (L, N_MOD * D_MODEL), 0.02),
        'norm_mix': 1.0 + nrm(ks[6], (L, D_MODEL), 0.05),
        'norm_ffn': 1.0 + nrm(ks[7], (L, D_MODEL), 0.05),
        'w_in': nrm(ks[8], (L, D_MODEL, PROJ_WIDTH), D_MODEL ** -0.5),
        'sink_a': nrm(ks[9], (L, A_HEADS), 0.5),
        'qn_b': 1.0 + nrm(ks[10], (L, HEAD_DIM), 0.05),
        'kn_b': 1.0 + nrm(ks[11], (L, HEAD_DIM), 0.05),
        'lb_fwd': nrm(ks[12], (L, C_HEADS * C_DK), 1.0),
        'lb_bwd': nrm(ks[13], (L, C_HEADS * C_DK), 1.0),
        'gn_c': 1.0 + nrm(ks[14], (L, C_DV), 0.05),
        'w_branch': nrm(ks[15], (L, N_BRANCH, BRANCH_WIDTH, D_MODEL), BRANCH_WIDTH ** -0.5),
        'w_out': nrm(ks[16], (L, D_MODEL, D_MODEL), D_MODEL ** -0.5),
        'w_up': nrm(ks[17], (L, D_MODEL, 2 * D_FF), D_MODEL ** -0.5),
        'w_dw': nrm(ks[18], (L, CONV_W, 2 * D_FF), CONV_W ** -0.5),
        'b_dw': nrm(ks[19], (L, 2 * D_FF), 0.02),
        'w_down': nrm(ks[20], (L, D_FF, D_MODEL), D_FF ** -0.5),
        'norm_final': 1.0 + nrm(ks[21], (D_MODEL,), 0.05),
    }

def second_block(x, c, ctx, c_ctx, w_mod, b_mod, norm_mix, norm_ffn, w_in, sink_a, qn_b, kn_b,
              lb_fwd, lb_bwd, gn_c, w_branch, w_out, w_up, w_dw, b_dw, w_down, norm_final):
    B_, S, D = x.shape
    rope = axial_rope(S)
    lbf = layer_lower_bounds(lb_fwd)
    lbb = layer_lower_bounds(lb_bwd)
    s0 = jnp.zeros((B_, C_HEADS, C_DK, C_DV), jnp.float32)
    for l in range(DEPTH_2):
        last = l == DEPTH_2 - 1
        m_lat = (jax.nn.silu(c) @ w_mod[l] + b_mod[l]).reshape(B_, 1, N_MOD, D)
        m_ctx = (jax.nn.silu(c_ctx) @ w_mod[l] + b_mod[l]).reshape(N_MOD, D)

        h_lat = rms_norm(x, norm_mix[l]) * (1.0 + m_lat[:, :, 1]) + m_lat[:, :, 0]
        h_ctx = rms_norm(ctx, norm_mix[l]) * (1.0 + m_ctx[1]) + m_ctx[0]
        aq, ak, av, bq, bk, bv, cq, cf, cb, ci, cg, gates = features(h_lat, w_in[l], qn_b[l], kn_b[l], rope)
        caq, cak, cav, cbq, cbk, cbv, ccq, ccf, ccb, cci, ccg, cgates = features(h_ctx, w_in[l], qn_b[l], kn_b[l], None)

        yc_ctx, s_f, s_b = hgrn2_bidir(ccq, ccf, ccb, cci, ccg, lbf[l], lbb[l], gn_c[l], s0, s0)
        yc = hgrn2_bidir(cq, cf, cb, ci, cg, lbf[l], lbb[l], gn_c[l], s_f, s_b)[0]
        ya = window_attn(aq, ak, av, cak, cav, sink_a[l])
        yb = global_attn(bq, bk, bv, cbk, cbv)
        x_mix = x + m_lat[:, :, 2] * merge_branches(ya, yb, yc, gates, w_branch[l], w_out[l])

        h = rms_norm(x_mix, norm_ffn[l]) * (1.0 + m_lat[:, :, 4]) + m_lat[:, :, 3]
        x = x_mix + m_lat[:, :, 5] * conv_ffn_2(h, w_up[l], w_dw[l], b_dw[l], w_down[l])

        if not last:
            ya_c = dense_attn(caq, cak, cav, sink_a[l])
            yb_c = dense_attn(cbq, cbk, cbv)
            ctx_mix = ctx + m_ctx[2] * merge_branches(ya_c, yb_c, yc_ctx, cgates, w_branch[l], w_out[l])
            hc = rms_norm(ctx_mix, norm_ffn[l]) * (1.0 + m_ctx[4]) + m_ctx[3]
            ctx = ctx_mix + m_ctx[5] * conv_ffn_2(hc, w_up[l], w_dw[l], b_dw[l], w_down[l])
    return rms_norm(x, norm_final)


def setup_inputs(seed=0):
    out = dict(first_inputs(seed))
    for name, value in second_inputs(seed + 1).items():
        if name != "x":
            out[name + "_2"] = value
    return out


def reference(
    x, w_in_even, idx_k_norm, w_in_odd, w_o, rel_bias, attn_norm, ffn_norm, w_up, conv_w,
    conv_b, w_down, final_norm, c_2, ctx_2, c_ctx_2, w_mod_2, b_mod_2, norm_mix_2, norm_ffn_2,
    w_in_2, sink_a_2, qn_b_2, kn_b_2, lb_fwd_2, lb_bwd_2, gn_c_2, w_branch_2, w_out_2, w_up_2,
    w_dw_2, b_dw_2, w_down_2, norm_final_2,
):
    x = first_block(
        x, w_in_even, idx_k_norm, w_in_odd, w_o, rel_bias, attn_norm, ffn_norm, w_up, conv_w,
        conv_b, w_down, final_norm,
    )
    return second_block(
        x, c_2, ctx_2, c_ctx_2, w_mod_2, b_mod_2, norm_mix_2, norm_ffn_2, w_in_2, sink_a_2,
        qn_b_2, kn_b_2, lb_fwd_2, lb_bwd_2, gn_c_2, w_branch_2, w_out_2, w_up_2, w_dw_2, b_dw_2,
        w_down_2, norm_final_2,
    )


_drawn_inputs = setup_inputs


def setup_inputs(seed=0):
    import zlib

    import numpy as np

    out = dict(_drawn_inputs(seed))
    spreads = {}
    factors = {'idx_k_norm': 4.696,
     'attn_norm': 2.96,
     'final_norm': 2.809,
     'ctx_2': 4.4,
     'b_mod_2': 2.826,
     'norm_mix_2': 7.284,
     'norm_ffn_2': 9.971,
     'sink_a_2': 8.0,
     'qn_b_2': 8.0,
     'kn_b_2': 8.0,
     'gn_c_2': 8.0,
     'b_dw_2': 23.633}
    for name, (base, spread) in spreads.items():
        noise = np.random.default_rng([zlib.crc32(name.encode()), seed]).standard_normal(out[name].shape)
        drawn = base * np.exp(spread * noise) if base else spread * noise
        out[name] = jnp.asarray(drawn.astype(out[name].dtype))
    for name, factor in factors.items():
        out[name] = (out[name] * factor).astype(out[name].dtype)
    return out
```

```python
import math
from contextlib import ExitStack

import numpy as np

import concourse.bass as bass
from concourse import mybir

F = mybir.dt.float32
R = mybir.dt.float32r
U8 = mybir.dt.uint8
ALU = mybir.AluOpType
ACT = mybir.ActivationFunctionType
AX = mybir.AxisListType

S = 512
D = 1024
KD = 8
DFF = 2816
HALF = 11
CTX = 256
EPS = 1e-6
BIG = 1e30
LOW = -3e38
KEEP = 128
TOEP = 640
LEVELS = (64, 32, 16, 8, 4, 2, 1)
N_SLOT = HALF * 128

SM = {}
_at = 0
for _name, _n in (("attn0", 8), ("attn1", 8), ("ffn0", 8), ("ffn1", 8), ("final", 8), ("mix2", 8), ("ffn2", 8),
                  ("final2", 8), ("cw0", 132), ("cw1", 132), ("cb0", 44), ("cb1", 44), ("dw2", 132), ("db2", 44),
                  ("bmod", 48), ("idxk", 1), ("qn", 1), ("kn", 1), ("gn", 1), ("sink", 8), ("c", 8), ("cctx", 8)):
    SM[_name] = (_at, _at + _n)
    _at += _n
N_SM = _at

CN = {}
_at = 0
for _name, _n in (("ident", 128), ("ones", 128), ("blk", 128), ("causal", 128), ("rot", 128), ("uf", 128), ("ub", 128), ("anti", 128)):
    CN[_name] = (_at, _at + _n)
    _at += _n
N_CN = _at


def weight_units():
    out = [("we", 0), ("wi", 0)] + [("we", 1 + n) for n in range(8 + 24)]
    mods = [("wmod", n) for n in range(48)]

    def block(wo, up, down, spare):
        for m in range(8):
            out.append((wo, m))
        for half in range(2):
            for j in range(HALF):
                n = half * HALF + j
                out.append((up, n))
                out.append((up, 22 + n))
                for _ in range(2 if spare and j < 10 else 1):
                    if spare and mods:
                        out.append(mods.pop(0))
            for m in range(8):
                out.append((down, half * 8 + m))

    block("wo0", "up0", "dn0", True)
    for n in range(24):
        out.append(("wq1", n))
    block("wo1", "up1", "dn1", True)
    assert not mods
    for n in [4, 5, 10, 11] + [0, 1, 2, 3] + [6, 7, 8, 9]:
        out.append(("win", n))
    for h in range(4):
        for base in (16, 20, 24, 12, 28):
            out.append(("win", base + h))
    for m in range(8):
        for n in range(3):
            out.append(("win", 32 + 8 * n + m))
            out.append(("wbr", 8 * n + m))
    block("wout", "up2", "dn2", False)
    return out


KTS = {"we": 8, "wi": 8, "wmod": 8, "wq1": 8, "win": 8, "wbr": 4, "wout": 8}
for _l in range(3):
    KTS[f"up{_l}"] = 8
    KTS[f"dn{_l}"] = HALF
    KTS[f"wo{_l}"] = 8


class Queue:

    def __init__(self, sem):
        self.sem, self.n, self.items = sem, 0, []

    def put(self, fn, *waits, inc=1):
        self.items.append((flat(waits), fn, self.sem, inc))
        self.n += inc
        return (self.sem, self.n)

    def dma(self, fn, slot, *waits):
        slot[1] += 16
        self.items.append((flat(waits), fn, slot[0], 16))
        return (slot[0], slot[1])

    def run(self, eng):
        seen = {}
        for waits, fn, sem, inc in self.items:
            for s, v in waits:
                if seen.get(id(s), 0) < v:
                    eng.wait_ge(s, v)
                    seen[id(s)] = v
            ins = fn(eng)
            if inc:
                ins.then_inc(sem, inc)


def flat(x):
    out = []
    for y in x:
        if y is None:
            continue
        if isinstance(y, list):
            out += flat(y)
        else:
            out.append(y)
    return out


def build(nc, t, out, dbg=None, stop=99):
    ctx = ExitStack()
    with ctx:
        build_in(nc, t, out, ctx, dbg or {}, stop)


def build_in(nc, t, out, ctx, dbg, stop):
    def sem(name):
        return ctx.enter_context(nc.semaphore(name))

    PE, V, A, P, SP = (Queue(sem(f"s_{x}")) for x in ("pe", "dve", "act", "pool", "sp"))

    base0 = (nc.sbuf_base + 63) // 64 * 64
    top = [base0]


    def sb(name, shape, dt=F, at=None):
        n = int(np.prod(shape[1:])) * (1 if dt == U8 else 4)
        n = (n + 63) // 64 * 64
        if at is None:
            off = top[0]
            top[0] += n
        else:
            off = at
        assert off + n <= nc.sbuf_usable_end, (name, off + n)
        return nc.alloc_sbuf_tensor_at(name, list(shape), dt, offset=off)

    ps = [ctx.enter_context(nc.psum_tensor(f"ps{i}", [128, 1024], F)) for i in range(4)]
    bank = [ps[i // 2][:, (i % 2) * 512:(i % 2) * 512 + 512] for i in range(8)]
    free = [[] for _ in range(8)]

    def slot(name):
        return [sem(name), 0]

    XT = sb("XT", [128, KD, S])
    hH = sb("hH", [128, KD, S], R)
    hL = sb("hL", [128, KD, S], R)
    NR, NH = 3, 2
    rawb = [sb(f"raw{i}", [128, N_SLOT]) for i in range(NR)]
    wHb = [sb(f"wH{i}", [128, N_SLOT], R) for i in range(NH)]
    wLb = [sb(f"wL{i}", [128, N_SLOT], R) for i in range(NH)]
    sm = sb("sm", [128, N_SM])
    cn = sb("cn", [128, N_CN])
    modT = sb("modT", [128, 48, 2])
    cs = sb("cs", [128, KD, 2])
    sc1 = sb("sc1", [128, 64])
    mark0 = top[0]

    def C(name, a=0, b=None):
        lo, hi = CN[name]
        return cn[:, lo + a:(hi if b is None else lo + b)]

    def M(name, a=0, b=None):
        lo, hi = SM[name]
        return sm[:, lo + a:(hi if b is None else lo + b)]

    ident = C("ident")
    d_cn, d_sm, d_x, d_misc = slot("d_cn"), slot("d_sm"), slot("d_x"), slot("d_misc")
    t_sm = SP.dma(lambda e: e.dma_start(sm[:], t["smalls"]), d_sm)
    t_x = SP.dma(lambda e: e.dma_start(XT[:], t["xT"]), d_x)
    t_cn = SP.dma(lambda e: e.dma_start(cn[:], t["consts"]), d_cn)

    units = weight_units()
    d_raw = [slot(f"d_raw{i}") for i in range(NR)]
    U = {"load": 0, "split": 0, "take": 0, "hs": 0, "rel": 0}
    raw_tok, raw_free, h_tok, h_slot = {}, {}, {}, {}
    h_free = [[] for _ in range(NH)]

    def is_split(n):
        return units[n][0] != "wmod"

    def size(n):
        name = units[n][0]
        kt = KTS[name]
        return kt, (16 if name == "wi" else 128)

    def advance():
        while True:
            n = U["load"]
            if n < len(units) and (n < NR or (n - NR) in raw_free):
                kt, nc_ = size(n)
                name, i = units[n]
                dst = rawb[n % NR][:, :kt * nc_]
                src = t[name][i]
                raw_tok[n] = SP.dma(lambda e, dst=dst, src=src: e.dma_start(dst, src), d_raw[n % NR],
                                    raw_free.get(n - NR))
                U["load"] += 1
                continue
            n = U["split"]
            if n < U["load"] and n < U["take"] + 4:
                if not is_split(n):
                    U["split"] += 1
                    continue
                if U["hs"] < U["rel"] + NH:
                    k = U["hs"] % NH
                    kt, nc_ = size(n)
                    r, H, L = rawb[n % NR][:, :kt * nc_], wHb[k][:, :kt * nc_], wLb[k][:, :kt * nc_]
                    th = split_hi(H, r, raw_tok[n], h_free[k])
                    tl = P.put(lambda e, L=L, r=r, H=H: e.tensor_tensor(L, r, H.bitcast(F), ALU.subtract), th)
                    h_tok[n], h_slot[n] = [th, tl], k
                    raw_free[n] = [tl]
                    U["hs"] += 1
                    U["split"] += 1
                    continue
            break

    def split_hi(H, r, *w):
        return A.put(lambda e: e.activation(H, r, ACT.Copy), *w)

    def take(name, i):
        n = U["take"]
        assert units[n] == (name, i), (units[n], name, i)
        U["take"] += 1
        advance()
        kt, nc_ = size(n)
        if not is_split(n):
            return n, rawb[n % NR][:, :kt * nc_].rearrange("p (k c) -> p k c", k=kt), None, [raw_tok[n]]
        k = h_slot[n]
        return (n, wHb[k][:, :kt * nc_].rearrange("p (k c) -> p k c", k=kt),
                wLb[k][:, :kt * nc_].rearrange("p (k c) -> p k c", k=kt), h_tok[n])

    def release(n, tok):
        if is_split(n):
            h_free[h_slot[n]] = [tok]
            U["rel"] += 1
        else:
            raw_free[n] = [tok]
        advance()

    def mm(o, l, r, start, stop, *w, inc=0):
        return PE.put(lambda e: e.matmul(o, l, r, start=start, stop=stop), *w, inc=inc)

    def gemm_cols(name, i, b, parts, *w):
        n, H, L, tok = take(name, i)
        kt = size(n)[0]
        last = None
        for xH, xL, o in parts:
            for k in range(kt):
                mm(o, H[:, k, :], xH(k), k == 0, False, tok, *w)
                mm(o, H[:, k, :], xL(k), False, False)
                last = mm(o, L[:, k, :], xH(k), False, k == kt - 1, inc=int(k == kt - 1))
        release(n, last)
        return last

    def gemm_rows(name, i, parts, *w, cols=128):
        n, H, L, tok = take(name, i)
        kt = size(n)[0]
        last = None
        for xH, xL, o in parts:
            for k in range(kt):
                mm(o, xH(k), H[:, k, :cols], k == 0, False, tok, *w)
                mm(o, xH(k), L[:, k, :cols], False, False)
                last = mm(o, xL(k), H[:, k, :cols], False, k == kt - 1, inc=int(k == kt - 1))
        release(n, last)
        return last

    def copy(q, o, i, *w, scale=1.0):
        if q is A:
            return A.put(lambda e: e.activation(o, i, ACT.Copy, scale=scale), *w)
        if scale == 1.0:
            return q.put(lambda e: e.tensor_copy(o, i), *w)
        return q.put(lambda e: e.tensor_scalar(o, i, scale, None, ALU.mult), *w)

    def act(o, i, f, *w, **kw):
        return A.put(lambda e: e.activation(o, i, f, **kw), *w)

    def tt(q, o, a, b, op, *w):
        return q.put(lambda e: e.tensor_tensor(o, a, b, op), *w)

    def stt(o, a, s, b, op0, op1, *w):
        return V.put(lambda e: e.scalar_tensor_tensor(o, a, s, b, op0, op1), *w)

    def ts(q, o, a, s1, s2, op0, op1, *w):
        if s2 is None:
            return q.put(lambda e: e.tensor_scalar(o, a, s1, None, op0), *w)
        return q.put(lambda e: e.tensor_scalar(o, a, s1, s2, op0, op1), *w)

    def pair_mult(q, o, a, b, u, *w):
        return q.put(lambda e: e.tensor_tensor(o[:, :, :, u, :], a[:, :, :, u, :], b[:, :, :, u, :], ALU.mult), *w)

    sq = [sb(f"sq{i}", [128, S]) for i in range(2)]
    sq_free = [[], []]
    rs = sb("rs", [128, S])
    hf = [sb(f"hf{i}", [128, S]) for i in range(2)]
    hf_free = [[], []]
    rs_free = [[]]
    eps_t = sb("eps_t", [128, 1])
    mn = sb("mn", [128, 16, 4])
    den = sb("den", [128, 16, 4])
    t_eps = V.put(lambda e: e.memset(eps_t[:], EPS))
    mark1 = top[0]

    def rsqrt_of(o, ss, n, *w):
        a = act(o, ss, ACT.Ln, t_eps, *w, scale=1.0 / n, bias=eps_t[:, 0:1])
        return act(o, o, ACT.Exp, a, scale=-0.5), a

    def sumsq(src, kt, n, ones, b, ready):
        last = None
        for k in range(kt):
            j = k % 2
            a = act(sq[j][:, :n], src(k), ACT.Square, ready(k), sq_free[j])
            last = mm(bank[b][:, :n], ones, sq[j][:, :n], k == 0, k == kt - 1, a, t_cn, free[b], inc=1)
            sq_free[j] = [last]
        return last

    def norm_scale(src, kt, n, ready, b=7):
        last = sumsq(src, kt, n, C("ones"), b, ready)
        r, a = rsqrt_of(rs[:, :n], bank[b][:, :n], 128 * kt, last, rs_free[0])
        free[b] = [a]
        return r

    def norm_split(src, kt, n, ready, gain, dH, dL, d_free, shift=None, gtok=None, b=7):
        r = norm_scale(src, kt, n, ready, b)
        toks = []
        for k in range(kt):
            j = k % 2
            h = hf[j][:, :n]
            a = stt(h, src(k), gain(k), rs[:, :n], ALU.mult, ALU.mult, r, hf_free[j], gtok)
            if shift is None:
                c = copy(A, dH(k), h, a, d_free)
                d = tt(P, dL(k), h, dH(k).bitcast(F), ALU.subtract, c, a, d_free)
            else:
                c = act(dH(k), h, ACT.Identity, a, d_free, bias=shift(k))
                d = stt(dL(k), h, shift(k), dH(k).bitcast(F), ALU.add, ALU.subtract, c, d_free)
            hf_free[j] = [c, d]
            toks += [c, d]
            rs_free[0] = [a]
        return toks

    mrow = sb("mrow", [32, TOEP])
    rel = sb("rel", [32, 32])
    oh = sb("oh", [32, TOEP])
    d_rel = [slot(f"d_rel{i}") for i in range(4)]
    ta = SP.dma(lambda e: e.dma_start(rel[:], t["rel"]), d_rel[0])
    tb = SP.dma(lambda e: e.dma_start(oh[:], t["onehot"]), d_rel[1])
    tc = SP.dma(lambda e: e.dma_start(mrow[:], t["maskrow"]), d_rel[2])
    mm(bank[0][0:32, :], rel[:], oh[:, 0:512], True, True, ta, tb)
    a = mm(bank[1][0:32, 0:TOEP - 512], rel[:], oh[:, 512:TOEP], True, True, inc=1)
    a1 = tt(V, mrow[:, 0:512], bank[0][0:32, :], mrow[:, 0:512], ALU.add, a, tc)
    a2 = tt(V, mrow[:, 512:TOEP], bank[1][0:32, 0:TOEP - 512], mrow[:, 512:TOEP], ALU.add, a)
    free[0], free[1] = [a1], [a2]
    t_toep = SP.dma(lambda e: e.dma_start(t["toep"], mrow[:]), d_rel[3], a1, a2)
    advance()

    def toep_src(h):
        return bass.AP(t["toep"].tensor, h * TOEP, [[1, 128], [1, 512]])

    top[0] = mark1
    tm = [sb(f"tm{i}", [128, S]) for i in range(2)]
    d_tm = [slot(f"d_tm{i}") for i in range(2)]
    Sp = [sb(f"Sp{i}", [128, S]) for i in range(2)]
    Pr = [sb(f"Pr{i}", [128, S]) for i in range(2)]
    PT = [sb(f"PT{i}", [128, S]) for i in range(2)]
    Sp_free, Pr_free, PT_free = [[], []], [[], []], [[], []]
    tm_free = [[], []]
    stat_free = [[]]
    mark2 = top[0]

    def attention(items, width2, qk, bias, vblk, init, finish, sink=None, fill=None):
        st = {}
        n = len(items)
        for step in range(n + 2):
            if step < n:
                h, i, nb = items[step]
                W = nb * 128
                sbk = step % 2
                S_ps = ps[sbk]
                fr = free[2 * sbk] + free[2 * sbk + 1]
                last = None
                for lhsT, rhs, col, w_, tok in qk(h, i):
                    last = mm(S_ps[:, col:col + w_], lhsT, rhs, True, True, tok, fr, inc=1)
                j = step % 2
                bi = bias(h, i)
                mcol = mn[:, h:h + 1, i]
                ini = init(h)
                if bi is None:
                    assert isinstance(ini, float)
                    m = V.put(lambda e, o=mcol, x=S_ps[:, :W]: e.tensor_reduce(o, x, AX.X, ALU.min), last,
                              stat_free[0])
                    src, sfree = S_ps[:, :W], True
                else:
                    bap, btok = bi
                    m = V.put(lambda e, o=Sp[j][:, :W], x=S_ps[:, :W], y=bap, c=mcol, ini=ini:
                              e.tensor_tensor_reduce(o, x, y, 1.0, ini, ALU.add, ALU.min, c),
                              last, btok, Sp_free[j], stat_free[0])
                    src, sfree = Sp[j][:, :W], False
                    free[2 * sbk] = free[2 * sbk + 1] = [m]
                x = act(Pr[j][:, :W], src, ACT.Exp, m, Pr_free[j], stat_free[0], scale=-1.0, bias=mcol,
                        accum_out=den[:, h:h + 1, i])
                if sfree:
                    free[2 * sbk] = free[2 * sbk + 1] = [x]
                else:
                    Sp_free[j] = [x]
                if fill is not None:
                    fill(h, i, m)
                st[step] = dict(x=x, m=m)
            if 1 <= step <= n:
                q = step - 1
                h, i, nb = items[q]
                j = q % 2
                if width2:
                    T_ps, tb_ = ps[2], [4, 5]
                else:
                    T_ps, tb_ = ps[2][:, 512 * j:512 * j + 512], [4 + j]
                last = None
                for b in range(nb):
                    last = PE.put(lambda e, o=T_ps[:, b * 128:b * 128 + 128], x=Pr[j][:, b * 128:b * 128 + 128]:
                                  e.transpose(o, x, ident), st[q]["x"], t_cn, [free[z] for z in tb_],
                                  inc=int(b == nb - 1))
                Pr_free[j] = [last]
                eq = (V, A)[q % 2]
                c = copy(eq, PT[j][:, :nb * 128], T_ps[:, :nb * 128], last, PT_free[j])
                for z in tb_:
                    free[z] = [c]
                st[q]["pt"] = c
            if step >= 2:
                q = step - 2
                h, i, nb = items[q]
                j = q % 2
                ob = 6 + h % 2
                last = None
                for b in range(nb):
                    vap, vtok = vblk(h, i, b)
                    last = mm(bank[ob][:, i * 64:i * 64 + 64], PT[j][:, b * 128:b * 128 + 128], vap, b == 0,
                              b == nb - 1, st[q]["pt"], vtok, free[ob] if i == 0 else None, inc=int(b == nb - 1))
                PT_free[j] = [last]
                if i == 3:
                    ds = []
                    if sink is not None:
                        s_ = sink(h)
                        a = ts(V, sc1[:, 0:4], mn[:, h, :], s_, None, ALU.add, None, st[q]["m"], t_sm, sink_free[0])
                        a = act(sc1[:, 4:8], sc1[:, 0:4], ACT.Exp, a)
                        a = tt(V, den[:, h, :], den[:, h, :], sc1[:, 4:8], ALU.add, a, st[q]["x"])
                        sink_free[0] = [a]
                        ds = [a]
                    a = V.put(lambda e, x=den[:, h, :]: e.reciprocal(x, x), st[q]["x"], ds)
                    o3 = bank[ob][:, 0:256].rearrange("p (i d) -> p i d", i=4)
                    dd = den[:, h:h + 1, :].rearrange("p a i -> p i a").to_broadcast([128, 4, 64])
                    a = tt(V, finish(h), o3, dd, ALU.mult, a, last)
                    free[ob] = [a]
                    st["done"] = a
        stat_free[0] = [st["done"]]
        return st["done"]

    sink_free = [[]]

    def rows_to_cols(src, nchunk, dH, dL, ready, d_free, rows=None):
        toks = []
        for c in range(nchunk):
            b = c % 4
            last = None
            for i in range(4):
                last = PE.put(lambda e, o=bank[b][:, i * 128:i * 128 + 128], x=src(i, c): e.transpose(o, x, ident),
                              ready, t_cn, free[b], inc=int(i == 3))
            x = (rows or in_blocks)(bank[b])
            a = copy(A, in_blocks(dH(c)), x, last, d_free)
            d = tt(V, in_blocks(dL(c)), x, in_blocks(dH(c)).bitcast(F), ALU.subtract, a, d_free)
            free[b] = [d]
            toks += [a, d]
        return toks

    def in_blocks(x):
        return x.rearrange("p (i n) -> p i n", n=128)

    def turned(x):
        return x.rearrange("p (i n) -> p i n", n=128)[:, :, ::-1]

    def hk(z):
        return lambda k: z[:, k, :]

    xready = {k: [t_x] for k in range(KD)}
    h_done = [[]]

    def add_x(m, b, tok, scale=None, w=None):
        if scale is None:
            a = tt(V, XT[:, m, :], bank[b], XT[:, m, :], ALU.add, tok, xready[m])
        else:
            a = stt(XT[:, m, :], bank[b], scale, XT[:, m, :], ALU.mult, ALU.add, tok, xready[m], w)
        free[b] = [a]
        xready[m] = [a]
        return a

    def pe_done():
        return (PE.sem, PE.n)

    dslots = {}

    def debug(name, ap, *w):
        if name in dbg:
            dslots[name] = slot("dbg_" + name)
            tk = SP.dma(lambda e: e.dma_start(dbg[name], ap), dslots[name], *w)
            SP.items.append(([tk], lambda e: None, None, 0))
            return tk

    def xdbg(name):
        tk = debug(name, XT[:], [xready[m] for m in range(8)])
        if tk:
            for m in range(8):
                xready[m] = xready[m] + [tk]

    mod_state = {"n": 0, "last": None}

    def mod_unit():
        if "cs" not in mod_state:
            a1 = act(cs[:, :, 0], M("c"), ACT.Silu, t_sm)
            a2 = act(cs[:, :, 1], M("cctx"), ACT.Silu, t_sm)
            mod_state["cs"] = [a1, a2]
        u = mod_state["n"]
        mod_state["n"] += 1
        n, W_, _, tok = take("wmod", u)
        for k in range(KD):
            last = mm(bank[7][:, 2 * u:2 * u + 2], W_[:, k, :], cs[:, k, :], k == 0, k == KD - 1, tok, mod_state["cs"],
                      free[7], inc=int(k == KD - 1))
        release(n, last)
        mod_state["last"] = last
        return last

    def mod_flush():
        lo, hi = mod_state.get("from", 0), mod_state["n"]
        if hi > lo:
            a = tt(V, modT[:, lo:hi, :], bank[7][:, 2 * lo:2 * hi].rearrange("p (a b) -> p a b", b=2),
                   M("bmod")[:, lo:hi].unsqueeze(2).to_broadcast([128, hi - lo, 2]), ALU.add, mod_state["last"], t_sm)
            free[7] = [a]
            mod_state["from"] = hi
            mod_state["tok"] = a

    top[0] = mark1
    gH = sb("gH", [128, HALF, S], R)
    gL = sb("gL", [128, HALF, S], R)
    cv = [sb(f"cv{i}", [128, S]) for i in range(2)]
    cg_ = [sb(f"cg{i}", [128, S]) for i in range(2)]
    sg = [sb(f"sg{i}", [128, S]) for i in range(2)]
    hw_ffn = top[0]
    ffn_free = {"cv": [[], []], "cg": [[], []], "sg": [[], []], "g": []}

    def ffn(layer, up, down, gain, taps, cw, cb, spare, start, shift=None, gtok=None, scale=None):
        hw = norm_split(lambda k: XT[:, k, :], KD, S, lambda k: xready[k], gain, hk(hH), hk(hL), h_done[0], shift, gtok)
        for q in "cv", "cg", "sg":
            ffn_free[q] = [list(start), list(start)]
        ffn_free["g"] = list(start)

        def conv(b, n, dst, tok, fr):
            off0, j0 = taps[0]
            assert off0 == 0
            a = act(dst, bank[b], ACT.Identity, tok, fr, t_sm, scale=M(cw, j0 * 44 + n, j0 * 44 + n + 1),
                    bias=M(cb, n, n + 1))
            for off, j in taps[1:]:
                w_ = M(cw, j * 44 + n, j * 44 + n + 1)
                if off > 0:
                    a = stt(dst[:, off:], bank[b][:, :S - off], w_, dst[:, off:], ALU.mult, ALU.add, a)
                else:
                    a = stt(dst[:, :S + off], bank[b][:, -off:], w_, dst[:, :S + off], ALU.mult, ALU.add, a)
            free[b] = [a]
            return a

        for half in range(2):
            g_tok = []
            for j in range(HALF):
                n = half * HALF + j
                z = j % 2
                bv, bg = 0 + z, 2 + z
                tv = gemm_cols(up, n, bv, [(hk(hH), hk(hL), bank[bv])], hw, free[bv])
                av = conv(bv, n, cv[z][:], tv, ffn_free["cv"][z])
                tg = gemm_cols(up, 22 + n, bg, [(hk(hH), hk(hL), bank[bg])], hw, free[bg])
                ag = conv(bg, 22 + n, cg_[z][:], tg, ffn_free["cg"][z])
                s_ = act(sg[z][:], cg_[z][:], ACT.Silu, ag, ffn_free["sg"][z])
                ffn_free["cg"][z] = [s_]
                p_ = tt(P, sg[z][:], sg[z][:], cv[z][:], ALU.mult, s_, av)
                ffn_free["cv"][z] = [p_]
                gh = copy(A, gH[:, j, :], sg[z][:], p_, ffn_free["g"])
                gl = tt(P, gL[:, j, :], sg[z][:], gH[:, j, :].bitcast(F), ALU.subtract, gh, ffn_free["g"])
                ffn_free["sg"][z] = [gl]
                g_tok += [gh, gl]
                for _ in range(2 if spare and j < 10 else 1):
                    if spare and mod_state["n"] < 48:
                        mod_unit()
            h_done[0] = [pe_done()]
            for m in range(8):
                b = 4 + m % 3
                tk = gemm_cols(down, half * 8 + m, b, [(hk(gH), hk(gL), bank[b])], g_tok, free[b])
                add_x(m, b, tk, None if scale is None else scale(m), gtok)
            ffn_free["g"] = [tk]
        if spare:
            mod_flush()
        return [tk, ffn_free["sg"][0], ffn_free["sg"][1], [xready[m] for m in range(8)]]

    TAPS1 = ((0, 2), (1, 1), (2, 0))
    TAPS2 = ((0, 1), (1, 0), (-1, 2))

    def attn_load_bias(h, slot_i, row, need):
        return SP.dma(lambda e: e.dma_start(tm[slot_i][:], toep_src(row)), d_tm[slot_i], t_toep, need)

    top[0] = mark2
    qT = sb("qT", [128, 8, S])
    kT = sb("kT", [128, 8, S])
    vR = sb("vR", [128, 4, D])
    mixed = sb("mixed", [128, 4, D])
    kiT = sb("kiT", [128, S])
    wiR = sb("wiR", [128, 4, 16])
    sco = [None] + [sb(f"sco{i}", [128, 128 * (i + 1)]) for i in range(1, 4)]
    m8 = sb("m8", [128, 8])
    rl = [sb(f"rl{i}", [128, S]) for i in range(2)]
    bz = [sb(f"bz{i}", [128, S]) for i in range(2)]
    qiT = mixed[:, :, :].rearrange("p a b -> p (a b)").rearrange("p (c n) -> p c n", c=8)

    def att_gain(name):
        return lambda k: M(name, k, k + 1)

    hw = norm_split(lambda k: XT[:, k, :], KD, S, lambda k: xready[k], att_gain("attn0"), hk(hH), hk(hL), None,
                    gtok=t_sm)
    tk = gemm_cols("we", 0, 0, [(hk(hH), hk(hL), bank[0])], hw, free[0])
    c0 = copy(V, kiT[:], bank[0], tk)
    free[0] = [c0]
    a = sumsq(lambda k: kiT[:], 1, S, C("blk"), 6, lambda k: [c0])
    r, a = rsqrt_of(rs[:], bank[6], 64, a, rs_free[0])
    free[6] = [a]
    t_ki = stt(kiT[:], kiT[:], M("idxk"), rs[:], ALU.mult, ALU.mult, r, c0)
    rs_free[0] = [t_ki]
    tk = gemm_rows("wi", 0, [(lambda k, i=i: hH[:, k, i * 128:i * 128 + 128], lambda k, i=i: hL[:, k, i * 128:i * 128 + 128],
                              bank[1][:, i * 16:i * 16 + 16]) for i in range(4)], hw, free[1], cols=16)
    w64 = wiR[:].rearrange("p a b -> p (a b)")
    a = ts(V, w64, bank[1][:, 0:64], 0.25, None, ALU.mult, None, tk)
    free[1] = [a]
    tk = mm(bank[1][:, 0:64], C("anti"), w64, True, True, a, t_cn, free[1], inc=1)
    t_wi = copy(V, w64, bank[1][:, 0:64], tk)
    free[1] = [t_wi]
    t_qi = []
    for c in range(8):
        b = c % 4
        tk = gemm_cols("we", 1 + c, b, [(hk(hH), hk(hL), bank[b])], hw, free[b])
        a = copy((V, A)[c % 2], turned(qiT[:, c, :]), in_blocks(bank[b]), tk)
        free[b] = [a]
        t_qi.append(a)
    t_sco = {}
    sc_free = [[], []]
    n = 0
    for i in range(1, 4):
        W = 128 * (i + 1)
        prev = None
        for h in range(16):
            b, z = 4 + n % 3, n % 2
            p0 = 64 * (h % 2)
            tk = mm(bank[b][:, :W], qiT[p0:p0 + 64, h // 2, i * 128:i * 128 + 128], kiT[p0:p0 + 64, :W], True, True,
                    t_ki, t_qi[h // 2], free[b], inc=1)
            a = act(rl[z][:, :W], bank[b][:, :W], ACT.Relu, tk, sc_free[z], scale=0.125)
            free[b] = [a]
            w_ = wiR[:, i, h:h + 1]
            if h == 0:
                prev = ts(V, sco[i][:], rl[z][:, :W], w_, None, ALU.mult, None, a, t_wi)
            else:
                prev = stt(sco[i][:], rl[z][:, :W], w_, sco[i][:], ALU.mult, ALU.add, a, prev, t_wi)
            sc_free[z] = [prev]
            n += 1
        prev = tt(V, sco[i][:, W - 128:W], sco[i][:, W - 128:W], C("causal"), ALU.add, prev, t_cn)
        t_sco[i] = prev
    qi_free = [tk]

    topk_prog = []

    def topk_steps():
        for i in range(1, 4):
            src = sco[i]
            prev = t_sco[i]
            for r_ in range(KEEP // 8):
                a = V.put(lambda e, i=i: e.max(m8[:], sco[i][:]), prev)
                prev = V.put(lambda e, i=i: e.match_replace(sco[i][:], m8[:], sco[i][:], LOW), a)
                if r_ % 4 == 3:
                    yield None
            t_sco[i] = ts(V, sco[i][:], sco[i][:], -2e38, BIG, ALU.is_gt, ALU.mult, prev)
            yield None

    tki = topk_steps()
    t_qk = {}
    for c in range(24):
        b = c % 4
        kind, cc = (c % 12) // 4, c % 4
        g = c // 12
        if kind < 2:
            tk = gemm_cols("we", 9 + c, b, [(hk(hH), hk(hL), bank[b])], hw, free[b])
            dst = (qT, kT)[kind][:, g * 4 + cc, :]
            a = copy(A, turned(dst) if kind == 0 else in_blocks(dst), in_blocks(bank[b]), tk, scale=(-0.125, 1.0)[kind])
        else:
            tk = gemm_rows("we", 9 + c, [(lambda k, i=i: hH[:, k, i * 128:i * 128 + 128],
                                          lambda k, i=i: hL[:, k, i * 128:i * 128 + 128],
                                          bank[b][:, i * 128:i * 128 + 128]) for i in range(4)], hw, free[b])
            o = g * 512 + cc * 128
            a = copy(A, vR[:, :, o:o + 128], bank[b].rearrange("p (i d) -> p i d", i=4), tk)
        free[b] = [a]
        t_qk[(g, kind, cc)] = a
        next(tki, None)
    for _ in tki:
        pass
    h_done[0] = [pe_done()]

    def run_attn(heads, row0, masked):
        tmt = {}
        st = {"n": 0}

        def need(h):
            if h in tmt or h not in heads:
                return
            k = st["n"] % 2
            st["n"] += 1
            tmt[h] = (k, attn_load_bias(h, k, row0 + h, tm_free[k]))

        for h in heads[:2]:
            need(h)

        def qk(h, i):
            p0 = 64 * (h % 2)
            c = h // 2
            W = 128 * (i + 1)
            tok = [t_qk[(c // 4, 0, c % 4)], t_qk[(c // 4, 1, c % 4)]]
            return [(qT[p0:p0 + 64, c, i * 128:i * 128 + 128], kT[p0:p0 + 64, c, :W], 0, W, tok)]

        def bias(h, i):
            k, tok = tmt[h]
            bap = tm[k][:, 384 - 128 * i:512]
            if masked and i > 0:
                z = i % 2
                W = 128 * (i + 1)
                a = tt(P, bz[z][:, :W], bap, sco[i][:], ALU.add, tok, t_sco[i], bz_free[z])
                st["bz"] = (z, a)
                return bz[z][:, :W], [a]
            st["bz"] = None
            return bap, [tok]

        def fill(h, i, m):
            if st["bz"] is not None:
                bz_free[st["bz"][0]] = [m]
            if i == 3:
                k, _ = tmt[h]
                tm_free[k] = [m, st["bz"][1]] if st["bz"] else [m]
                later = [x for x in heads if x not in tmt]
                if later:
                    need(later[0])

        def vblk(h, i, b):
            c = h // 2
            return vR[:, b, h * 64:h * 64 + 64], [t_qk[(c // 4, 2, c % 4)]]

        return attention([(h, i, i + 1) for h in heads for i in range(4)], False, qk, bias, vblk, lambda h: BIG,
                         lambda h: mixed[:, :, h * 64:h * 64 + 64], fill=fill)

    bz_free = [[], []]
    free[6] = free[6] + qi_free
    free[7] = free[7] + qi_free
    V.put(lambda e: e.memset(sc1[:, 60:61], 0.0), qi_free)
    t_mix = run_attn(list(range(8)), 0, False)
    t_mix = run_attn(list(range(8, 16)), 0, True)
    debug("mixed0", mixed[:], t_mix)

    def mix_out(wo):
        mt = rows_to_cols(lambda i, c: mixed[:, i, c * 128:c * 128 + 128], 8, hk(hH), hk(hL), t_mix, h_done[0], turned)
        for m in range(8):
            b = 4 + m % 3
            tk = gemm_cols(wo, m, b, [(hk(hH), hk(hL), bank[b])], mt, free[b])
            add_x(m, b, tk)
        h_done[0] = [tk]
        return tk

    tk = mix_out("wo0")
    start = [tk, t_mix]
    if stop > 1:
        fin = ffn(0, "up0", "dn0", att_gain("ffn0"), TAPS1, "cw0", "cb0", True, start)
    xdbg("x1")

    if stop > 2:
        hw = norm_split(lambda k: XT[:, k, :], KD, S, lambda k: xready[k], att_gain("attn1"), hk(hH), hk(hL), h_done[0])
        for c in range(24):
            b = c % 4
            kind, cc = c // 8, c % 8
            if kind < 2:
                tk = gemm_cols("wq1", c, b, [(hk(hH), hk(hL), bank[b])], hw, free[b])
                dst = (qT, kT)[kind][:, cc, :]
                a = copy(A, turned(dst) if kind == 0 else in_blocks(dst), in_blocks(bank[b]), tk, fin, scale=(-0.125, 1.0)[kind])
            else:
                tk = gemm_rows("wq1", c, [(lambda k, i=i: hH[:, k, i * 128:i * 128 + 128],
                                           lambda k, i=i: hL[:, k, i * 128:i * 128 + 128],
                                           bank[b][:, i * 128:i * 128 + 128]) for i in range(4)], hw, free[b])
                a = copy(A, vR[:, :, cc * 128:cc * 128 + 128], bank[b].rearrange("p (i d) -> p i d", i=4), tk, fin)
            free[b] = [a]
            t_qk[(cc // 4, kind, cc % 4)] = a
        h_done[0] = [pe_done()]
        for f_ in (tm_free, Sp_free, Pr_free, PT_free):
            f_[0], f_[1] = f_[0] + flat([fin]), f_[1] + flat([fin])
        stat_free[0] = stat_free[0] + flat([fin])
        t_mix = run_attn(list(range(16)), 16, False)
        tk = mix_out("wo1")
        fin = ffn(1, "up1", "dn1", att_gain("ffn1"), TAPS1, "cw1", "cb1", True, [tk, t_mix])
        xdbg("x2")

    def fence():
        return [(q.sem, q.n) for q in (PE, V, A, P)]

    def join(f, *qs):
        for q in qs:
            q.items.append((flat([f]), lambda e: None, None, 0))

    if stop > 3:
        r = norm_scale(lambda k: XT[:, k, :], KD, S, lambda k: xready[k])
        for k in range(KD):
            a = stt(XT[:, k, :], XT[:, k, :], M("final", k, k + 1), rs[:], ALU.mult, ALU.mult, r, xready[k])
            xready[k] = [a]
        rs_free[0] = [a]
        tmod = mod_state["tok"]
        gm = sc1[:, 8:16]
        gc = sc1[:, 16:24]
        gf = sc1[:, 24:32]
        g1 = stt(gm, modT[:, 8:16, 0], 1.0, M("mix2"), ALU.add, ALU.mult, tmod, t_sm)
        g2 = stt(gc, modT[:, 8:16, 1], 1.0, M("mix2"), ALU.add, ALU.mult, tmod, t_sm)
        g3 = stt(gf, modT[:, 32:40, 0], 1.0, M("ffn2"), ALU.add, ALU.mult, tmod, t_sm)
        qn8 = ts(V, sc1[:, 32:33], M("qn"), -0.125, None, ALU.mult, None, t_sm)
        nsk = ts(V, sc1[:, 40:48], M("sink"), -1.0, None, ALU.mult, None, t_sm)
        smalls2 = [g1, g2, g3, qn8, nsk]
        f0 = fence()
        join(f0, V, A, P, PE)

        top[0] = mark1
        hcH = sb("hcH", [128, KD, CTX], R)
        hcL = sb("hcL", [128, KD, CTX], R)
        mixed2 = sb("mixed2", [128, 4, D])
        yc = sb("yc", [128, 4, S])
        mark3 = top[0]
        Sp = [sb(f"Sq{i}", [128, 768]) for i in range(2)]
        Pr = [sb(f"Pq{i}", [128, 768]) for i in range(2)]
        PT = [sb(f"PU{i}", [128, 768]) for i in range(2)]
        aqT = sb("aqT", [128, 4, S])
        bqT = sb("bqT", [128, 4, S])
        akT, bkT = sb("akT", [128, 768]), sb("bkT", [128, 768])
        avR, bvR = sb("avR", [128, 6, 128]), sb("bvR", [128, 6, 128])
        ropes = sb("ropes", [128, 2, S])
        band = sb("band", [128, 1152])
        d_b2 = [slot(f"d_b2{i}") for i in range(5)]
        ctxT = mixed2[:, :, :].rearrange("p a b -> p (a b)")[:, 0:2048].rearrange("p (k n) -> p k n", k=8)
        qtmp = [mixed2[:, 2, 0:512], mixed2[:, 2, 512:1024]]
        qt_free = [[], []]
        t_ctx = SP.dma(lambda e: e.dma_start(ctxT, t["ctxT"]), d_b2[0], f0)
        t_rope = SP.dma(lambda e: e.dma_start(ropes[:], t["ropes"]), d_b2[1], f0)
        t_band = SP.dma(lambda e: e.dma_start(band[:], t["band"]), d_b2[2], f0)
        for z in (Sp_free, Pr_free, PT_free):
            z[0], z[1] = [], []

        hw = norm_split(lambda k: XT[:, k, :], KD, S, lambda k: xready[k], lambda k: gm[:, k:k + 1], hk(hH), hk(hL),
                        h_done[0], shift=lambda k: modT[:, k, 0:1], gtok=smalls2)
        hc = norm_split(lambda k: ctxT[:, k, :], KD, CTX, lambda k: [t_ctx], lambda k: gc[:, k:k + 1], hk(hcH),
                        hk(hcL), None, shift=lambda k: modT[:, k, 1:2], gtok=smalls2)
        hboth = [hw, hc]

        def rows6(unit, b0, b1, *w):
            def part(H, L, i):
                return (lambda k: H[:, k, i * 128:i * 128 + 128], lambda k: L[:, k, i * 128:i * 128 + 128])
            parts = [(*part(hH, hL, i), bank[b0][:, i * 128:i * 128 + 128]) for i in range(4)]
            parts += [(*part(hcH, hcL, i), bank[b1][:, i * 128:i * 128 + 128]) for i in range(2)]
            return gemm_rows("win", unit, parts, hboth, free[b0], free[b1], *w)

        def b3(x, n):
            return x.rearrange("p (i d) -> p i d", i=n)

        def head_norm(x, n, gain, w, b=7):
            a = sumsq(lambda k: x, 1, n, C("blk"), b, lambda k: w)
            r, a1 = rsqrt_of(rs[:, :n], bank[b][:, :n], 64, a, rs_free[0])
            free[b] = [a1]
            a = stt(x, x, gain, rs[:, :n], ALU.mult, ALU.mult, r, w)
            rs_free[0] = [a]
            return a

        rope_n = [0]

        def rope(dst, x, w):
            b = 4 + rope_n[0] % 2
            j = rope_n[0] % 2
            rope_n[0] += 1
            a = mm(bank[b], C("rot"), x, True, True, w, t_cn, free[b], inc=1)
            u = tt(V, hf[j][:], bank[b], ropes[:, 1, :], ALU.mult, a, t_rope, hf_free[j])
            free[b] = [u]
            c = tt(P, dst, x, ropes[:, 0, :], ALU.mult, w, t_rope)
            d = tt(P, dst, dst, hf[j][:], ALU.add, c, u)
            hf_free[j] = [d]
            return a, d

        t_k2, t_v2, t_q2 = {}, {}, {}
        for g, (kT2, vR2, uk, uv) in enumerate(((akT, avR, 4, 5), (bkT, bvR, 10, 11))):
            tk = gemm_cols("win", uk, 0, [(hk(hH), hk(hL), bank[0]), (hk(hcH), hk(hcL), bank[1][:, :CTX])], hboth,
                           free[0], free[1])
            a = copy(A, qtmp[g], bank[0], tk, qt_free[g])
            c = copy(A, kT2[:, S:], bank[1][:, :CTX], tk)
            free[0], free[1] = [a], [c]
            if g == 1:
                a = head_norm(qtmp[g], S, M("kn"), [a])
                c = head_norm(kT2[:, S:], CTX, M("kn"), [c])
            x1, x2 = rope(kT2[:, 0:S], qtmp[g], [a])
            qt_free[g] = [x1, x2]
            t_k2[g] = [x2, c]
            tk = rows6(uv, 2, 3)
            a = copy(A, vR2[:, 0:4, :], b3(bank[2], 4), tk)
            c = copy(A, vR2[:, 4:6, :], b3(bank[3][:, :CTX], 2), tk)
            free[2], free[3] = [a], [c]
            t_v2[g] = [a, c]
        for g in range(2):
            for c in range(4):
                b, j = c % 4, c % 2
                tk = gemm_cols("win", (0, 6)[g] + c, b, [(hk(hH), hk(hL), bank[b])], hboth, free[b])
                a = copy(A, qtmp[j], bank[b], tk, qt_free[j], scale=(-0.125, 1.0)[g])
                free[b] = [a]
                if g == 1:
                    a = head_norm(qtmp[j], S, sc1[:, 32:33], [a, qn8])
                x1, x2 = rope((aqT, bqT)[g][:, c, :], qtmp[j], [a])
                qt_free[j] = [x1, x2]
                t_q2[(g, c)] = x2
        mixed_ready = [qt_free[0], qt_free[1], hc]
        join(mixed_ready, V)

        def local(i):
            return max(i - 1, 0), min(i + 1, 3)

        def qk2(h, i):
            g, h = h // 8, h % 8
            p0 = 64 * (h // 4)
            q = (aqT, bqT)[g][p0:p0 + 64, h % 4, i * 128:i * 128 + 128]
            k = (akT, bkT)[g][p0:p0 + 64, :]
            tok = [t_q2[(g, h % 4)], t_k2[g]]
            if g == 1:
                return [(q, k[:, 0:512], 0, 512, tok), (q, k[:, 512:768], 512, 256, tok)]
            lo, hi = local(i)
            out_ = [(q, k[:, 512:768], 0, 256, tok), (q, k[:, lo * 128:lo * 128 + 256], 256, 256, tok)]
            if hi - lo == 2:
                out_.append((q, k[:, hi * 128:hi * 128 + 128], 512, 128, tok))
            return out_

        def bias2(h, i):
            if h >= 8:
                return None
            lo, hi = local(i)
            n_ = 256 + 128 * (hi - lo + 1)
            return (band[:, 640:640 + n_] if i == 0 else band[:, 0:n_]), [t_band]

        def vblk2(h, i, b):
            g, h = h // 8, h % 8
            if g == 0:
                blk_ = 4 + b if b < 2 else local(i)[0] + b - 2
            else:
                blk_ = b
            return (avR, bvR)[g][:, blk_, 64 * (h // 4):64 * (h // 4) + 64], [t_v2[g]]

        def nb2(h, i):
            lo, hi = local(i)
            return 6 if h >= 8 else 2 + hi - lo + 1

        sink_free[0] = []
        tA = attention([(h, i, nb2(h, i)) for h in range(8) for i in range(4)], True, qk2, bias2, vblk2,
                       lambda h: sc1[:, 40 + h:41 + h], lambda h: mixed2[:, :, h * 64:h * 64 + 64],
                       sink=lambda h: M("sink", h, h + 1))
        tB = attention([(h, i, 6) for h in range(8, 16) for i in range(4)], True, qk2, bias2, vblk2,
                       lambda h: BIG, lambda h: mixed2[:, :, h * 64:h * 64 + 64])
        tk = debug("yab", mixed2[:], tA, tB)

        f1 = fence()
        join(f1, V, A, P, PE)
        top[0] = mark3
        decay = sb("decay", [128, 2, 1024])
        lmask = sb("lmask", [128, 14, 128], U8)
        z6, t6 = sb("z6", [128, 6, 128]), sb("t6", [128, 6, 128])
        lf = [sb(f"lf{i}", [128, 6, 128]) for i in range(2)]
        kr = [sb(f"kr{i}", [128, 6, 128]) for i in range(2)]
        kd = [sb(f"kd{i}", [128, 6, 128]) for i in range(2)]
        vr = sb("vr", [128, 6, 128])
        qt = sb("qt", [128, 4, 128])
        kc = [sb(f"kc{i}", [128, 4, 128]) for i in range(2)]
        sgc = sb("sgc", [128, S])
        E4 = sb("E4", [128, 4, 4, 128])
        qa = [sb(f"qa{i}", [128, 4, 128]) for i in range(2)]
        Z = [sb("Z0", [128, 4, 128])[:, :, :], hf[1][:, :].rearrange("p (c n) -> p c n", c=4)]
        scT = hf[0][:, :].rearrange("p (c n) -> p c n", c=4)
        stt_ = [sb(f"st{i}", [128, 4, 128]) for i in range(2)]
        f6 = sb("f6", [128, 2, 6])
        t_dec = SP.dma(lambda e: e.dma_start(decay[:], t["decay"]), d_b2[3], f1)
        lmf = E4[:, :, :, :].rearrange("p a b c -> p (a b c)")[:, 0:14 * 128].rearrange("p (m n) -> p m n", m=14)
        a = SP.dma(lambda e: e.dma_start(lmf, t["lmask"]), d_b2[4], f1)
        t_lm = V.put(lambda e: e.tensor_copy(lmask[:], lmf), a)
        b128 = lambda b, c: bank[b][:, c * 128:c * 128 + 128]
        head_free = []
        for h in range(4):
            lf_t, kr_t, kd_t, kc_t, f6_t = {}, {}, {}, {}, {}
            z_free, t_free = list(head_free), list(head_free)
            for d in range(2):
                tk = rows6((16, 20)[d] + h, 0, 1)
                a = copy(V, z6[:, 0:4, :], b3(bank[0], 4), tk, z_free)
                c = copy(V, z6[:, 4:6, :], b3(bank[1][:, :CTX], 2), tk)
                free[0], free[1] = [a], [c]
                x = act(t6[:], z6[:], ACT.Abs, a, c, t_free)
                x = act(t6[:], t6[:], ACT.Exp, x, scale=-1.0)
                x = act(t6[:], t6[:], ACT.Ln, x, bias=1.0)
                lf_t[d] = stt(lf[d][:], z6[:], 0.0, t6[:], ALU.min, ALU.subtract, x, a, c, head_free)
                x = tt(P, t6[:], lf[d][:], z6[:], ALU.subtract, lf_t[d], a, c)
                z_free = [x, lf_t[d]]
                kr_t[d] = act(kr[d][:], t6[:], ACT.Exp, x, head_free)
                u = C(("uf", "ub")[d])
                mm(bank[2], u, lf[d][:, 0:4, :], True, True, lf_t[d], free[2], t_cn)
                x = mm(bank[3][:, :CTX], u, lf[d][:, 4:6, :], True, True, free[3], inc=1)
                e1 = act(t6[:, 0:4, :], b3(bank[2], 4), ACT.Exp, x, kr_t[d])
                e2 = act(t6[:, 4:6, :], b3(bank[3][:, :CTX], 2), ACT.Exp, x, kr_t[d])
                free[2], free[3] = [e1], [e2]
                kd_t[d] = tt(P, kd[d][:], kr[d][:], t6[:], ALU.mult, e1, e2, kr_t[d], head_free)
                t_free = [kd_t[d]]
                for c in range(6):
                    x = mm(bank[4][:, c:c + 1], lf[d][:, c, :], C("ones", 0, 1), True, True, free[4], inc=int(c == 5))
                f6_t[d] = act(f6[:, d, :], bank[4][:, 0:6], ACT.Exp, x, head_free)
                free[4] = [f6_t[d]]
                for c in range(4):
                    x = PE.put(lambda e, o=b128(5, c), i_=kr[d][:, c, :]: e.transpose(o, i_, ident), kr_t[d], free[5],
                               inc=int(c == 3))
                kc_t[d] = copy(V, kc[d][:], b3(bank[5], 4), x, head_free)
                free[5] = [kc_t[d]]
            tk = rows6(24 + h, 0, 1)
            a = copy(V, vr[:, 0:4, :], b3(bank[0], 4), tk, head_free)
            c = copy(V, vr[:, 4:6, :], b3(bank[1][:, :CTX], 2), tk)
            free[0], free[1] = [a], [c]
            v_t = [a, c]
            tk = gemm_cols("win", 12 + h, 2, [(hk(hH), hk(hL), bank[2])], hboth, free[2])
            q_t = act(qt[:], b3(bank[2], 4), ACT.Silu, tk, head_free)
            free[2] = [q_t]
            tk = gemm_cols("win", 28 + h, 3, [(hk(hH), hk(hL), bank[3])], hboth, free[3])
            sg_t = act(sgc[:], bank[3], ACT.Silu, tk, head_free)
            free[3] = [sg_t]
            st_t = {}
            for d in range(2):
                for c in range(6):
                    o = b128(0, c) if c < 4 else b128(1, c - 4)
                    x = mm(o, kd[d][:, c, :], vr[:, c, :], True, True, kd_t[d], v_t, free[0], free[1], inc=int(c == 5))
                first, second = ((4, 5), (5, 4))[d]
                order = ((0, 1, 2), (3, 2, 1))[d]
                s0 = (0, 3)[d]
                prev = copy(V, stt_[d][:, s0, :], b128(1, first - 4), x, head_free)
                prev = stt(stt_[d][:, s0, :], stt_[d][:, s0, :], f6[:, d, second:second + 1], b128(1, second - 4),
                           ALU.mult, ALU.add, prev, f6_t[d])
                free[1] = [prev]
                for c in order:
                    to = c + (1, -1)[d]
                    prev = stt(stt_[d][:, to, :], stt_[d][:, c, :], f6[:, d, c:c + 1], b128(0, c), ALU.mult, ALU.add,
                               prev)
                free[0] = [prev]
                st_t[d] = prev
            x = tt(P, Z[0], kc[0][:], kc[1][:], ALU.add, kc_t[0], kc_t[1], head_free)
            for c in range(4):
                y = mm(b128(6, c), Z[0][:, c, :], qt[:, c, :], True, True, x, q_t, free[6], inc=int(c == 3))
            z_f = [[y], list(head_free)]
            sc_t = tt(V, scT, b3(bank[6], 4), ident.unsqueeze(1).to_broadcast([128, 4, 128]), ALU.mult, y,
                      head_free)
            free[6] = [sc_t]
            e_free = [t_lm] + list(head_free)
            qa_t = {}
            zi = 0
            for d in range(2):
                for grp in range(2):
                    et = []
                    for c in range(4):
                        b = 2 + c
                        x = mm(bank[b], lf[d][:, c, :], decay[:, d, grp * 512:grp * 512 + 512], True, True, t_dec,
                               lf_t[d], free[b], inc=1)
                        x = act(E4[:, c, :, :], b3(bank[b], 4), ACT.Exp, x, e_free)
                        free[b] = [x]
                        et.append(x)
                    e_free = []
                    for m_ in range(4):
                        mat = grp * 4 + m_
                        if mat == 0:
                            qa_t[d] = tt(V, qa[d][:], qt[:], E4[:, :, 0, :], ALU.mult, et, q_t, head_free)
                            e_free.append(qa_t[d])
                            continue
                        lv = mat - 1
                        b_ = LEVELS[lv]
                        zi += 1
                        zz = Z[zi % 2]

                        def view(y_):
                            return y_.rearrange("p c (n u b) -> p c n u b", u=2, b=b_)

                        uq = (1, 0)[d]
                        Ev, Zv, Qv, Kv = view(E4[:, :, m_, :]), view(zz), view(qt[:]), view(kc[d][:])
                        w1 = pair_mult(V, Zv, Ev, Qv, uq, et, z_f[zi % 2], q_t)
                        w2 = pair_mult(P, Zv, Ev, Kv, 1 - uq, et, z_f[zi % 2], kc_t[d])
                        e_free += [w1, w2]
                        pb = 6 + zi % 2
                        for c in range(4):
                            x = mm(b128(pb, c), zz[:, c, :], zz[:, c, :], True, True, w1, w2, free[pb],
                                   inc=int(c == 3))
                        z_f[zi % 2] = [x]
                        mk = lmask[:, 2 * lv + d:2 * lv + d + 1, :].to_broadcast([128, 4, 128])
                        sc_t = V.put(lambda e, mk=mk, y_=b3(bank[pb], 4): e.copy_predicated(scT, mk, y_), x, sc_t,
                                     t_lm)
                        free[pb] = [sc_t]
            for c in range(4):
                mm(b128(2, c), vr[:, c, :], scT[:, c, :], True, False, v_t, sc_t, free[2])
                mm(b128(2, c), stt_[0][:, c, :], qa[0][:, c, :], False, False, st_t[0], qa_t[0])
                x = mm(b128(2, c), stt_[1][:, c, :], qa[1][:, c, :], False, True, st_t[1], qa_t[1], inc=1)
            a = sumsq(lambda k: bank[2], 1, S, C("ones"), 3, lambda k: [x])
            r, a1 = rsqrt_of(rs[:], bank[3], 128, a, rs_free[0])
            free[3] = [a1]
            y = stt(yc[:, h, :], bank[2], M("gn"), rs[:], ALU.mult, ALU.mult, r, x)
            free[2] = [y]
            rs_free[0] = [y]
            y = tt(P, yc[:, h, :], yc[:, h, :], sgc[:], ALU.mult, y, sg_t)
            head_free = fence()
        debug("yc", yc[:], y)

        f2 = fence()
        join(f2, V, A, P, PE)
        top[0] = mark3
        yH, yL = sb("yH", [128, 12, S], R), sb("yL", [128, 12, S], R)
        acc = [sb(f"acc{i}", [128, S]) for i in range(2)]
        gt = [sb(f"gt{i}", [128, S]) for i in range(2)]
        tmp = [sb(f"tmp{i}", [128, S]) for i in range(2)]
        top[0] = mark1
        mH, mL = sb("mH", [128, KD, S], R), sb("mL", [128, KD, S], R)
        ty = rows_to_cols(lambda i, c: mixed2[:, i, c * 128:c * 128 + 128], 8, hk(yH), hk(yL), [tA, tB], None)
        join(pe_done(), V, A, P)
        for c in range(4):
            a = copy(A, yH[:, 8 + c, :], yc[:, c, :])
            b = tt(P, yL[:, 8 + c, :], yc[:, c, :], yH[:, 8 + c, :].bitcast(F), ALU.subtract, a)
            ty += [a, b]
        acc_f, gt_f, tmp_f = [[], []], [[], []], [[], []]
        tm_ = []
        n = 0
        for m in range(8):
            j = m % 2
            for br in range(3):
                z = n % 2
                n += 1
                tk = gemm_cols("win", 32 + 8 * br + m, z, [(hk(hH), hk(hL), bank[z])], hboth, free[z])
                g_ = act(gt[z][:], bank[z], ACT.Sigmoid, tk, gt_f[z])
                free[z] = [g_]
                tk = gemm_cols("wbr", 8 * br + m, 2 + z, [(lambda k, br=br: yH[:, 4 * br + k, :],
                                                           lambda k, br=br: yL[:, 4 * br + k, :], bank[2 + z])],
                               ty, free[2 + z])
                if br == 0:
                    a = tt(V, acc[j][:], bank[2 + z], gt[z][:], ALU.mult, tk, g_, acc_f[j])
                    free[2 + z], gt_f[z] = [a], [a]
                    prev = a
                else:
                    a = tt(V, tmp[z][:], bank[2 + z], gt[z][:], ALU.mult, tk, g_, tmp_f[z])
                    free[2 + z], gt_f[z] = [a], [a]
                    prev = tt(P, acc[j][:], acc[j][:], tmp[z][:], ALU.add, a, prev)
                    tmp_f[z] = [prev]
            a = copy(A, mH[:, m, :], acc[j][:], prev)
            b = tt(P, mL[:, m, :], acc[j][:], mH[:, m, :].bitcast(F), ALU.subtract, a, prev)
            acc_f[j] = [a, b]
            tm_ += [a, b]
        h_done[0] = [tk]
        for m in range(8):
            b = 4 + m % 3
            tk = gemm_cols("wout", m, b, [(hk(mH), hk(mL), bank[b])], tm_, free[b])
            add_x(m, b, tk, modT[:, 16 + m, 0:1], tmod)
        xdbg("x3")
        f3 = fence()
        ffn(2, "up2", "dn2", lambda k: gf[:, k:k + 1], TAPS2, "dw2", "db2", False, f3,
            shift=lambda k: modT[:, 24 + k, 0:1], gtok=smalls2, scale=lambda m: modT[:, 40 + m, 0:1])

    if stop > 3:
        r = norm_scale(lambda k: XT[:, k, :], KD, S, lambda k: xready[k])
        g = "final2"
    else:
        r = norm_scale(lambda k: XT[:, k, :], KD, S, lambda k: xready[k])
        g = "final"
    d_out = slot("d_out")
    for k in range(KD):
        a = stt(XT[:, k, :], XT[:, k, :], M(g, k, k + 1), rs[:], ALU.mult, ALU.mult, r, xready[k])
        tk = SP.dma(lambda e, k=k: e.dma_start(out[:, k, :], XT[:, k, :]), d_out, a)
    SP.items.append(([tk], lambda e: None, None, 0))
    SP.items.append(([t_toep], lambda e: None, None, 0))

    print("sbuf", hw_ffn, top, nc.sbuf_usable_end) if dbg else None
    blk = ctx.enter_context(nc.Block())

    @blk.sync
    def _(e):
        SP.run(e)

    @blk.tensor
    def _(e):
        PE.run(e)

    @blk.vector
    def _(e):
        V.run(e)

    @blk.scalar
    def _(e):
        A.run(e)

    @blk.gpsimd
    def _(e):
        P.run(e)


def constants():
    c = np.zeros((128, N_CN), np.float32)

    def put(name, v):
        c[:, CN[name][0]:CN[name][1]] = v

    i = np.arange(128)
    put("ident", np.eye(128))
    put("ones", 1.0)
    put("blk", (i[:, None] // 64 == i[None, :] // 64))
    put("anti", np.eye(128)[::-1])
    put("causal", np.where(i[None, :] <= 127 - i[:, None], 0.0, -BIG))
    rot = np.zeros((128, 128), np.float32)
    for a in range(64):
        rot[2 * a + 1, 2 * a] = -1.0
        rot[2 * a, 2 * a + 1] = 1.0
    put("rot", rot)
    s, tt_ = i[:, None], i[None, :]
    put("uf", s > tt_)
    put("ub", s < tt_)
    mf, mb = [s <= tt_], [s >= tt_]
    masks = []
    for b in LEVELS:
        mid = tt_ // (2 * b) * (2 * b) + b
        up = tt_ >= mid
        mf.append(np.where(up, (s >= mid) & (s <= tt_), (s > tt_) & (s < mid)))
        mb.append(np.where(up, (s >= mid) & (s < tt_), (s >= tt_) & (s < mid)))
        same = s // (2 * b) == tt_ // (2 * b)
        masks.append(same & (s < mid) & (tt_ >= mid))
        masks.append(same & (s >= mid) & (tt_ < mid))
    msk = np.stack(masks, 1).astype(np.float32)
    w = np.arange(TOEP)
    d = 511 - w
    n = np.maximum(d, 0)
    nf = np.maximum(n, 16).astype(np.float32)
    large = 16 + (np.log(nf / np.float32(16)) / np.float32(math.log(128 / 16)) * np.float32(16)).astype(np.int32)
    bucket = np.where(n < 16, n, np.minimum(large, 31))
    oh = np.zeros((32, TOEP), np.float32)
    oh[bucket, w] = -1.0
    mr = np.zeros((32, TOEP), np.float32)
    mr[:, d < 0] = BIG
    cnt = ((d >= 0) & (d <= 128)).astype(int) + ((d >= 0) & (d % 4 == 0)) + ((d >= 0) & (d % 16 == 0))
    mr[16:, :] = np.where(cnt > 0, -np.log(np.maximum(cnt, 1)), BIG)
    tpos = np.arange(S)
    inv = (np.float32(10000.0) ** (-np.arange(0, 32, 2, dtype=np.float32) / np.float32(32))).astype(np.float32)
    ang = np.concatenate([(tpos // 64).astype(np.float32)[:, None] * inv, (tpos % 64).astype(np.float32)[:, None] * inv], 1)
    cs = np.stack([np.cos(ang), np.sin(ang)], 0).astype(np.float32)
    cs = np.repeat(cs, 2, axis=2).transpose(2, 0, 1)
    cs = np.concatenate([cs, cs], 0)
    j = np.arange(384)
    near = np.where(np.abs(j[None, :] - 128 - i[:, None]) <= 128, 0.0, BIG)
    band = np.zeros((128, 1152), np.float32)
    band[:, 256:640] = near
    band[:, 896:] = near[:, 128:]
    return {"consts": c, "decay": np.stack([np.concatenate(mf, 1), np.concatenate(mb, 1)], 1).astype(np.float32), "lmask": msk, "onehot": oh, "maskrow": mr, "ropes": np.ascontiguousarray(cs), "band": band}


def pack(w, kt=None):
    K, N = w.shape
    return np.ascontiguousarray(w.reshape(K // 128, 128, N // 128, 128).transpose(2, 1, 0, 3)).reshape(
        N // 128, 128, K)


def cols(v):
    return v.reshape(-1, 128).T


def lay(i):
    o = constants()
    g = {k: np.asarray(v) for k, v in i.items()}
    sm = np.zeros((128, N_SM), np.float32)

    def put(name, v):
        sm[:, SM[name][0]:SM[name][1]] = v

    for l in range(2):
        put(f"attn{l}", cols(g["attn_norm"][l]))
        put(f"ffn{l}", cols(g["ffn_norm"][l]))
        put(f"cw{l}", cols(g["conv_w"][l]))
        put(f"cb{l}", cols(g["conv_b"][l]))
    put("final", cols(g["final_norm"]))
    put("mix2", cols(g["norm_mix_2"]))
    put("ffn2", cols(g["norm_ffn_2"]))
    put("final2", cols(g["norm_final_2"]))
    put("dw2", cols(g["w_dw_2"]))
    put("db2", cols(g["b_dw_2"]))
    put("bmod", cols(g["b_mod_2"]))
    put("idxk", np.tile(g["idx_k_norm"].reshape(64), 2)[:, None])
    put("qn", np.tile(g["qn_b_2"].reshape(64), 2)[:, None])
    put("kn", np.tile(g["kn_b_2"].reshape(64), 2)[:, None])
    put("gn", g["gn_c_2"].reshape(128, 1))
    put("sink", np.broadcast_to(g["sink_a_2"].reshape(1, 8), (128, 8)))
    put("c", cols(g["c_2"]))
    put("cctx", cols(g["c_ctx_2"]))
    o["smalls"] = sm
    o["xT"] = np.ascontiguousarray(g["x"][0].T.reshape(8, 128, S).transpose(1, 0, 2))
    o["ctxT"] = np.ascontiguousarray(g["ctx_2"][0].T.reshape(8, 128, CTX).transpose(1, 0, 2))
    o["rel"] = np.concatenate([g["rel_bias"], g["rel_bias"]], 1)
    we = g["w_in_even"][0]
    o["we"] = np.concatenate([pack(np.concatenate([we[:, 4096:4160], we[:, 4096:4160]], 1)), pack(we[:, 3072:4096]),
                              pack(we[:, :3072])], 0)
    o["wi"] = np.ascontiguousarray(we[:, 4160:4176].reshape(8, 128, 16).transpose(1, 0, 2)).reshape(1, 128, 128)
    o["wq1"] = pack(g["w_in_odd"][0])
    for l in range(2):
        o[f"wo{l}"] = pack(g["w_o"][l])
        o[f"up{l}"] = pack(g["w_up"][l])
        o[f"dn{l}"] = np.concatenate([pack(g["w_down"][l][:1408]), pack(g["w_down"][l][1408:])], 0)
    o["wmod"] = pack(g["w_mod_2"][0])
    wi = g["w_in_2"][0]
    perm = np.concatenate([np.arange(h * 64, h * 64 + 64) for c in range(4) for h in (c, c + 4)])
    aq, bq = wi[:, :512][:, perm], wi[:, 768:1280][:, perm]
    o["win"] = pack(np.concatenate([aq, wi[:, 512:768], bq, wi[:, 1280:]], 1))
    o["wbr"] = np.concatenate([pack(g["w_branch_2"][0, n]) for n in range(3)], 0)
    o["wout"] = pack(g["w_out_2"][0])
    o["up2"] = pack(g["w_up_2"][0])
    o["dn2"] = np.concatenate([pack(g["w_down_2"][0][:1408]), pack(g["w_down_2"][0][1408:])], 0)
    return o


def kernel(**inputs):
    import concourse.bacc as _bacc
    from concourse.bass_utils import run_bass_kernel_spmd as _run

    nc = _bacc.Bacc("TRN2", target_bir_lowering=False, num_devices=1)
    arrays = lay(inputs)
    t = {k: nc.dram_tensor(f"in_{k}", v.shape, mybir.dt.from_np(v.dtype), kind="ExternalInput").ap()
         for k, v in arrays.items()}
    t["toep"] = nc.dram_tensor("toep", (32, TOEP), F, kind="Internal").ap()
    out = nc.dram_tensor("out_y", (128, KD, S), F, kind="ExternalOutput").ap()
    build(nc, t, out)
    r = _run(nc, [{f"in_{k}": v for k, v in arrays.items()}], core_ids=[0])
    y = r.results[0]["out_y"]
    return np.ascontiguousarray(y.transpose(2, 1, 0)).reshape(1, S, D)
```

```python
import math
from contextlib import ExitStack

import numpy as np

import concourse.bass as bass
from concourse import mybir

F = mybir.dt.float32
R = mybir.dt.float32r
U8 = mybir.dt.uint8
ALU = mybir.AluOpType
ACT = mybir.ActivationFunctionType
AX = mybir.AxisListType

S = 512
D = 1024
KD = 8
DFF = 2816
HALF = 11
CTX = 256
EPS = 1e-6
BIG = 1e30
LOW = -3e38
KEEP = 128
TOEP = 640
LEVELS = (64, 32, 16, 8, 4, 2, 1)
N_SLOT = HALF * 128

SM = {}
_at = 0
for _name, _n in (("attn0", 8), ("attn1", 8), ("ffn0", 8), ("ffn1", 8), ("final", 8), ("mix2", 8), ("ffn2", 8),
                  ("final2", 8), ("cw0", 132), ("cw1", 132), ("cb0", 44), ("cb1", 44), ("dw2", 132), ("db2", 44),
                  ("bmod", 48), ("idxk", 1), ("qn", 1), ("kn", 1), ("gn", 1), ("sink", 8), ("c", 8), ("cctx", 8)):
    SM[_name] = (_at, _at + _n)
    _at += _n
N_SM = _at

CN = {}
_at = 0
for _name, _n in (("ident", 128), ("ones", 128), ("blk", 128), ("causal", 128), ("rot", 128), ("uf", 128), ("ub", 128), ("anti", 128)):
    CN[_name] = (_at, _at + _n)
    _at += _n
N_CN = _at


def weight_units():
    out = [("we", 0), ("wi", 0)] + [("we", 1 + n) for n in range(8 + 24)]

    def block(wo, up, down):
        for m in range(8):
            out.append((wo, m))
        for half in range(2):
            for j in range(HALF):
                n = half * HALF + j
                out.append((up, n))
                out.append((up, 22 + n))
            for m in range(8):
                out.append((down, half * 8 + m))

    block("wo0", "up0", "dn0")
    for n in range(24):
        out.append(("wq1", n))
    block("wo1", "up1", "dn1")
    for n in [4, 5, 10, 11] + [0, 1, 2, 3] + [6, 7, 8, 9]:
        out.append(("win", n))
    for h in range(4):
        for base in (16, 24, 12, 20, 28):
            out.append(("win", base + h))
    for m in range(8):
        for n in range(3):
            out.append(("win", 32 + 8 * n + m))
            out.append(("wbr", 8 * n + m))
    block("wout", "up2", "dn2")
    return out


KTS = {"we": 8, "wi": 8, "wq1": 8, "win": 8, "wbr": 4, "wout": 8}
for _l in range(3):
    KTS[f"up{_l}"] = 8
    KTS[f"dn{_l}"] = HALF
    KTS[f"wo{_l}"] = 8


class Queue:

    def __init__(self, sem):
        self.sem, self.n, self.items = sem, 0, []

    def put(self, fn, *waits, inc=1):
        self.items.append((flat(waits), fn, self.sem, inc))
        self.n += inc
        return (self.sem, self.n)

    def dma(self, fn, slot, *waits):
        slot[1] += 16
        self.items.append((flat(waits), fn, slot[0], 16))
        return (slot[0], slot[1])

    def run(self, eng):
        seen = {}
        for waits, fn, sem, inc in self.items:
            for s, v in waits:
                if seen.get(id(s), 0) < v:
                    eng.wait_ge(s, v)
                    seen[id(s)] = v
            ins = fn(eng)
            if inc:
                ins.then_inc(sem, inc)


def flat(x):
    out = []
    for y in x:
        if y is None:
            continue
        if isinstance(y, list):
            out += flat(y)
        else:
            out.append(y)
    return out


def build(nc, t, out, dbg=None, stop=99):
    ctx = ExitStack()
    with ctx:
        build_in(nc, t, out, ctx, dbg or {}, stop)


def build_in(nc, t, out, ctx, dbg, stop):
    def sem(name):
        return ctx.enter_context(nc.semaphore(name))

    PE, V, A, P, SP = (Queue(sem(f"s_{x}")) for x in ("pe", "dve", "act", "pool", "sp"))

    base0 = (nc.sbuf_base + 63) // 64 * 64
    top = [base0]


    def sb(name, shape, dt=F, at=None):
        n = int(np.prod(shape[1:])) * (1 if dt == U8 else 4)
        n = (n + 63) // 64 * 64
        if at is None:
            off = top[0]
            top[0] += n
        else:
            off = at
        assert off + n <= nc.sbuf_usable_end, (name, off + n)
        return nc.alloc_sbuf_tensor_at(name, list(shape), dt, offset=off)

    ps = [ctx.enter_context(nc.psum_tensor(f"ps{i}", [128, 1024], F)) for i in range(4)]
    bank = [ps[i // 2][:, (i % 2) * 512:(i % 2) * 512 + 512] for i in range(8)]
    free = [[] for _ in range(8)]

    def slot(name):
        return [sem(name), 0]

    XT = sb("XT", [128, KD, S])
    hH = sb("hH", [128, KD, S], R)
    hL = sb("hL", [128, KD, S], R)
    NR, NH = 3, 3
    ring_at = top[0]
    rawb = [sb(f"raw{i}", [128, N_SLOT]) for i in range(NR)]
    wHb = [sb(f"wH{i}", [128, N_SLOT], R) for i in range(NH)]
    wLb = [sb(f"wL{i}", [128, N_SLOT], R) for i in range(NH)]
    tails = [ring_at + i * N_SLOT * 4 + 4096 for i in range(NR + 2 * NH)]
    sm = sb("sm", [128, N_SM])
    cn = sb("cn", [128, N_CN])
    modT = sb("modT", [128, 48, 2])
    cs = sb("cs", [128, KD, 2])
    sc1 = sb("sc1", [128, 64])
    mark0 = top[0]

    def C(name, a=0, b=None):
        lo, hi = CN[name]
        return cn[:, lo + a:(hi if b is None else lo + b)]

    def M(name, a=0, b=None):
        lo, hi = SM[name]
        return sm[:, lo + a:(hi if b is None else lo + b)]

    ident = C("ident")
    d_cn, d_sm, d_x, d_misc = slot("d_cn"), slot("d_sm"), slot("d_x"), slot("d_misc")
    t_sm = SP.dma(lambda e: e.dma_start(sm[:], t["smalls"]), d_sm)
    t_x = SP.dma(lambda e: e.dma_start(XT[:], t["xT"]), d_x)
    t_cn = SP.dma(lambda e: e.dma_start(cn[:], t["consts"]), d_cn)

    units = weight_units()
    d_raw = [slot(f"d_raw{i}") for i in range(NR)]
    U = {"load": 0, "split": 0, "take": 0, "hs": 0, "rel": 0}
    raw_tok, raw_free, h_tok, h_slot = {}, {}, {}, {}
    h_free = [[] for _ in range(NH)]

    def size(n):
        name = units[n][0]
        kt = KTS[name]
        return kt, (16 if name == "wi" else 128)

    def advance():
        while True:
            n = U["load"]
            if n < len(units) and (n < NR or (n - NR) in raw_free):
                kt, nc_ = size(n)
                name, i = units[n]
                dst = rawb[n % NR][:, :kt * nc_]
                src = t[name][i]
                raw_tok[n] = SP.dma(lambda e, dst=dst, src=src: e.dma_start(dst, src), d_raw[n % NR],
                                    raw_free.get(n - NR))
                U["load"] += 1
                continue
            n = U["split"]
            if n < U["load"] and n < U["take"] + 4:
                if U["hs"] < U["rel"] + NH:
                    k = U["hs"] % NH
                    kt, nc_ = size(n)
                    r, H, L = rawb[n % NR][:, :kt * nc_], wHb[k][:, :kt * nc_], wLb[k][:, :kt * nc_]
                    th = split_hi(H, r, raw_tok[n], h_free[k])
                    tl = V.put(lambda e, L=L, r=r, H=H: e.tensor_tensor(L, r, H.bitcast(F), ALU.subtract), th)
                    h_tok[n], h_slot[n] = [th, tl], k
                    raw_free[n] = [tl]
                    U["hs"] += 1
                    U["split"] += 1
                    continue
            break

    def split_hi(H, r, *w):
        return A.put(lambda e: e.activation(H, r, ACT.Copy), *w)

    def take(name, i):
        n = U["take"]
        assert units[n] == (name, i), (units[n], name, i)
        U["take"] += 1
        advance()
        kt, nc_ = size(n)
        k = h_slot[n]
        return (n, wHb[k][:, :kt * nc_].rearrange("p (k c) -> p k c", k=kt),
                wLb[k][:, :kt * nc_].rearrange("p (k c) -> p k c", k=kt), h_tok[n])

    def release(n, tok):
        h_free[h_slot[n]] = [tok]
        U["rel"] += 1
        advance()

    def mm(o, l, r, start, stop, *w, inc=0):
        return PE.put(lambda e: e.matmul(o, l, r, start=start, stop=stop), *w, inc=inc)

    def gemm_cols(name, i, parts, *w):
        n, H, L, tok = take(name, i)
        kt = size(n)[0]
        last = None
        for xH, xL, o, xt in parts:
            for k in range(kt):
                mm(o, H[:, k, :], xH(k), k == 0, False, tok, xt[k], *w)
                mm(o, H[:, k, :], xL(k), False, False)
                last = mm(o, L[:, k, :], xH(k), False, k == kt - 1, inc=int(k == kt - 1))
        release(n, last)
        return last

    def gemm_rows16(name, i, parts, *w):
        n, H, L, tok = take(name, i)
        last = None
        for xH, xL, o in parts:
            for k in range(KD):
                mm(o, xH(k), H[:, k, :], k == 0, False, tok, *w)
                mm(o, xH(k), L[:, k, :], False, False)
                last = mm(o, xL(k), H[:, k, :], False, k == KD - 1, inc=int(k == KD - 1))
        release(n, last)
        return last

    def copy(q, o, i, *w, scale=1.0):
        if q is A:
            return A.put(lambda e: e.activation(o, i, ACT.Copy, scale=scale), *w)
        if scale == 1.0:
            return q.put(lambda e: e.tensor_copy(o, i), *w)
        return q.put(lambda e: e.tensor_scalar(o, i, scale, None, ALU.mult), *w)

    def act(o, i, f, *w, **kw):
        return A.put(lambda e: e.activation(o, i, f, **kw), *w)

    def tt(q, o, a, b, op, *w):
        return q.put(lambda e: e.tensor_tensor(o, a, b, op), *w)

    def stt(o, a, s, b, op0, op1, *w):
        return V.put(lambda e: e.scalar_tensor_tensor(o, a, s, b, op0, op1), *w)

    def ts(q, o, a, s1, s2, op0, op1, *w):
        if s2 is None:
            return q.put(lambda e: e.tensor_scalar(o, a, s1, None, op0), *w)
        return q.put(lambda e: e.tensor_scalar(o, a, s1, s2, op0, op1), *w)

    def pair_mult(q, o, a, b, u, *w):
        return q.put(lambda e: e.tensor_tensor(o[:, :, :, u, :], a[:, :, :, u, :], b[:, :, :, u, :], ALU.mult), *w)

    sq = [sb(f"sq{i}", [128, S]) for i in range(2)]
    sq_free = [[], []]
    rs = sb("rs", [128, S])
    hf = [sb(f"hf{i}", [128, S]) for i in range(2)]
    hf_free = [[], []]
    rs_free = [[]]
    eps_t = sb("eps_t", [128, 1])
    mn = sb("mn", [128, 16, 4])
    den = sb("den", [128, 16, 4])
    t_eps = V.put(lambda e: e.memset(eps_t[:], EPS))
    ssum = sb("ssum", [128, S])
    mark1 = top[0]

    def rsqrt_of(o, ss, n, *w):
        a = act(o, ss, ACT.Ln, t_eps, *w, scale=1.0 / n, bias=eps_t[:, 0:1])
        return act(o, o, ACT.Exp, a, scale=-0.5), a

    def sumsq(x, n, ones, b, ready):
        a = act(sq[0][:, :n], x, ACT.Square, ready, sq_free[0])
        last = mm(bank[b][:, :n], ones, sq[0][:, :n], True, True, a, t_cn, free[b], inc=1)
        sq_free[0] = [last]
        return last

    ss = {"free": [], "tok": None}

    def add_square(x, k, ready):
        n = x.shape[1]
        if k == 0:
            ss["tok"] = act(ssum[:, :n], x, ACT.Square, ready, ss["free"])
            return
        j = k % 2
        a = act(sq[j][:, :n], x, ACT.Square, ready, sq_free[j])
        ss["tok"] = tt(P, ssum[:, :n], ssum[:, :n], sq[j][:, :n], ALU.add, a, ss["tok"])
        sq_free[j] = [ss["tok"]]

    def norm_scale(n, b=7):
        last = mm(bank[b][:, :n], C("ones"), ssum[:, :n], True, True, ss["tok"], t_cn, free[b], inc=1)
        ss["free"] = [last]
        r, a = rsqrt_of(rs[:, :n], bank[b][:, :n], D, last, rs_free[0])
        free[b] = [a]
        return r

    def norm_split(src, n, ready, gain, dH, dL, d_free, shift=None, gtok=None):
        r = norm_scale(n)
        toks = []
        for k in range(KD):
            j = k % 2
            h = hf[j][:, :n]
            a = stt(h, src(k), gain(k), rs[:, :n], ALU.mult, ALU.mult, r, ready(k), hf_free[j], gtok)
            if shift is None:
                c = copy(A, dH(k), h, a, d_free)
                d = tt(P, dL(k), h, dH(k).bitcast(F), ALU.subtract, c, a, d_free)
            else:
                c = act(dH(k), h, ACT.Identity, a, d_free, bias=shift(k))
                d = stt(dL(k), h, shift(k), dH(k).bitcast(F), ALU.add, ALU.subtract, c, d_free)
            hf_free[j] = [c, d]
            toks.append([c, d])
            rs_free[0] = [a]
        return toks

    mrow = sb("mrow", [32, TOEP])
    rel = sb("rel", [32, 32])
    oh = sb("oh", [32, TOEP])
    d_rel = [slot(f"d_rel{i}") for i in range(4)]
    ta = SP.dma(lambda e: e.dma_start(rel[:], t["rel"]), d_rel[0])
    tb = SP.dma(lambda e: e.dma_start(oh[:], t["onehot"]), d_rel[1])
    tc = SP.dma(lambda e: e.dma_start(mrow[:], t["maskrow"]), d_rel[2])
    mm(bank[0][0:32, :], rel[:], oh[:, 0:512], True, True, ta, tb)
    a = mm(bank[1][0:32, 0:TOEP - 512], rel[:], oh[:, 512:TOEP], True, True, inc=1)
    a1 = tt(V, mrow[:, 0:512], bank[0][0:32, :], mrow[:, 0:512], ALU.add, a, tc)
    a2 = tt(V, mrow[:, 512:TOEP], bank[1][0:32, 0:TOEP - 512], mrow[:, 512:TOEP], ALU.add, a)
    free[0], free[1] = [a1], [a2]
    t_toep = SP.dma(lambda e: e.dma_start(t["toep"], mrow[:]), d_rel[3], a1, a2)
    advance()

    def toep_src(h):
        return bass.AP(t["toep"].tensor, h * TOEP, [[1, 128], [1, 512]])

    top[0] = mark1
    tm = [sb(f"tm{i}", [128, S]) for i in range(2)]
    d_tm = [slot(f"d_tm{i}") for i in range(2)]
    Sp = [sb(f"Sp{i}", [128, S]) for i in range(2)]
    Pr = [sb(f"Pr{i}", [128, S]) for i in range(2)]
    Pr.append(sb("Pr2", [128, S]))
    PT_at = top[0]
    PT = [sb(f"PT{i}", [128, 4, S]) for i in range(2)]
    Sp_free, Pr_free, PT_free = [[], []], [[], [], []], [[], []]
    tm_free = [[], []]
    mark2 = top[0]

    def fence():
        return [(q.sem, q.n) for q in (PE, V, A, P)]

    def join(f, *qs):
        for q in qs:
            q.items.append((flat([f]), lambda e: None, None, 0))

    def attention(items, wide, lead, qk, bias, slots, vpair, init, finish, fill=None):
        st = {}
        n = len(items)
        pend = []
        heads = -1
        for step in range(n + 4):
            for f_ in pend:
                f_()
            pend = []
            if step < n:
                h, i = items[step]
                W = 128 * len(slots(h, i))
                sbk = step % 2
                S_ps = ps[sbk]
                fr = free[2 * sbk] + free[2 * sbk + 1]
                last = None
                for lhsT, rhs, col, w_, tok in qk(h, i):
                    last = mm(S_ps[:, col:col + w_], lhsT, rhs, True, True, tok, fr, inc=1)
                j, jp = step % 2, step % 3
                bi = bias(h, i)
                mcol = mn[:, h:h + 1, i]
                ini = init(h)
                if bi is None:
                    m = V.put(lambda e, o=mcol, x=S_ps[:, :W]: e.tensor_reduce(o, x, AX.X, ALU.min), last)
                    src = S_ps[:, :W]
                else:
                    bap, btok = bi
                    if lead:
                        copy(V, Sp[j][:, 0:1], ini, Sp_free[j])
                    m = V.put(lambda e, o=Sp[j][:, lead:lead + W], x=S_ps[:, :W], y=bap, c=mcol, ini=ini:
                              e.tensor_tensor_reduce(o, x, y, 1.0, ini, ALU.add, ALU.min, c),
                              last, btok, Sp_free[j])
                    src = Sp[j][:, :lead + W]
                    free[2 * sbk] = free[2 * sbk + 1] = [m]
                x = act(Pr[jp][:, :lead + W], src, ACT.Exp, m, Pr_free[jp], scale=-1.0, bias=mcol,
                        accum_out=den[:, h:h + 1, i])
                if bi is None:
                    free[2 * sbk] = free[2 * sbk + 1] = [x]
                else:
                    Sp_free[j] = [x]
                if fill is not None:
                    fill(h, i, m)
                st[step] = dict(x=x)
            if 1 <= step <= n:
                h, i = items[step - 1]
                W = 128 * len(slots(h, i))
                p_ = Pr[(step - 1) % 3][:, lead:lead + W]
                dcol = den[:, h:h + 1, i]
                a = V.put(lambda e, d_=dcol: e.reciprocal(d_, d_), st[step - 1]["x"])
                st[step - 1]["p"] = ts(V, p_, p_, dcol, None, ALU.mult, None, a)
            if step >= 3 and step - 3 < n and items[step - 3][1] == 3:
                h = items[step - 3][0]
                heads += 1
                ob = 6 + heads % 2
                z = heads % len(PT)
                cover = {}
                for i in range(4):
                    for b in slots(h, i):
                        cover.setdefault(b, []).append(i)
                order = sorted(cover, key=lambda b: -len(cover[b]))
                assert len(cover[order[0]]) == 4
                for b in order:
                    lo, hi = 128 * cover[b][0], 128 * cover[b][-1] + 128
                    vap, vtok = vpair(h, b)
                    last = mm(bank[ob][:, lo:hi], vap, PT[z][:, b, lo:hi], b == order[0], b == order[-1],
                              st["pt"], vtok, free[ob], inc=int(b == order[-1]))
                PT_free[z] = [last]
                st["pt"] = []
                free[ob], then = finish(h, ob, last)
                pend.append(then)
            if 2 <= step <= n + 1:
                q = step - 2
                h, i = items[q]
                j, jp = q % 2, q % 3
                z = (heads + 1) % len(PT)
                if wide:
                    T_ps, tb_ = ps[2], [4, 5]
                else:
                    T_ps, tb_ = ps[2][:, 512 * j:512 * j + 512], [4 + j]
                bs = slots(h, i)
                for n_ in range(len(bs)):
                    c_ = n_ * 128
                    last = PE.put(lambda e, o=T_ps[:, c_:c_ + 128], x=Pr[jp][:, lead + c_:lead + c_ + 128]:
                                  e.transpose(o, x, ident), st[q]["p"], t_cn, [free[y] for y in tb_],
                                  inc=int(n_ == len(bs) - 1))
                Pr_free[jp] = [last]
                runs = []
                for n_, b in enumerate(bs):
                    if runs and b == runs[-1][1] + runs[-1][2]:
                        runs[-1][2] += 1
                    else:
                        runs.append([n_, b, 1])
                cs_ = []
                for n_, b, w_ in runs:
                    eq = (A, V)[q % 2]
                    cs_.append(copy(eq, PT[z][:, b:b + w_, i * 128:i * 128 + 128],
                                    T_ps[:, n_ * 128:(n_ + w_) * 128].rearrange("p (b n) -> p b n", n=128), last,
                                    PT_free[z]))
                for y in tb_:
                    free[y] = list(cs_)
                st["pt"] = st.get("pt", []) + cs_
        for f_ in pend:
            f_()
        return fence()

    def in_blocks(x):
        return x.rearrange("p (i n) -> p i n", n=128)

    def turned(x):
        return x.rearrange("p (i n) -> p i n", n=128)[:, :, ::-1]

    def hk(z):
        return lambda k: z[:, k, :]

    xready = {k: [t_x] for k in range(KD)}
    h_done = [[]]
    for k in range(KD):
        add_square(XT[:, k, :], k, t_x)

    def add_x(m, b, tok, scale=None, w=None, square=True):
        if scale is None:
            a = tt(V, XT[:, m, :], bank[b], XT[:, m, :], ALU.add, tok, xready[m])
        else:
            a = stt(XT[:, m, :], bank[b], scale, XT[:, m, :], ALU.mult, ALU.add, tok, xready[m], w)
        free[b] = [a]
        xready[m] = [a]
        if square:
            add_square(XT[:, m, :], m, a)
        return a

    def pe_done():
        return (PE.sem, PE.n)

    dslots = {}

    def debug(name, ap, *w):
        if name in dbg:
            dslots[name] = slot("dbg_" + name)
            tk = SP.dma(lambda e: e.dma_start(dbg[name], ap), dslots[name], *w)
            SP.items.append(([tk], lambda e: None, None, 0))
            return tk

    def xdbg(name):
        tk = debug(name, XT[:], [xready[m] for m in range(8)])
        if tk:
            for m in range(8):
                xready[m] = xready[m] + [tk]

    later = []

    def flush_later():
        while later:
            later.pop(0)()

    macc_free = [[], [], [], []]
    mod_state = {"i": 0, "n": 0, "last": None}

    def mod_unit():
        if "cs" not in mod_state:
            a1 = act(cs[:, :, 0], M("c"), ACT.Silu, t_sm)
            a2 = act(cs[:, :, 1], M("cctx"), ACT.Silu, t_sm)
            mod_state["cs"] = [a1, a2]
        u = mod_state["n"]
        mod_state["n"] += 1
        W_, tok = mbuf[u % 4], m_tok.pop(u)
        for r_ in range(2 if u < 16 else 1):
            j = mod_state["i"] % 4
            mod_state["i"] += 1
            a = ts(V, macc[j][:], W_[:, 0, :], cs[:, 0, r_:r_ + 1], None, ALU.mult, None, tok, mod_state["cs"],
                   macc_free[j])
            for k in range(1, KD):
                a = stt(macc[j][:], W_[:, k, :], cs[:, k, r_:r_ + 1], macc[j][:], ALU.mult, ALU.add, a)
            macc_t = a

            def total(j=j, r_=r_, a=a):
                x = mm(bank[7][:, 2 * u + r_:2 * u + r_ + 1], macc[j][:], C("ones", 0, 1), True, True, a, t_cn,
                       free[7], inc=1)
                macc_free[j] = [x]
                mod_state["last"] = x

            later.append(total)
        mbuf_free[u % 4] = [macc_t]

    m_tok, mbuf_free = {}, [[], [], [], []]
    d_mod = [slot(f"d_mod{i}") for i in range(4)]

    def mod_load(u):
        mod_state["loaded"] = u + 1
        m_tok[u] = SP.dma(lambda e: e.dma_start(mbuf[u % 4][:, :, :].rearrange("p k c -> p (k c)"), t["wmod"][u]),
                          d_mod[u % 4], mbuf_free[u % 4])

    def mod_flush():
        flush_later()
        lo, hi = mod_state.get("from", 0), mod_state["n"]
        if hi > lo:
            pm = bank[7][:, 0:96].rearrange("p (a b) -> p a b", b=2)
            a = tt(V, modT[:, lo:hi, 0], pm[:, lo:hi, 0], M("bmod")[:, lo:hi], ALU.add, mod_state["last"], t_sm)
            mid = min(hi, 16)
            if mid > lo:
                a = tt(V, modT[:, lo:mid, 1], pm[:, lo:mid, 1], M("bmod")[:, lo:mid], ALU.add, mod_state["last"], t_sm)
            free[7] = [a]
            mod_state["from"] = hi
            mod_state["tok"] = a

    top[0] = mark1
    gH = sb("gH", [128, HALF, S], R)
    gL = sb("gL", [128, HALF, S], R)
    cv = [sb(f"cv{i}", [128, S]) for i in range(2)]
    cg_ = [sb(f"cg{i}", [128, S]) for i in range(2)]
    sg = [sb(f"sg{i}", [128, S]) for i in range(2)]
    macc = [sb(f"macc{i}", [128, 128]) for i in range(4)]
    mbuf = [sb(f"mbuf{i}", [128, KD, 128]) for i in range(4)]
    hw_ffn = top[0]
    ffn_free = {"cv": [[], []], "cg": [[], []], "sg": [[], []], "g": []}

    def ffn(layer, up, down, gain, taps, cw, cb, spare, start, shift=None, gtok=None, scale=None):
        hw = norm_split(lambda k: XT[:, k, :], S, lambda k: xready[k], gain, hk(hH), hk(hL), h_done[0], shift, gtok)
        for q in "cv", "cg", "sg":
            ffn_free[q] = [list(start), list(start)]
        ffn_free["g"] = list(start)
        if spare:
            macc_free[:] = [list(start) for _ in macc]
            mbuf_free[:] = [list(start) for _ in mbuf]
            end = mod_state["n"] + 24
            for u in range(4):
                mod_load(mod_state["n"] + u)
            assert mod_state["loaded"] == mod_state["n"] + 4

        def conv(b, n, dst, tok, fr):
            off0, j0 = taps[0]
            assert off0 == 0
            a = act(dst, bank[b], ACT.Identity, tok, fr, t_sm, scale=M(cw, j0 * 44 + n, j0 * 44 + n + 1),
                    bias=M(cb, n, n + 1))
            for off, j in taps[1:]:
                w_ = M(cw, j * 44 + n, j * 44 + n + 1)
                if off > 0:
                    a = stt(dst[:, off:], bank[b][:, :S - off], w_, dst[:, off:], ALU.mult, ALU.add, a)
                else:
                    a = stt(dst[:, :S + off], bank[b][:, -off:], w_, dst[:, :S + off], ALU.mult, ALU.add, a)
            free[b] = [a]
            return a

        for half in range(2):
            g_tok = []
            for j in range(HALF):
                n = half * HALF + j
                z = j % 2
                bv, bg = 0 + z, 2 + z
                tv = gemm_cols(up, n, [(hk(hH), hk(hL), bank[bv], hw)], free[bv])
                av = conv(bv, n, cv[z][:], tv, ffn_free["cv"][z])
                tg = gemm_cols(up, 22 + n, [(hk(hH), hk(hL), bank[bg], hw)], free[bg])
                ag = conv(bg, 22 + n, cg_[z][:], tg, ffn_free["cg"][z])
                flush_later()
                s_ = act(sg[z][:], cg_[z][:], ACT.Silu, ag, ffn_free["sg"][z])
                ffn_free["cg"][z] = [s_]
                p_ = tt(P, sg[z][:], sg[z][:], cv[z][:], ALU.mult, s_, av)
                ffn_free["cv"][z] = [p_]
                gh = copy(A, gH[:, j, :], sg[z][:], p_, ffn_free["g"])
                gl = tt(P, gL[:, j, :], sg[z][:], gH[:, j, :].bitcast(F), ALU.subtract, gh, ffn_free["g"])
                ffn_free["sg"][z] = [gl]
                g_tok.append([gh, gl])
                if spare:
                    while mod_state["loaded"] < min(end, mod_state["n"] + 4):
                        mod_load(mod_state["loaded"])
                    for _ in range(2 if j == 0 else 1):
                        mod_unit()
            h_done[0] = [pe_done()]
            for m in range(8):
                b = 4 + m % 3
                tk = gemm_cols(down, half * 8 + m, [(hk(gH), hk(gL), bank[b], g_tok)], free[b])
                add_x(m, b, tk, None if scale is None else scale(m), gtok, half == 1)
            ffn_free["g"] = [tk]
        if spare:
            mod_flush()
        return [tk, ffn_free["sg"][0], ffn_free["sg"][1], [xready[m] for m in range(8)]]

    TAPS1 = ((0, 2), (1, 1), (2, 0))
    TAPS2 = ((0, 1), (1, 0), (-1, 2))

    def attn_load_bias(h, slot_i, row, need):
        return SP.dma(lambda e: e.dma_start(tm[slot_i][:], toep_src(row)), d_tm[slot_i], t_toep, need)

    top[0] = mark2
    qT = sb("qT", [128, 8, S])
    kT = sb("kT", [128, 8, S])
    vR = sb("vR", [128, 4, D])
    kiT = Pr[2]
    wiR = sb("wiR", [128, 4, 16])
    sco = [None] + [sb(f"sco{i}", [128, 128 * (i + 1)]) for i in range(1, 4)]
    m8 = sb("m8", [128, 8])
    rl = Pr
    bz = sq
    qiT = sb("qiT", [128, 8, S], at=PT_at)

    def att_gain(name):
        return lambda k: M(name, k, k + 1)

    hw = norm_split(lambda k: XT[:, k, :], S, lambda k: xready[k], att_gain("attn0"), hk(hH), hk(hL), None,
                    gtok=t_sm)
    tk = gemm_cols("we", 0, [(hk(hH), hk(hL), bank[0], hw)], free[0])
    c0 = copy(V, kiT[:], bank[0], tk)
    free[0] = [c0]
    a = sumsq(kiT[:], S, C("blk"), 6, [c0])
    r, a = rsqrt_of(rs[:], bank[6], 64, a, rs_free[0])
    free[6] = [a]
    t_ki = stt(kiT[:], kiT[:], M("idxk"), rs[:], ALU.mult, ALU.mult, r, c0)
    rs_free[0] = [t_ki]
    tk = gemm_rows16("wi", 0, [(lambda k, i=i: hH[:, k, i * 128:i * 128 + 128], lambda k, i=i: hL[:, k, i * 128:i * 128 + 128],
                              bank[1][:, i * 16:i * 16 + 16]) for i in range(4)], hw, free[1])
    w64 = wiR[:].rearrange("p a b -> p (a b)")
    a = ts(V, w64, bank[1][:, 0:64], 0.25, None, ALU.mult, None, tk)
    free[1] = [a]
    tk = mm(bank[1][:, 0:64], C("anti"), w64, True, True, a, t_cn, free[1], inc=1)
    t_wi = copy(V, w64, bank[1][:, 0:64], tk)
    free[1] = [t_wi]
    t_qi = []
    for c in range(8):
        b = c % 4
        tk = gemm_cols("we", 1 + c, [(hk(hH), hk(hL), bank[b], hw)], free[b])
        a = copy((V, A)[c % 2], turned(qiT[:, c, :]), in_blocks(bank[b]), tk)
        free[b] = [a]
        t_qi.append(a)
    t_sco = {}
    sc_free = [[], []]
    n = 0
    for i in range(1, 4):
        W = 128 * (i + 1)
        prev = None
        for h in range(16):
            b, z = 4 + n % 3, n % 2
            p0 = 64 * (h % 2)
            tk = mm(bank[b][:, :W], qiT[p0:p0 + 64, h // 2, i * 128:i * 128 + 128], kiT[p0:p0 + 64, :W], True, True,
                    t_ki, t_qi[h // 2], free[b], inc=1)
            a = act(rl[z][:, :W], bank[b][:, :W], ACT.Relu, tk, sc_free[z], scale=0.125)
            free[b] = [a]
            w_ = wiR[:, i, h:h + 1]
            if h == 0:
                prev = ts(V, sco[i][:], rl[z][:, :W], w_, None, ALU.mult, None, a, t_wi)
            else:
                prev = stt(sco[i][:], rl[z][:, :W], w_, sco[i][:], ALU.mult, ALU.add, a, prev, t_wi)
            sc_free[z] = [prev]
            n += 1
        prev = tt(V, sco[i][:, W - 128:W], sco[i][:, W - 128:W], C("causal"), ALU.add, prev, t_cn)
        t_sco[i] = prev
    topk_prog = []

    def topk_steps():
        for i in range(1, 4):
            src = sco[i]
            prev = t_sco[i]
            for r_ in range(KEEP // 8):
                a = V.put(lambda e, i=i: e.max(m8[:], sco[i][:]), prev)
                prev = V.put(lambda e, i=i: e.match_replace(sco[i][:], m8[:], sco[i][:], LOW), a)
                if r_ % 4 == 3:
                    yield None
            t_sco[i] = ts(V, sco[i][:], sco[i][:], -2e38, BIG, ALU.is_gt, ALU.mult, prev)
            yield None

    def v_unit(name, c, b, dst, key, *w):
        tk = gemm_cols(name, c, [(hk(hH), hk(hL), bank[b], hw)], free[b])
        j = c % 2
        a = copy(A, sq[j][:], bank[b], tk, sq_free[j])
        free[b] = [a]
        flush_later()

        def turn():
            z = 4 + j
            for i in range(4):
                x = PE.put(lambda e, o=bank[z][:, i * 128:i * 128 + 128], i_=sq[j][:, i * 128:i * 128 + 128]:
                           e.transpose(o, i_, ident), a, t_cn, free[z], inc=int(i == 3))
            sq_free[j] = [x]
            free[z] = [copy(A, dst, in_blocks(bank[z]), x, *w)]
            t_qk[key] = free[z][0]

        later.append(turn)

    tki = topk_steps()
    t_qk = {}
    for c in range(24):
        b = c % 4
        kind, cc = (c % 12) // 4, c % 4
        g = c // 12
        if kind < 2:
            tk = gemm_cols("we", 9 + c, [(hk(hH), hk(hL), bank[b], hw)], free[b])
            flush_later()
            dst = (qT, kT)[kind][:, g * 4 + cc, :]
            a = copy(A, turned(dst) if kind == 0 else in_blocks(dst), in_blocks(bank[b]), tk,
                     scale=(-0.125, 1.0)[kind])
            free[b] = [a]
            t_qk[(g, kind, cc)] = a
        else:
            o = g * 512 + cc * 128
            v_unit("we", 9 + c, b, vR[:, :, o:o + 128], (g, kind, cc))
        next(tki, None)
    flush_later()
    for _ in tki:
        pass
    h_done[0] = [pe_done()]

    def run_attn(heads, row0, masked):
        tmt = {}
        st = {"n": 0}

        def need(h):
            if h in tmt or h not in heads:
                return
            k = st["n"] % 2
            st["n"] += 1
            tmt[h] = (k, attn_load_bias(h, k, row0 + h, tm_free[k]))

        for h in heads[:2]:
            need(h)

        def qk(h, i):
            p0 = 64 * (h % 2)
            c = h // 2
            W = 128 * (i + 1)
            tok = [t_qk[(c // 4, 0, c % 4)], t_qk[(c // 4, 1, c % 4)]]
            return [(qT[p0:p0 + 64, c, i * 128:i * 128 + 128], kT[p0:p0 + 64, c, :W], 0, W, tok)]

        def bias(h, i):
            k, tok = tmt[h]
            bap = tm[k][:, 384 - 128 * i:512]
            if masked and i > 0:
                z = i % 2
                W = 128 * (i + 1)
                a = tt(P, bz[z][:, :W], bap, sco[i][:], ALU.add, tok, t_sco[i], bz_free[z])
                st["bz"] = (z, a)
                return bz[z][:, :W], [a]
            st["bz"] = None
            return bap, [tok]

        def fill(h, i, m):
            if st["bz"] is not None:
                bz_free[st["bz"][0]] = [m]
            if i == 3:
                k, _ = tmt[h]
                tm_free[k] = [m, st["bz"][1]] if st["bz"] else [m]
                later = [x for x in heads if x not in tmt]
                if later:
                    need(later[0])

        def vpair(h, b):
            c = h // 2
            return vR[:, b, c * 128:c * 128 + 128], [t_qk[(c // 4, 2, c % 4)]]

        def finish(h, ob, tok):
            p0, c = 64 * (h % 2), h // 2
            x = turned(bank[ob][p0:p0 + 64, :])
            H, L = in_blocks(hH[p0:p0 + 64, c, :]), in_blocks(hL[p0:p0 + 64, c, :])
            a = copy(A, H, x, tok, h_done[0])
            free_ = []

            def low():
                d = tt(V, L, x, H.bitcast(F), ALU.subtract, a, h_done[0])
                free_.append(d)
                mt[c] += [a, d]

            return free_, low

        return attention([(h, i) for h in heads for i in range(4)], False, 0, qk, bias,
                         lambda h, i: list(range(i + 1)), vpair, lambda h: BIG, finish, fill)

    bz_free = sq_free
    mt = [[] for _ in range(8)]
    t_mix = run_attn(list(range(8)), 0, False)
    t_mix = run_attn(list(range(8, 16)), 0, True)

    def mix_out(wo):
        for m in range(8):
            b = 4 + m % 3
            tk = gemm_cols(wo, m, [(hk(hH), hk(hL), bank[b], mt)], free[b])
            add_x(m, b, tk)
        h_done[0] = [tk]
        return tk

    tk = mix_out("wo0")
    start = [tk, t_mix]
    if stop > 1:
        fin = ffn(0, "up0", "dn0", att_gain("ffn0"), TAPS1, "cw0", "cb0", True, start)
    xdbg("x1")

    if stop > 2:
        hw = norm_split(lambda k: XT[:, k, :], S, lambda k: xready[k], att_gain("attn1"), hk(hH), hk(hL), h_done[0])
        for c in range(24):
            b = c % 4
            kind, cc = c // 8, c % 8
            if kind < 2:
                tk = gemm_cols("wq1", c, [(hk(hH), hk(hL), bank[b], hw)], free[b])
                dst = (qT, kT)[kind][:, cc, :]
                a = copy(A, turned(dst) if kind == 0 else in_blocks(dst), in_blocks(bank[b]), tk, fin,
                         scale=(-0.125, 1.0)[kind])
                free[b] = [a]
                t_qk[(cc // 4, kind, cc % 4)] = a
            else:
                v_unit("wq1", c, b, vR[:, :, cc * 128:cc * 128 + 128], (cc // 4, kind, cc % 4), fin)
        flush_later()
        h_done[0] = [pe_done()]
        for f_ in (tm_free, Sp_free, Pr_free, PT_free):
            f_[:] = [y + flat([fin]) for y in f_]
        mt = [[] for _ in range(8)]
        t_mix = run_attn(list(range(16)), 16, False)
        tk = mix_out("wo1")
        fin = ffn(1, "up1", "dn1", att_gain("ffn1"), TAPS1, "cw1", "cb1", True, [tk, t_mix])
        xdbg("x2")

    if stop > 3:
        r = norm_scale(S)
        for k in range(KD):
            a = stt(XT[:, k, :], XT[:, k, :], M("final", k, k + 1), rs[:], ALU.mult, ALU.mult, r, xready[k])
            xready[k] = [a]
            add_square(XT[:, k, :], k, a)
        rs_free[0] = [a]
        tmod = mod_state["tok"]
        gm = sc1[:, 8:16]
        gc = sc1[:, 16:24]
        gf = sc1[:, 24:32]
        g1 = stt(gm, modT[:, 8:16, 0], 1.0, M("mix2"), ALU.add, ALU.mult, tmod, t_sm)
        g2 = stt(gc, modT[:, 8:16, 1], 1.0, M("mix2"), ALU.add, ALU.mult, tmod, t_sm)
        g3 = stt(gf, modT[:, 32:40, 0], 1.0, M("ffn2"), ALU.add, ALU.mult, tmod, t_sm)
        qn8 = ts(V, sc1[:, 32:33], M("qn"), -0.125, None, ALU.mult, None, t_sm)
        nsk = ts(V, sc1[:, 40:48], M("sink"), -1.0, None, ALU.mult, None, t_sm)
        smalls2 = [g1, g2, g3, qn8, nsk]
        f0 = fence()
        join(f0, V, A, P, PE)

        top[0] = mark1
        hcH = sb("hcH", [128, KD, CTX], R)
        hcL = sb("hcL", [128, KD, CTX], R)
        mixed2 = sb("mixed2", [128, 8, S])
        yc_at = top[0]
        yc = sb("yc", [128, 4, S])
        mark3 = top[0]
        Sp = [sb(f"Sq{i}", [128, 641]) for i in range(2)]
        Pr = [sb(f"Pq{i}", [128, 768]) for i in range(3)]
        PT = [sb("PU", [128, 6, S])]
        aqT = sb("aqT", [128, 4, S])
        bqT = sb("bqT", [128, 4, S])
        akT, bkT = sb("akT", [128, 768], at=yc_at), sb("bkT", [128, 768])
        avR, bvR = [[sb(f"{x}{i}", [128, 3, 128], at=tails[2 * (x == "bvR") + i]) for i in range(2)]
                    for x in ("avR", "bvR")]
        ropes = sb("ropes", [128, 2, S], at=yc_at + 3072)
        band = sb("band", [128, 1152])
        d_b2 = [slot(f"d_b2{i}") for i in range(5)]
        ctxT = mixed2[:, :, :].rearrange("p a b -> p (a b)")[:, 0:2048].rearrange("p (k n) -> p k n", k=8)
        qtmp = [mixed2[:, 4, :], mixed2[:, 5, :]]
        qt_free = [[], []]
        t_ctx = SP.dma(lambda e: e.dma_start(ctxT, t["ctxT"]), d_b2[0], f0)
        t_rope = SP.dma(lambda e: e.dma_start(ropes[:], t["ropes"]), d_b2[1], f0)
        t_band = SP.dma(lambda e: e.dma_start(band[:], t["band"]), d_b2[2], f0)
        for z in (Sp_free, Pr_free, PT_free):
            z[:] = [[] for _ in z]

        hw = norm_split(lambda k: XT[:, k, :], S, lambda k: xready[k], lambda k: gm[:, k:k + 1], hk(hH), hk(hL),
                        h_done[0], shift=lambda k: modT[:, k, 0:1], gtok=smalls2)
        for k in range(KD):
            add_square(ctxT[:, k, :], k, t_ctx)
        hc = norm_split(lambda k: ctxT[:, k, :], CTX, lambda k: [t_ctx], lambda k: gc[:, k:k + 1], hk(hcH),
                        hk(hcL), None, shift=lambda k: modT[:, k, 1:2], gtok=smalls2)
        hboth = [hw, hc]

        hcl = [hc[k] for k in range(KD)]

        def both(b0, b1):
            return [(hk(hH), hk(hL), bank[b0], hw), (hk(hcH), hk(hcL), bank[b1][:, :CTX], hcl)]

        def b128(b, c):
            return bank[b][:, c * 128:c * 128 + 128]

        def b3(x, n):
            return x.rearrange("p (i d) -> p i d", i=n)

        def head_norm(x, n, gain, w, b=7):
            a = sumsq(x, n, C("blk"), b, w)
            r, a1 = rsqrt_of(rs[:, :n], bank[b][:, :n], 64, a, rs_free[0])
            free[b] = [a1]
            a = stt(x, x, gain, rs[:, :n], ALU.mult, ALU.mult, r, w)
            rs_free[0] = [a]
            return a

        def turn6(dst, src, b0, b1, *w):
            for c in range(6):
                o = b128((b0, b1)[c // 3], c % 3)
                x = PE.put(lambda e, o=o, i_=src[:, c * 128:c * 128 + 128]: e.transpose(o, i_, ident), list(w), t_cn,
                           free[b0], free[b1], inc=int(c == 5))
            a = copy(V, dst[0], b3(bank[b0][:, 0:384], 3), x)
            c = copy(V, dst[1], b3(bank[b1][:, 0:384], 3), x)
            free[b0], free[b1] = [a], [c]
            return [a, c]

        rope_n = [0]

        def rope(dst, x, w):
            b = 4 + rope_n[0] % 2
            j = rope_n[0] % 2
            rope_n[0] += 1
            a = mm(bank[b], C("rot"), x, True, True, w, t_cn, free[b], inc=1)
            u = tt(V, hf[j][:], bank[b], ropes[:, 1, :], ALU.mult, a, t_rope, hf_free[j])
            free[b] = [u]
            c = tt(P, dst, x, ropes[:, 0, :], ALU.mult, w, t_rope)
            d = tt(P, dst, dst, hf[j][:], ALU.add, c, u)
            hf_free[j] = [d]
            return a, d

        t_k2, t_v2, t_q2 = {}, {}, {}
        for g, (kT2, vR2, uk, uv) in enumerate(((akT, avR, 4, 5), (bkT, bvR, 10, 11))):
            tk = gemm_cols("win", uk, both(0, 1), free[0], free[1])
            a = copy(A, qtmp[g], bank[0], tk, qt_free[g])
            c = copy(A, kT2[:, S:], bank[1][:, :CTX], tk)
            free[0], free[1] = [a], [c]
            if g == 1:
                a = head_norm(qtmp[g], S, M("kn"), [a])
                c = head_norm(kT2[:, S:], CTX, M("kn"), [c])
            x1, x2 = rope(kT2[:, 0:S], qtmp[g], [a])
            qt_free[g] = [x1, x2]
            t_k2[g] = [x2, c]
            tk = gemm_cols("win", uv, both(2, 3), free[2], free[3])
            a = copy(A, Pr[g][:, 0:S], bank[2], tk)
            c = copy(A, Pr[g][:, S:768], bank[3][:, :CTX], tk)
            free[2], free[3] = [a], [c]
            t_v2[g] = turn6([y[:, :, :] for y in vR2], Pr[g], 4, 5, a, c)
        for g in range(2):
            for c in range(4):
                b, j = c % 4, c % 2
                tk = gemm_cols("win", (0, 6)[g] + c, [(hk(hH), hk(hL), bank[b], hw)], free[b])
                a = copy(A, qtmp[j], bank[b], tk, qt_free[j], scale=(-0.125, 1.0)[g])
                free[b] = [a]
                if g == 1:
                    a = head_norm(qtmp[j], S, sc1[:, 32:33], [a, qn8])
                x1, x2 = rope((aqT, bqT)[g][:, c, :], qtmp[j], [a])
                qt_free[j] = [x1, x2]
                t_q2[(g, c)] = x2
        mixed_ready = [qt_free[0], qt_free[1], hc]
        join(mixed_ready, V, A)

        def local(i):
            return max(i - 1, 0), min(i + 1, 3)

        def qk2(h, i):
            g, h = h // 8, h % 8
            p0 = 64 * (h // 4)
            q = (aqT, bqT)[g][p0:p0 + 64, h % 4, i * 128:i * 128 + 128]
            k = (akT, bkT)[g][p0:p0 + 64, :]
            tok = [t_q2[(g, h % 4)], t_k2[g]]
            if g == 1:
                return [(q, k[:, 0:512], 0, 512, tok), (q, k[:, 512:768], 512, 256, tok)]
            lo, hi = local(i)
            out_ = [(q, k[:, 512:768], 0, 256, tok), (q, k[:, lo * 128:lo * 128 + 256], 256, 256, tok)]
            if hi - lo == 2:
                out_.append((q, k[:, hi * 128:hi * 128 + 128], 512, 128, tok))
            return out_

        def bias2(h, i):
            if h >= 8:
                return None
            lo, hi = local(i)
            n_ = 256 + 128 * (hi - lo + 1)
            return (band[:, 640:640 + n_] if i == 0 else band[:, 0:n_]), [t_band]

        def slots2(h, i):
            lo, hi = local(i)
            return list(range(6)) if h >= 8 else [0, 1] + [2 + b for b in range(lo, hi + 1)]

        def vpair2(h, b):
            g = h // 8
            blk_ = b if g else (4 + b if b < 2 else b - 2)
            return (avR, bvR)[g][blk_ // 3][:, blk_ % 3, :], [t_v2[g]]

        t_mx = {}

        def finish2(h, ob, tok):
            p0 = 64 * (h % 8 // 4)
            a = copy((V, A)[h % 2], mixed2[p0:p0 + 64, 4 * (h // 8) + h % 4, :], bank[ob][p0:p0 + 64, :], tok)
            return [a], lambda: None

        attention([(h, i) for h in range(8) for i in range(4)], True, 1, qk2, bias2, slots2, vpair2,
                  lambda h: sc1[:, 40 + h:41 + h], finish2)
        t_mx = attention([(h, i) for h in range(8, 16) for i in range(4)], True, 0, qk2, bias2, slots2, vpair2,
                         lambda h: BIG, finish2)
        tk = debug("yab", mixed2[:], t_mx)

        f1 = fence()
        join(f1, V, A, P, PE)
        top[0] = mark3
        decR = sb("decR", [128, 2, 1024], R)
        uR = sb("uR", [128, 2, 128], R, at=tails[0])
        lmask = [sb(f"lmask{i}", [128, 8 - i, 128], U8, at=tails[1 + i]) for i in range(2)]
        zc = [sb(f"zc{i}", [128, 768]) for i in range(2)]
        vc = sb("vc", [128, 768])
        t6, lfc = sb("t6", [128, 768]), sb("lfc", [128, 768])
        lfH, lfL = sb("lfH", [128, 6, 128], R), sb("lfL", [128, 6, 128], R)
        kcc = [sb(f"kcc{i}", [128, 768]) for i in range(2)]
        kd = lfc[:, :].rearrange("p (c n) -> p c n", n=128)
        vr = sb("vr", [128, 6, 128])
        qts = [sb(f"qt{i}", [128, S]) for i in range(2)]
        E4 = sb("E4", [128, 4, 4, 128])
        Z = [in_blocks(ssum[:, :]), in_blocks(hf[1][:, :])]
        scT = in_blocks(hf[0][:, :])
        qa = [in_blocks(sq[i][:, :]) for i in range(2)]
        st8 = [sb(f"st{i}", [128, 3, 128], at=tails[3 + i]) for i in range(3)]

        def state(d, c):
            n_ = 4 * d + c
            return st8[n_ // 3][:, n_ % 3, :]

        def mask(n_):
            return lmask[n_ // 8][:, n_ % 8:n_ % 8 + 1, :].to_broadcast([128, 4, 128])

        f6 = sb("f6", [128, 2, 6])
        f6r = sb("f6r", [128, 6])
        e4f = E4[:, :, :, :].rearrange("p a b c -> p (a b c)")
        a = SP.dma(lambda e: e.dma_start(e4f, t["decay"].rearrange("p a b -> p (a b)")), d_b2[3], f1)
        t_dec = V.put(lambda e: e.tensor_copy(decR[:, :, :].rearrange("p a b -> p (a b)"), e4f), a)
        lmf = e4f[:, 0:15 * 128].rearrange("p (m n) -> p m n", m=15)
        a = SP.dma(lambda e: e.dma_start(lmf, t["lmask"]), d_b2[4], t_dec)
        t_lm = [V.put(lambda e: e.tensor_copy(lmask[0][:], lmf[:, 0:8, :]), a),
                V.put(lambda e: e.tensor_copy(lmask[1][:], lmf[:, 8:15, :]))]
        t_u0 = copy(V, uR[:, 0, :], C("uf"), t_cn)
        t_u1 = copy(V, uR[:, 1, :], C("ub"), t_cn)
        t_u = [t_u0, t_u1]
        z_fr, vc_fr, q_fr = [[], []], [[]], [[], []]
        z_tk, vc_tk, q_tk, s_tk = {}, {}, {}, {}

        def projections(h):
            def two(unit, dst, fr):
                tk = gemm_cols("win", unit, both(0, 1), free[0], free[1])
                a = copy(A, dst[:, 0:S], bank[0], tk, fr)
                c = copy(A, dst[:, S:768], bank[1][:, :CTX], tk)
                free[0], free[1] = [a], [c]
                return [a, c]

            def one(unit, b, dst, fr):
                tk = gemm_cols("win", unit, [(hk(hH), hk(hL), bank[b], hw)], free[b])
                a = act(dst, bank[b], ACT.Silu, tk, fr)
                free[b] = [a]
                return a

            z_tk[(h, 0)] = two(16 + h, zc[0], z_fr[0])
            yield
            vc_tk[h] = two(24 + h, vc, vc_fr[0])
            yield
            q_tk[h] = one(12 + h, 0, qts[h % 2][:], q_fr[h % 2])
            yield
            z_tk[(h, 1)] = two(20 + h, zc[1], z_fr[1])
            yield
            s_tk[h] = one(28 + h, 1, yc[:, h, :], None)
            yield

        for _ in projections(0):
            pass
        lf_fr, kd_fr, kc_fr, vr_fr, qa_fr, st_fr, sc_fr2 = [], [], [[], []], [], [[], []], [[], []], []
        t6_fr, e_free, z_f = [], [t_lm], [[], []]
        sc_t = None
        for h in range(4):
            gen = projections(h + 1) if h < 3 else iter(())
            qt = in_blocks(qts[h % 2][:, :])
            v_t = None
            qa_t, st_t, kc_t = {}, {}, {}
            for d in range(2):
                zt = z_tk[(h, d)]
                x = act(t6[:], zc[d][:], ACT.Abs, zt, t6_fr)
                x = act(t6[:], t6[:], ACT.Exp, x, scale=-1.0)
                x = act(t6[:], t6[:], ACT.Ln, x, bias=1.0)
                lf_t = stt(lfc[:], zc[d][:], 0.0, t6[:], ALU.min, ALU.subtract, x, zt, lf_fr, kd_fr)
                x = tt(V, t6[:], lfc[:], zc[d][:], ALU.subtract, lf_t)
                z_fr[d] = [x]
                kc_t[d] = act(kcc[d][:], t6[:], ACT.Exp, x, kc_fr[d])
                x = V.put(lambda e: e.tensor_reduce(f6r[:], lfc[:, :].rearrange("p (c n) -> p c n", n=128), AX.X,
                                                    ALU.add), lf_t)
                f6_t = act(f6[:, d, :], f6r[:], ACT.Exp, x, st_fr[d])
                if d == 0:
                    v_t = turn6([vr[:, 0:3, :], vr[:, 3:6, :]], vc, 6, 7, vc_tk[h], vr_fr)
                    vc_fr[0] = v_t
                for c in range(6):
                    o = b128(2, c) if c < 4 else b128(3, c - 4)
                    x = PE.put(lambda e, o=o, i_=lfc[:, c * 128:c * 128 + 128]: e.transpose(o, i_, ident), lf_t,
                               free[2], free[3], inc=int(c == 5))
                lf_fr = [x]
                a1 = copy(A, lfH[:, 0:4, :], b3(bank[2], 4), x)
                a2 = copy(A, lfH[:, 4:6, :], b3(bank[3][:, :CTX], 2), x)
                b1 = tt(V, lfL[:, 0:4, :], b3(bank[2], 4), lfH[:, 0:4, :].bitcast(F), ALU.subtract, a1)
                b2 = tt(V, lfL[:, 4:6, :], b3(bank[3][:, :CTX], 2), lfH[:, 4:6, :].bitcast(F), ALU.subtract, a2)
                free[2], free[3] = [b1], [b2]
                lr_t = [a1, a2, b1, b2]
                for c in range(6):
                    o = b128(6, c) if c < 4 else b128(7, c - 4)
                    xk = PE.put(lambda e, o=o, i_=kcc[d][:, c * 128:c * 128 + 128]: e.transpose(o, i_, ident), kc_t[d],
                                free[6], free[7], inc=int(c == 5))
                next(gen, None)
                mm(bank[4], uR[:, d, :], lfH[:, 0:4, :], True, False, lr_t, free[4], t_u)
                mm(bank[4], uR[:, d, :], lfL[:, 0:4, :], False, True)
                mm(bank[5][:, :CTX], uR[:, d, :], lfH[:, 4:6, :], True, False, free[5])
                x = mm(bank[5][:, :CTX], uR[:, d, :], lfL[:, 4:6, :], False, True, inc=1)
                e1 = act(t6[:, 0:S], bank[4], ACT.Exp, x, kc_t[d])
                e2 = act(t6[:, S:768], bank[5][:, :CTX], ACT.Exp, x)
                free[4], free[5] = [e1], [e2]
                k1 = tt(V, kd[:, 0:4, :], b3(bank[6], 4), in_blocks(t6[:, 0:S]), ALU.mult, e1, xk, kd_fr)
                k2 = tt(V, kd[:, 4:6, :], b3(bank[7][:, :CTX], 2), in_blocks(t6[:, S:768]), ALU.mult, e2, xk, kd_fr)
                free[6], free[7] = [k1], [k2]
                t6_fr = [k1, k2]
                def decays(grp):
                    et_ = []
                    for c in range(4):
                        b = 4 + c
                        mm(bank[b], lfH[:, c, :], decR[:, d, grp * 512:grp * 512 + 512], True, False, t_dec, lr_t,
                           free[b])
                        x = mm(bank[b], lfL[:, c, :], decR[:, d, grp * 512:grp * 512 + 512], False, True, inc=1)
                        x = act(E4[:, c, :, :], b3(bank[b], 4), ACT.Exp, x, e_free)
                        free[b] = [x]
                        et_.append(x)
                    return et_

                et = decays(0)
                for c in range(6):
                    o = b128(2, c) if c < 4 else b128(3, c - 4)
                    x = mm(o, kd[:, c, :], vr[:, c, :], True, True, k1, k2, v_t, free[2], free[3], inc=int(c == 5))
                kd_fr = [x]
                first, second = ((4, 5), (5, 4))[d]
                s0 = (0, 3)[d]
                prev = copy(V, state(d, s0), b128(3, first - 4), x, st_fr[d])
                prev = stt(state(d, s0), state(d, s0), f6[:, d, second:second + 1], b128(3, second - 4),
                           ALU.mult, ALU.add, prev, f6_t)
                free[3] = [prev]
                for c in ((0, 1, 2), (3, 2, 1))[d]:
                    to = c + (1, -1)[d]
                    prev = stt(state(d, to), state(d, c), f6[:, d, c:c + 1], b128(2, c), ALU.mult, ALU.add,
                               prev)
                free[2] = [prev]
                st_t[d] = prev
                if d == 1:
                    zi_tok = tt(P, Z[0], in_blocks(kcc[0][:, 0:S]), in_blocks(kcc[1][:, 0:S]), ALU.add, kc_t[0],
                                kc_t[1], z_f[0])
                    for c in range(4):
                        y = mm(b128(2, c), Z[0][:, c, :], qt[:, c, :], True, True, zi_tok, q_tk[h], free[2],
                               inc=int(c == 3))
                    z_f[0] = [y]
                    mk = mask(14)
                    sc_t = V.put(lambda e, mk=mk: e.copy_predicated(scT, mk, b3(bank[2], 4)), y, sc_t, t_lm)
                    free[2] = [sc_t]
                zi = 0
                kv_ = in_blocks(kcc[d][:, 0:S])
                for grp in range(2):
                    if grp == 1:
                        et = decays(1)
                    e_free = []
                    for m_ in range(4):
                        mat = grp * 4 + m_
                        if mat == 0:
                            qa_t[d] = tt(V, qa[d], qt, E4[:, :, 0, :], ALU.mult, et, q_tk[h], qa_fr[d])
                            e_free.append(qa_t[d])
                            continue
                        lv = mat - 1
                        b_ = LEVELS[lv]
                        zi += 1
                        zz = Z[zi % 2]

                        def view(y_):
                            return y_.rearrange("p c (n u b) -> p c n u b", u=2, b=b_)

                        uq = (1, 0)[d]
                        Ev, Zv, Qv, Kv = view(E4[:, :, m_, :]), view(zz), view(qt), view(kv_)
                        w1 = pair_mult(V, Zv, Ev, Qv, uq, et, z_f[zi % 2], q_tk[h])
                        w2 = pair_mult(P, Zv, Ev, Kv, 1 - uq, et, z_f[zi % 2], kc_t[d])
                        e_free += [w1, w2]
                        pb = 2 + zi % 2
                        for c in range(4):
                            x = mm(b128(pb, c), zz[:, c, :], zz[:, c, :], True, True, w1, w2, free[pb],
                                   inc=int(c == 3))
                        z_f[zi % 2] = [x]
                        mk = mask(2 * lv + d)
                        sc_t = V.put(lambda e, mk=mk, y_=b3(bank[pb], 4): e.copy_predicated(scT, mk, y_), x, sc_t,
                                     t_lm, sc_fr2)
                        free[pb] = [sc_t]
                        if m_ == 1 and (grp == 0 or d == 0):
                            next(gen, None)
                kc_fr[d] = [w2, zi_tok] if d == 1 else [w2]
            kc_fr[0] = [w2, zi_tok]
            for _ in gen:
                pass
            for c in range(4):
                mm(b128(2, c), vr[:, c, :], scT[:, c, :], True, False, v_t, sc_t, free[2])
                mm(b128(2, c), state(0, c), qa[0][:, c, :], False, False, st_t[0], qa_t[0])
                x = mm(b128(2, c), state(1, c), qa[1][:, c, :], False, True, st_t[1], qa_t[1], inc=1)
            vr_fr, sc_fr2 = [x], [x]
            qa_fr, st_fr = [[x], [x]], [[x], [x]]
            q_fr[h % 2] = [x]
            sq_free[0] = [x]
            a = sumsq(bank[2], S, C("ones"), 3, x)
            qa_fr[0] = [a]
            r, a1 = rsqrt_of(rs[:], bank[3], 128, a, rs_free[0])
            free[3] = [a1]
            y = stt(rs[:], bank[2], M("gn"), rs[:], ALU.mult, ALU.mult, r, x)
            free[2] = [y]
            y = tt(P, yc[:, h, :], yc[:, h, :], rs[:], ALU.mult, y, s_tk[h])
            rs_free[0] = [y]
        tk = debug("yc", yc[:], y)

        f2 = fence()
        join(f2, V, A, P, PE)
        top[0] = mark3
        yH, yL = sb("yH", [128, 12, S], R), sb("yL", [128, 12, S], R)
        acc = [rs, sb("acc1", [128, S])]
        gt, tmp = sq, hf
        top[0] = mark1
        mH, mL = sb("mH", [128, KD, S], R), sb("mL", [128, KD, S], R)
        ty = []
        for c in range(12):
            src = mixed2[:, c, :] if c < 8 else yc[:, c - 8, :]
            a = copy(A, yH[:, c, :], src)
            b = tt((V, P)[c % 2], yL[:, c, :], src, yH[:, c, :].bitcast(F), ALU.subtract, a)
            ty.append([a, b])
        acc_f, gt_f, tmp_f = [rs_free[0], []], sq_free, hf_free
        tm_ = []
        n = 0
        for m in range(8):
            j = m % 2
            for br in range(3):
                z = n % 2
                n += 1
                tk = gemm_cols("win", 32 + 8 * br + m, [(hk(hH), hk(hL), bank[z], hw)], free[z])
                g_ = act(gt[z][:], bank[z], ACT.Sigmoid, tk, gt_f[z])
                free[z] = [g_]
                tk = gemm_cols("wbr", 8 * br + m, [(lambda k, br=br: yH[:, 4 * br + k, :],
                                                    lambda k, br=br: yL[:, 4 * br + k, :], bank[2 + z],
                                                    ty[4 * br:4 * br + 4])], free[2 + z])
                if br == 0:
                    a = tt(V, acc[j][:], bank[2 + z], gt[z][:], ALU.mult, tk, g_, acc_f[j])
                    free[2 + z], gt_f[z] = [a], [a]
                    prev = a
                else:
                    a = tt(V, tmp[z][:], bank[2 + z], gt[z][:], ALU.mult, tk, g_, tmp_f[z])
                    free[2 + z], gt_f[z] = [a], [a]
                    prev = tt(P, acc[j][:], acc[j][:], tmp[z][:], ALU.add, a, prev)
                    tmp_f[z] = [prev]
            a = copy(A, mH[:, m, :], acc[j][:], prev)
            b = tt(P, mL[:, m, :], acc[j][:], mH[:, m, :].bitcast(F), ALU.subtract, a, prev)
            acc_f[j] = [a, b]
            tm_.append([a, b])
        rs_free[0] = acc_f[0]
        h_done[0] = [tk]
        for m in range(8):
            b = 4 + m % 3
            tk = gemm_cols("wout", m, [(hk(mH), hk(mL), bank[b], tm_)], free[b])
            add_x(m, b, tk, modT[:, 16 + m, 0:1], tmod)
        xdbg("x3")
        f3 = fence()
        ffn(2, "up2", "dn2", lambda k: gf[:, k:k + 1], TAPS2, "dw2", "db2", False, f3,
            shift=lambda k: modT[:, 24 + k, 0:1], gtok=smalls2, scale=lambda m: modT[:, 40 + m, 0:1])

    if stop > 3:
        r = norm_scale(S)
        g = "final2"
    else:
        r = norm_scale(S)
        g = "final"
    d_out = slot("d_out")
    for k in range(KD):
        a = stt(XT[:, k, :], XT[:, k, :], M(g, k, k + 1), rs[:], ALU.mult, ALU.mult, r, xready[k])
        tk = SP.dma(lambda e, k=k: e.dma_start(out[:, k, :], XT[:, k, :]), d_out, a)
    SP.items.append(([tk], lambda e: None, None, 0))
    SP.items.append(([t_toep], lambda e: None, None, 0))

    print("sbuf", hw_ffn, top, nc.sbuf_usable_end) if dbg else None
    blk = ctx.enter_context(nc.Block())

    @blk.sync
    def _(e):
        SP.run(e)

    @blk.tensor
    def _(e):
        PE.run(e)

    @blk.vector
    def _(e):
        V.run(e)

    @blk.scalar
    def _(e):
        A.run(e)

    @blk.gpsimd
    def _(e):
        P.run(e)


def constants():
    c = np.zeros((128, N_CN), np.float32)

    def put(name, v):
        c[:, CN[name][0]:CN[name][1]] = v

    i = np.arange(128)
    put("ident", np.eye(128))
    put("ones", 1.0)
    put("blk", (i[:, None] // 64 == i[None, :] // 64))
    put("anti", np.eye(128)[::-1])
    put("causal", np.where(i[None, :] <= 127 - i[:, None], 0.0, -BIG))
    rot = np.zeros((128, 128), np.float32)
    for a in range(64):
        rot[2 * a + 1, 2 * a] = -1.0
        rot[2 * a, 2 * a + 1] = 1.0
    put("rot", rot)
    s, tt_ = i[:, None], i[None, :]
    put("uf", s > tt_)
    put("ub", s < tt_)
    mf, mb = [s <= tt_], [s >= tt_]
    masks = []
    for b in LEVELS:
        mid = tt_ // (2 * b) * (2 * b) + b
        up = tt_ >= mid
        mf.append(np.where(up, (s >= mid) & (s <= tt_), (s > tt_) & (s < mid)))
        mb.append(np.where(up, (s >= mid) & (s < tt_), (s >= tt_) & (s < mid)))
        same = s // (2 * b) == tt_ // (2 * b)
        masks.append(same & (s < mid) & (tt_ >= mid))
        masks.append(same & (s >= mid) & (tt_ < mid))
    masks.append(np.eye(128))
    msk = np.stack(masks, 1).astype(np.float32)
    w = np.arange(TOEP)
    d = 511 - w
    n = np.maximum(d, 0)
    nf = np.maximum(n, 16).astype(np.float32)
    large = 16 + (np.log(nf / np.float32(16)) / np.float32(math.log(128 / 16)) * np.float32(16)).astype(np.int32)
    bucket = np.where(n < 16, n, np.minimum(large, 31))
    oh = np.zeros((32, TOEP), np.float32)
    oh[bucket, w] = -1.0
    mr = np.zeros((32, TOEP), np.float32)
    mr[:, d < 0] = BIG
    cnt = ((d >= 0) & (d <= 128)).astype(int) + ((d >= 0) & (d % 4 == 0)) + ((d >= 0) & (d % 16 == 0))
    mr[16:, :] = np.where(cnt > 0, -np.log(np.maximum(cnt, 1)), BIG)
    tpos = np.arange(S)
    inv = (np.float32(10000.0) ** (-np.arange(0, 32, 2, dtype=np.float32) / np.float32(32))).astype(np.float32)
    ang = np.concatenate([(tpos // 64).astype(np.float32)[:, None] * inv, (tpos % 64).astype(np.float32)[:, None] * inv], 1)
    cs = np.stack([np.cos(ang), np.sin(ang)], 0).astype(np.float32)
    cs = np.repeat(cs, 2, axis=2).transpose(2, 0, 1)
    cs = np.concatenate([cs, cs], 0)
    j = np.arange(384)
    near = np.where(np.abs(j[None, :] - 128 - i[:, None]) <= 128, 0.0, BIG)
    band = np.zeros((128, 1152), np.float32)
    band[:, 256:640] = near
    band[:, 896:] = near[:, 128:]
    return {"consts": c, "decay": np.stack([np.concatenate(mf, 1), np.concatenate(mb, 1)], 1).astype(np.float32), "lmask": msk, "onehot": oh, "maskrow": mr, "ropes": np.ascontiguousarray(cs), "band": band}


def pack(w, kt=None):
    K, N = w.shape
    return np.ascontiguousarray(w.reshape(K // 128, 128, N // 128, 128).transpose(2, 1, 0, 3)).reshape(
        N // 128, 128, K)


def cols(v):
    return v.reshape(-1, 128).T


def lay(i):
    o = constants()
    g = {k: np.asarray(v) for k, v in i.items()}
    sm = np.zeros((128, N_SM), np.float32)

    def put(name, v):
        sm[:, SM[name][0]:SM[name][1]] = v

    for l in range(2):
        put(f"attn{l}", cols(g["attn_norm"][l]))
        put(f"ffn{l}", cols(g["ffn_norm"][l]))
        put(f"cw{l}", cols(g["conv_w"][l]))
        put(f"cb{l}", cols(g["conv_b"][l]))
    put("final", cols(g["final_norm"]))
    put("mix2", cols(g["norm_mix_2"]))
    put("ffn2", cols(g["norm_ffn_2"]))
    put("final2", cols(g["norm_final_2"]))
    put("dw2", cols(g["w_dw_2"]))
    put("db2", cols(g["b_dw_2"]))
    put("bmod", cols(g["b_mod_2"]))
    put("idxk", np.tile(g["idx_k_norm"].reshape(64), 2)[:, None])
    put("qn", np.tile(g["qn_b_2"].reshape(64), 2)[:, None])
    put("kn", np.tile(g["kn_b_2"].reshape(64), 2)[:, None])
    put("gn", g["gn_c_2"].reshape(128, 1))
    put("sink", np.broadcast_to(g["sink_a_2"].reshape(1, 8), (128, 8)))
    put("c", cols(g["c_2"]))
    put("cctx", cols(g["c_ctx_2"]))
    o["smalls"] = sm
    o["xT"] = np.ascontiguousarray(g["x"][0].T.reshape(8, 128, S).transpose(1, 0, 2))
    o["ctxT"] = np.ascontiguousarray(g["ctx_2"][0].T.reshape(8, 128, CTX).transpose(1, 0, 2))
    o["rel"] = np.concatenate([g["rel_bias"], g["rel_bias"]], 1)
    we = g["w_in_even"][0]
    o["we"] = np.concatenate([pack(np.concatenate([we[:, 4096:4160], we[:, 4096:4160]], 1)), pack(we[:, 3072:4096]),
                              pack(we[:, :3072])], 0)
    o["wi"] = np.ascontiguousarray(we[:, 4160:4176].reshape(8, 128, 16).transpose(1, 0, 2)).reshape(1, 128, 128)
    o["wq1"] = pack(g["w_in_odd"][0])
    for l in range(2):
        o[f"wo{l}"] = pack(g["w_o"][l])
        o[f"up{l}"] = pack(g["w_up"][l])
        o[f"dn{l}"] = np.concatenate([pack(g["w_down"][l][:1408]), pack(g["w_down"][l][1408:])], 0)
    o["wmod"] = pack(g["w_mod_2"][0])
    wi = g["w_in_2"][0]
    perm = np.concatenate([np.arange(h * 64, h * 64 + 64) for c in range(4) for h in (c, c + 4)])
    aq, bq = wi[:, :512][:, perm], wi[:, 768:1280][:, perm]
    o["win"] = pack(np.concatenate([aq, wi[:, 512:768], bq, wi[:, 1280:]], 1))
    wb = g["w_branch_2"][0]
    o["wbr"] = np.concatenate([pack(wb[0][perm]), pack(wb[1][perm]), pack(wb[2])], 0)
    o["wout"] = pack(g["w_out_2"][0])
    o["up2"] = pack(g["w_up_2"][0])
    o["dn2"] = np.concatenate([pack(g["w_down_2"][0][:1408]), pack(g["w_down_2"][0][1408:])], 0)
    return o


def kernel(**inputs):
    import concourse.bacc as _bacc
    from concourse.bass_utils import run_bass_kernel_spmd as _run

    nc = _bacc.Bacc("TRN2", target_bir_lowering=False, num_devices=1)
    arrays = lay(inputs)
    t = {k: nc.dram_tensor(f"in_{k}", v.shape, mybir.dt.from_np(v.dtype), kind="ExternalInput").ap()
         for k, v in arrays.items()}
    t["toep"] = nc.dram_tensor("toep", (32, TOEP), F, kind="Internal").ap()
    out = nc.dram_tensor("out_y", (128, KD, S), F, kind="ExternalOutput").ap()
    build(nc, t, out)
    r = _run(nc, [{f"in_{k}": v for k, v in arrays.items()}], core_ids=[0])
    y = r.results[0]["out_y"]
    return np.ascontiguousarray(y.transpose(2, 1, 0)).reshape(1, S, D)
```

```python
import math
from contextlib import ExitStack

import numpy as np

import concourse.bass as bass
from concourse import mybir

F = mybir.dt.float32
R = mybir.dt.float32r
U8 = mybir.dt.uint8
ALU = mybir.AluOpType
ACT = mybir.ActivationFunctionType
AX = mybir.AxisListType

S = 512
D = 1024
KD = 8
DFF = 2816
HALF = 11
CTX = 256
EPS = 1e-6
BIG = 1e30
LOW = -3e38
KEEP = 128
TOEP = 640
LEVELS = (64, 32, 16, 8, 4, 2, 1)
N_SLOT = HALF * 128

SM = {}
_at = 0
for _name, _n in (("attn0", 8), ("attn1", 8), ("ffn0", 8), ("ffn1", 8), ("final", 8), ("mix2", 8), ("ffn2", 8),
                  ("final2", 8), ("cw0", 132), ("cw1", 132), ("cb0", 44), ("cb1", 44), ("dw2", 132), ("db2", 44),
                  ("bmod", 48), ("idxk", 1), ("qn", 1), ("kn", 1), ("gn", 1), ("sink", 8), ("c", 8), ("cctx", 8)):
    SM[_name] = (_at, _at + _n)
    _at += _n
N_SM = _at

CN = {}
_at = 0
for _name, _n in (("ident", 128), ("ones", 128), ("blk", 128), ("causal", 128), ("rot", 128), ("uf", 128), ("ub", 128)):
    CN[_name] = (_at, _at + _n)
    _at += _n
N_CN = _at


def weight_units():
    out = [("we", 0), ("wi", 0)] + [("we", 1 + n) for n in range(8 + 24)]

    def block(wo, up, down):
        for m in range(8):
            out.append((wo, m))
        for half in range(2):
            for j in range(HALF):
                n = half * HALF + j
                out.append((up, n))
                out.append((up, 22 + n))
            for m in range(8):
                out.append((down, half * 8 + m))

    block("wo0", "up0", "dn0")
    for n in range(24):
        out.append(("wq1", n))
    block("wo1", "up1", "dn1")
    for n in [0, 1, 2, 3] + [4, 5, 10, 11] + [6, 7, 8, 9]:
        out.append(("win", n))
    for h in range(4):
        for base in (16, 24, 12, 20, 28):
            out.append(("win", base + h))
    for m in range(8):
        for n in range(3):
            out.append(("win", 32 + 8 * n + m))
            out.append(("wbr", 8 * n + m))
    block("wout", "up2", "dn2")
    return out


KTS = {"we": 8, "wi": 8, "wq1": 8, "win": 8, "wbr": 4, "wout": 8}
for _l in range(3):
    KTS[f"up{_l}"] = 8
    KTS[f"dn{_l}"] = HALF
    KTS[f"wo{_l}"] = 8


class Queue:

    def __init__(self, sem):
        self.sem, self.n, self.items = sem, 0, []

    def put(self, fn, *waits, inc=1):
        self.items.append((flat(waits), fn, self.sem, inc))
        self.n += inc
        return (self.sem, self.n)

    def dma(self, fn, slot, *waits):
        slot[1] += 16
        self.items.append((flat(waits), fn, slot[0], 16))
        return (slot[0], slot[1])

    def run(self, eng):
        seen = {}
        for waits, fn, sem, inc in self.items:
            for s, v in waits:
                if seen.get(id(s), 0) < v:
                    eng.wait_ge(s, v)
                    seen[id(s)] = v
            ins = fn(eng)
            if inc:
                ins.then_inc(sem, inc)


def flat(x):
    out = []
    for y in x:
        if y is None:
            continue
        if isinstance(y, list):
            out += flat(y)
        else:
            out.append(y)
    return out


def build(nc, t, out):
    ctx = ExitStack()
    with ctx:
        build_in(nc, t, out, ctx)


def build_in(nc, t, out, ctx):
    def sem(name):
        return ctx.enter_context(nc.semaphore(name))

    PE, V, A, P, SP = (Queue(sem(f"s_{x}")) for x in ("pe", "dve", "act", "pool", "sp"))

    base0 = (nc.sbuf_base + 63) // 64 * 64
    top = [base0]

    def sb(name, shape, dt=F, at=None):
        n = int(np.prod(shape[1:])) * (1 if dt == U8 else 4)
        n = (n + 63) // 64 * 64
        if at is None:
            off = top[0]
            top[0] += n
        else:
            off = at
        assert off + n <= nc.sbuf_usable_end, (name, off + n)
        return nc.alloc_sbuf_tensor_at(name, list(shape), dt, offset=off)

    ps = [ctx.enter_context(nc.psum_tensor(f"ps{i}", [128, 1024], F)) for i in range(4)]
    bank = [ps[i // 2][:, (i % 2) * 512:(i % 2) * 512 + 512] for i in range(8)]
    free = [[] for _ in range(8)]

    def slot(name):
        return [sem(name), 0]

    XT = sb("XT", [128, KD, S])
    hH = sb("hH", [128, KD, S], R)
    hL = sb("hL", [128, KD, S], R)
    NR, NH = 3, 3
    ring_at = top[0]
    rawb = [sb(f"raw{i}", [128, N_SLOT]) for i in range(NR)]
    wHb = [sb(f"wH{i}", [128, N_SLOT], R) for i in range(NH)]
    wLb = [sb(f"wL{i}", [128, N_SLOT], R) for i in range(NH)]
    tails = [ring_at + i * N_SLOT * 4 + 4096 for i in range(NR + 2 * NH)]
    sm = sb("sm", [128, N_SM])
    cn = sb("cn", [128, N_CN])
    modT = sb("modT", [128, 48, 2])
    cs = sb("cs", [128, KD, 2])
    sc1 = sb("sc1", [128, 64])
    mark0 = top[0]

    def C(name, a=0, b=None):
        lo, hi = CN[name]
        return cn[:, lo + a:(hi if b is None else lo + b)]

    def M(name, a=0, b=None):
        lo, hi = SM[name]
        return sm[:, lo + a:(hi if b is None else lo + b)]

    ident = C("ident")
    d_cn, d_sm, d_x = slot("d_cn"), slot("d_sm"), [slot(f"d_x{i}") for i in range(4)]
    t_x = [SP.dma(lambda e, i=i: e.dma_start(XT[:, 2 * i:2 * i + 2, :], t["xT"][:, 2 * i:2 * i + 2, :]), d_x[i])
           for i in range(4)]
    t_sm = SP.dma(lambda e: e.dma_start(sm[:], t["smalls"]), d_sm)
    t_cn = SP.dma(lambda e: e.dma_start(cn[:], t["consts"]), d_cn)

    units = weight_units()
    d_raw = [slot(f"d_raw{i}") for i in range(NR)]
    U = {"load": 0, "split": 0, "take": 0, "hs": 0, "rel": 0}
    raw_tok, raw_free, h_tok, h_slot = {}, {}, {}, {}
    h_free = [[] for _ in range(NH)]

    def size(n):
        name = units[n][0]
        kt = KTS[name]
        return kt, (16 if name == "wi" else 128)

    def advance():
        while True:
            n = U["load"]
            if n < len(units) and (n < NR or (n - NR) in raw_free):
                kt, nc_ = size(n)
                name, i = units[n]
                dst = rawb[n % NR][:, :kt * nc_]
                src = t[name][i]
                raw_tok[n] = SP.dma(lambda e, dst=dst, src=src: e.dma_start(dst, src), d_raw[n % NR],
                                    raw_free.get(n - NR, t_x))
                U["load"] += 1
                continue
            n = U["split"]
            if n < U["load"] and n < U["take"] + 4:
                if U["hs"] < U["rel"] + NH:
                    k = U["hs"] % NH
                    kt, nc_ = size(n)
                    r, H, L = rawb[n % NR][:, :kt * nc_], wHb[k][:, :kt * nc_], wLb[k][:, :kt * nc_]
                    th = split_hi(H, r, raw_tok[n], h_free[k])
                    tl = (P if U.get("pool") and n % 2 else V).put(lambda e, L=L, r=r, H=H: e.tensor_tensor(L, r, H.bitcast(F), ALU.subtract), th)
                    h_tok[n], h_slot[n] = [th, tl], k
                    raw_free[n] = [tl]
                    U["hs"] += 1
                    U["split"] += 1
                    continue
            break

    def split_hi(H, r, *w):
        return A.put(lambda e: e.activation(H, r, ACT.Copy), *w)

    def take(name, i):
        n = U["take"]
        assert units[n] == (name, i), (units[n], name, i)
        U["take"] += 1
        advance()
        kt, nc_ = size(n)
        k = h_slot[n]
        return (n, wHb[k][:, :kt * nc_].rearrange("p (k c) -> p k c", k=kt),
                wLb[k][:, :kt * nc_].rearrange("p (k c) -> p k c", k=kt), h_tok[n])

    def release(n, tok):
        h_free[h_slot[n]] = [tok]
        U["rel"] += 1
        advance()

    def mm(o, l, r, start, stop, *w, inc=0):
        return PE.put(lambda e: e.matmul(o, l, r, start=start, stop=stop), *w, inc=inc)

    def gemm_steps(name, i, parts, group, result, *w):
        n, H, L, tok = take(name, i)
        kt = size(n)[0]
        last = None
        for k in range(kt):
            for xH, xL, o, xt in parts:
                mm(o, H[:, k, :], xH(k), k == 0, False, tok, xt[k], *w)
                mm(o, H[:, k, :], xL(k), False, False)
                last = mm(o, L[:, k, :], xH(k), False, k == kt - 1, inc=int(k == kt - 1))
            if k % group == group - 1:
                if k == kt - 1:
                    release(n, last)
                    result.append(last)
                yield

    def gemm_cols(name, i, parts, *w):
        result = []
        for _ in gemm_steps(name, i, parts, KTS[name], result, *w):
            pass
        return result[0]

    def copy(q, o, i, *w, scale=1.0):
        if q is A:
            return A.put(lambda e: e.activation(o, i, ACT.Copy, scale=scale), *w)
        if scale == 1.0:
            return q.put(lambda e: e.tensor_copy(o, i), *w)
        return q.put(lambda e: e.tensor_scalar(o, i, scale, None, ALU.mult), *w)

    def act(o, i, f, *w, **kw):
        return A.put(lambda e: e.activation(o, i, f, **kw), *w)

    def tt(q, o, a, b, op, *w):
        return q.put(lambda e: e.tensor_tensor(o, a, b, op), *w)

    def stt(o, a, s, b, op0, op1, *w):
        return V.put(lambda e: e.scalar_tensor_tensor(o, a, s, b, op0, op1), *w)

    def ts(q, o, a, s1, s2, op0, op1, *w):
        if s2 is None:
            return q.put(lambda e: e.tensor_scalar(o, a, s1, None, op0), *w)
        return q.put(lambda e: e.tensor_scalar(o, a, s1, s2, op0, op1), *w)

    def pair_mult(q, o, a, b, u, *w):
        return q.put(lambda e: e.tensor_tensor(o[:, :, :, u, :], a[:, :, :, u, :], b[:, :, :, u, :], ALU.mult), *w)

    sq = [sb(f"sq{i}", [128, S]) for i in range(2)]
    sq_free = [[], []]
    rs = sb("rs", [128, S])
    hf = [sb(f"hf{i}", [128, S]) for i in range(2)]
    hf_free = [[], []]
    rs_free = [[]]
    eps_t = sb("eps_t", [128, 1])
    mn = sb("mn", [128, 16, 4])
    den = sb("den", [128, 16, 4])
    t_eps = V.put(lambda e: e.memset(eps_t[:], EPS))
    ssum = sb("ssum", [128, S])
    mark1 = top[0]

    def rsqrt_of(o, ss, n, *w):
        a = act(o, ss, ACT.Ln, t_eps, *w, scale=1.0 / n, bias=eps_t[:, 0:1])
        return act(o, o, ACT.Exp, a, scale=-0.5), a

    def sumsq(x, n, ones, b, ready):
        a = act(sq[0][:, :n], x, ACT.Square, ready, sq_free[0])
        last = mm(bank[b][:, :n], ones, sq[0][:, :n], True, True, a, t_cn, free[b], inc=1)
        sq_free[0] = [last]
        return last

    ss = {"free": [], "tok": None}

    def add_square(x, k, ready, q=None):
        n = x.shape[1]
        if k == 0:
            ss["tok"] = act(ssum[:, :n], x, ACT.Square, ready, ss["free"])
            return
        j = k % 2
        a = act(sq[j][:, :n], x, ACT.Square, ready, sq_free[j])
        if k >= KD - 2:
            ss[j] = a
            return
        ss["tok"] = tt(q or P, ssum[:, :n], ssum[:, :n], sq[j][:, :n], ALU.add, a, ss["tok"])
        sq_free[j] = [ss["tok"]]

    def total_squares(n, b):
        mm(bank[b][:, :n], C("ones"), ssum[:, :n], True, False, ss["tok"], t_cn, free[b])
        mm(bank[b][:, :n], C("ones"), sq[0][:, :n], False, False, ss[0])
        last = mm(bank[b][:, :n], C("ones"), sq[1][:, :n], False, True, ss[1], inc=1)
        ss["free"], sq_free[0], sq_free[1] = [last], [last], [last]
        return last

    def norm_scale(n, b=7):
        last = total_squares(n, b)
        r, a = rsqrt_of(rs[:, :n], bank[b][:, :n], D, last, rs_free[0])
        free[b] = [a]
        return r

    def norm_split(src, n, ready, gain, dH, dL, d_free, shift=None, gtok=None, scale=None):
        sc, r = scale or (rs[:, :n], norm_scale(n))
        toks = []
        for k in range(KD):
            j = k % 2
            h = hf[j][:, :n]
            a = stt(h, src(k), gain(k), sc, ALU.mult, ALU.mult, r, ready(k), hf_free[j], gtok)
            if shift is None:
                c = copy(A, dH(k), h, a, d_free)
                d = tt((V, P)[k % 2], dL(k), h, dH(k).bitcast(F), ALU.subtract, c, a, d_free)
            elif k % 2:
                c = act(dH(k), h, ACT.Identity, a, d_free, bias=shift(k))
                c2 = act(h, h, ACT.Identity, c, bias=shift(k))
                d = tt(P, dL(k), h, dH(k).bitcast(F), ALU.subtract, c2, d_free)
            else:
                c = act(dH(k), h, ACT.Identity, a, d_free, bias=shift(k))
                d = stt(dL(k), h, shift(k), dH(k).bitcast(F), ALU.add, ALU.subtract, c, d_free)
            hf_free[j] = [c, d]
            toks.append([c, d])
            rs_free[0] = [a]
        return toks

    mrow = sb("mrow", [32, TOEP])
    rel = sb("rel", [32, 32])
    oh = sb("oh", [32, TOEP])
    d_rel = [slot(f"d_rel{i}") for i in range(4)]
    ta = SP.dma(lambda e: e.dma_start(rel[:], t["rel"]), d_rel[0])
    tb = SP.dma(lambda e: e.dma_start(oh[:], t["onehot"]), d_rel[1])
    tc = SP.dma(lambda e: e.dma_start(mrow[:], t["maskrow"]), d_rel[2])

    def tables():
        mm(bank[4][0:32, :], rel[:], oh[:, 0:512], True, True, ta, tb)
        a = mm(bank[5][0:32, 0:TOEP - 512], rel[:], oh[:, 512:TOEP], True, True, inc=1)
        a1 = tt(V, mrow[:, 0:512], bank[4][0:32, :], mrow[:, 0:512], ALU.add, a, tc)
        a2 = tt(V, mrow[:, 512:TOEP], bank[5][0:32, 0:TOEP - 512], mrow[:, 512:TOEP], ALU.add, a)
        free[4], free[5] = [a1], [a2]
        return SP.dma(lambda e: e.dma_start(t["toep"], mrow[:]), d_rel[3], a1, a2)

    def toep_src(h):
        return bass.AP(t["toep"].tensor, h * TOEP, [[1, 128], [1, 512]])

    top[0] = mark1
    tm = [sb(f"tm{i}", [128, S]) for i in range(4)]
    d_tm = [slot(f"d_tm{i}") for i in range(4)]
    Sp = [sb(f"Sp{i}", [128, S]) for i in range(2)]
    Pr = [sb(f"Pr{i}", [128, S]) for i in range(2)]
    Pr.append(sb("Pr2", [128, S]))
    PT_at = top[0]
    PT = [sb(f"PT{i}", [128, 4, S]) for i in range(2)]
    Sp_free, Pr_free, PT_free = [[], []], [[], [], []], [[], []]
    tm_free = [[] for _ in tm]
    mark2 = top[0]

    def fence():
        return [(q.sem, q.n) for q in (PE, V, A, P)]

    def join(f, *qs):
        for q in qs:
            q.items.append((flat([f]), lambda e: None, None, 0))

    def attention(items, wide, lead, qk, bias, slots, vpair, init, finish, fill=None):
        st = {}
        n = len(items)
        pend = []
        last_of = {h: q for q, (h, _) in enumerate(items)}
        for step in range(n + 4):
            for f_ in pend:
                f_()
            pend = []
            if step < n:
                h, i = items[step]
                W = 128 * len(slots(h, i))
                sbk = step % 2
                S_ps = ps[sbk]
                fr = free[2 * sbk] + free[2 * sbk + 1]
                last = None
                for lhsT, rhs, col, w_, tok in qk(h, i):
                    last = mm(S_ps[:, col:col + w_], lhsT, rhs, True, True, tok, fr, inc=1)
                j, jp = step % 2, step % 3
                bi = bias(h, i)
                mcol = mn[:, h:h + 1, i]
                ini = init(h)
                if bi is None:
                    m = V.put(lambda e, o=mcol, x=S_ps[:, :W]: e.tensor_reduce(o, x, AX.X, ALU.min), last)
                    src_, W_ = S_ps[:, :W], W
                else:
                    bap, btok = bi
                    if lead:
                        copy(V, Sp[j][:, 0:1], ini, Sp_free[j])
                    m = V.put(lambda e, o=Sp[j][:, lead:lead + W], x=S_ps[:, :W], y=bap, c=mcol, ini=ini:
                              e.tensor_tensor_reduce(o, x, y, 1.0, ini, ALU.add, ALU.min, c),
                              last, btok, Sp_free[j])
                    src_, W_ = Sp[j][:, :lead + W], W
                    free[2 * sbk] = free[2 * sbk + 1] = [m]
                st[step] = dict(m=m)
                if fill is not None:
                    fill(h, i, m)
            if step >= 3 and step - 3 < n and last_of[items[step - 3][0]] == step - 3:
                h = items[step - 3][0]
                ob = 6 + h % 2
                z = h % len(PT)
                cover = {}
                for i in range(4):
                    for b in slots(h, i):
                        cover.setdefault(b, []).append(i)
                order = sorted(cover, key=lambda b: -len(cover[b]))
                assert len(cover[order[0]]) == 4
                for b in order:
                    lo, hi = 128 * cover[b][0], 128 * cover[b][-1] + 128
                    vap, vtok = vpair(h, b)
                    last = mm(bank[ob][:, lo:hi], vap, PT[z][:, b, lo:hi], b == order[0], b == order[-1],
                              st["pt", h], vtok, free[ob], inc=int(b == order[-1]))
                PT_free[z] = [last]
                free[ob], then = finish(h, ob, last)
                pend.append(then)
            if 2 <= step <= n + 1:
                q = step - 2
                h, i = items[q]
                j, jp = q % 2, q % 3
                z = h % len(PT)
                if wide:
                    T_ps, tb_ = ps[2], [4, 5]
                else:
                    T_ps, tb_ = ps[2][:, 512 * j:512 * j + 512], [4 + j]
                bs = slots(h, i)
                for n_ in range(len(bs)):
                    c_ = n_ * 128
                    last = PE.put(lambda e, o=T_ps[:, c_:c_ + 128], x=Pr[jp][:, lead + c_:lead + c_ + 128]:
                                  e.transpose(o, x, ident), st[q]["p"], t_cn, [free[y] for y in tb_],
                                  inc=int(n_ == len(bs) - 1))
                Pr_free[jp] = [last]
                runs = []
                for n_, b in enumerate(bs):
                    if runs and b == runs[-1][1] + runs[-1][2]:
                        runs[-1][2] += 1
                    else:
                        runs.append([n_, b, 1])
                cs_ = []
                for n_, b, w_ in runs:
                    eq = A
                    cs_.append(copy(eq, PT[z][:, b:b + w_, i * 128:i * 128 + 128],
                                    T_ps[:, n_ * 128:(n_ + w_) * 128].rearrange("p (b n) -> p b n", n=128), last,
                                    PT_free[z]))
                for y in tb_:
                    free[y] = list(cs_)
                st["pt", h] = st.get(("pt", h), []) + cs_
            if step < n:
                h, i = items[step]
                j, jp = step % 2, step % 3
                sbk = j
                mcol = mn[:, h:h + 1, i]
                x = act(Pr[jp][:, :lead + W_], src_, ACT.Exp, st[step]["m"], Pr_free[jp], scale=-1.0, bias=mcol,
                        accum_out=den[:, h:h + 1, i])
                if bi is None:
                    free[2 * sbk] = free[2 * sbk + 1] = [x]
                else:
                    Sp_free[j] = [x]
                st[step]["x"] = x
            if 1 <= step <= n:
                h, i = items[step - 1]
                W = 128 * len(slots(h, i))
                p_ = Pr[(step - 1) % 3][:, lead:lead + W]
                dcol = den[:, h:h + 1, i]
                a = V.put(lambda e, d_=dcol: e.reciprocal(d_, d_), st[step - 1]["x"])
                st[step - 1]["p"] = ts(V, p_, p_, dcol, None, ALU.mult, None, a)
        for f_ in pend:
            f_()
        return fence()

    def in_blocks(x):
        return x.rearrange("p (i n) -> p i n", n=128)

    def turned(x):
        return x.rearrange("p (i n) -> p i n", n=128)[:, :, ::-1]

    def hk(z):
        return lambda k: z[:, k, :]

    xready = {k: [t_x[k // 2]] for k in range(KD)}
    h_done = [[]]
    for k in range(KD):
        add_square(XT[:, k, :], k, xready[k], V)
    advance()

    ssg = {"on": False, "tok": None}
    ssum_g = hf[1]

    def add_x(m, b, tok, scale=None, w=None, square=True):
        if scale is None:
            a = tt(V, XT[:, m, :], bank[b], XT[:, m, :], ALU.add, tok, xready[m])
        else:
            a = stt(XT[:, m, :], bank[b], scale, XT[:, m, :], ALU.mult, ALU.add, tok, xready[m], w)
        free[b] = [a]
        xready[m] = [a]
        if square:
            if ssg["on"]:
                g_ = M("final", m, m + 1)
                if m == 0:
                    ssg["tok"] = act(ssum_g[:], XT[:, m, :], ACT.Square, a, hf_free[1], scale=g_)
                else:
                    z = act(hf[0][:], XT[:, m, :], ACT.Square, a, hf_free[0], scale=g_)
                    ssg["tok"] = tt(V, ssum_g[:], ssum_g[:], hf[0][:], ALU.add, z, ssg["tok"])
                    hf_free[0] = [ssg["tok"]]
            add_square(XT[:, m, :], m, a)
        return a

    def pe_done():
        return (PE.sem, PE.n)

    later = []

    def flush_later():
        while later:
            later.pop(0)()

    macc_free = [[] for _ in range(8)]
    mod_state = {"i": 0, "n": 0, "last": None}

    def mod_unit():
        if "cs" not in mod_state:
            a1 = act(cs[:, :, 0], M("c"), ACT.Silu, t_sm)
            a2 = act(cs[:, :, 1], M("cctx"), ACT.Silu, t_sm)
            mod_state["cs"] = [a1, a2]
        u = mod_state["n"]
        mod_state["n"] += 1
        W_, tok = mbuf[u % 4], m_tok.pop(u)
        for r_ in range(2 if u < 16 else 1):
            j = mod_state["i"] % 8
            mod_state["i"] += 1
            a = ts(V, macc[j][:], W_[:, 0, :], cs[:, 0, r_:r_ + 1], None, ALU.mult, None, tok, mod_state["cs"],
                   macc_free[j])
            for k in range(1, KD):
                a = stt(macc[j][:], W_[:, k, :], cs[:, k, r_:r_ + 1], macc[j][:], ALU.mult, ALU.add, a)
            macc_t = a

            def total(j=j, r_=r_, a=a):
                x = mm(bank[7][:, 2 * u + r_:2 * u + r_ + 1], macc[j][:], C("ones", 0, 1), True, True, a, t_cn,
                       free[7], inc=1)
                macc_free[j] = [x]
                mod_state["last"] = x

            mod_later.append((mod_state["step"], total))
        mbuf_free[u % 4] = [macc_t]

    mod_later = []

    def mod_totals(step):
        while mod_later and mod_later[0][0] < step:
            mod_later.pop(0)[1]()

    m_tok, mbuf_free = {}, [[], [], [], []]
    d_mod = [slot(f"d_mod{i}") for i in range(4)]

    def mod_load(u):
        mod_state["loaded"] = u + 1
        m_tok[u] = SP.dma(lambda e: e.dma_start(mbuf[u % 4][:, :, :].rearrange("p k c -> p (k c)"), t["wmod"][u]),
                          d_mod[u % 4], mbuf_free[u % 4])

    def mod_flush():
        mod_totals(1 << 30)
        lo, hi = mod_state.get("from", 0), mod_state["n"]
        if hi > lo:
            pm = bank[7][:, 0:96].rearrange("p (a b) -> p a b", b=2)
            a = tt(V, modT[:, lo:hi, 0], pm[:, lo:hi, 0], M("bmod")[:, lo:hi], ALU.add, mod_state["last"], t_sm)
            mid = min(hi, 16)
            if mid > lo:
                a = tt(V, modT[:, lo:mid, 1], pm[:, lo:mid, 1], M("bmod")[:, lo:mid], ALU.add, mod_state["last"], t_sm)
            free[7] = [a]
            mod_state["from"] = hi
            mod_state["tok"] = a

    top[0] = mark1
    gH = sb("gH", [128, HALF, S], R)
    gL = sb("gL", [128, HALF, S], R)
    cv = [sb(f"cv{i}", [128, S]) for i in range(2)]
    cg_ = [sb(f"cg{i}", [128, S]) for i in range(2)]
    sg = [sb(f"sg{i}", [128, S]) for i in range(2)]
    macc = [sb(f"macc{i}", [128, 128]) for i in range(8)]
    mbuf = [sb(f"mbuf{i}", [128, KD, 128]) for i in range(4)]
    ffn_free = {"cv": [[], []], "cg": [[], []], "sg": [[], []], "g": []}

    def ffn(layer, up, down, gain, taps, cw, cb, spare, start, shift=None, gtok=None, scale=None):
        hw = norm_split(lambda k: XT[:, k, :], S, lambda k: xready[k], gain, hk(hH), hk(hL), h_done[0], shift, gtok)
        for q in "cv", "cg", "sg":
            ffn_free[q] = [list(start), list(start)]
        ffn_free["g"] = list(start)
        U["pool"] = spare
        if spare:
            macc_free[:] = [list(start) for _ in macc]
            mbuf_free[:] = [list(start) for _ in mbuf]
            end = mod_state["n"] + 24
            for u in range(4):
                mod_load(mod_state["n"] + u)
            assert mod_state["loaded"] == mod_state["n"] + 4

        def conv(b, n, dst, tok, fr):
            off0, j0 = taps[0]
            assert off0 == 0
            a = act(dst, bank[b], ACT.Identity, tok, fr, t_sm, scale=M(cw, j0 * 44 + n, j0 * 44 + n + 1),
                    bias=M(cb, n, n + 1))
            for off, j in taps[1:]:
                w_ = M(cw, j * 44 + n, j * 44 + n + 1)
                if off > 0:
                    a = stt(dst[:, off:], bank[b][:, :S - off], w_, dst[:, off:], ALU.mult, ALU.add, a)
                else:
                    a = stt(dst[:, :S + off], bank[b][:, -off:], w_, dst[:, :S + off], ALU.mult, ALU.add, a)
            free[b] = [a]
            return a

        for half in range(2):
            g_tok = []
            for j in range(HALF):
                n = half * HALF + j
                z = j % 2
                bv, bg = 0 + z, 2 + z
                tv = gemm_cols(up, n, [(hk(hH), hk(hL), bank[bv], hw)], free[bv])
                av = conv(bv, n, cv[z][:], tv, ffn_free["cv"][z])
                tg = gemm_cols(up, 22 + n, [(hk(hH), hk(hL), bank[bg], hw)], free[bg])
                ag = conv(bg, 22 + n, cg_[z][:], tg, ffn_free["cg"][z])
                mod_state["step"] = step_ = mod_state.get("step", 0) + 1
                mod_totals(step_ - 1)
                s_ = act(sg[z][:], cg_[z][:], ACT.Silu, ag, ffn_free["sg"][z])
                ffn_free["cg"][z] = [s_]
                p_ = tt(P, sg[z][:], sg[z][:], cv[z][:], ALU.mult, s_, av)
                ffn_free["cv"][z] = [p_]
                gh = copy(A, gH[:, j, :], sg[z][:], p_, ffn_free["g"])
                gl = tt(P, gL[:, j, :], sg[z][:], gH[:, j, :].bitcast(F), ALU.subtract, gh, ffn_free["g"])
                ffn_free["sg"][z] = [gl]
                g_tok.append([gh, gl])
                if spare:
                    while mod_state["loaded"] < min(end, mod_state["n"] + 4):
                        mod_load(mod_state["loaded"])
                    for _ in range(2 if j == 0 else 1):
                        mod_unit()
            h_done[0] = [pe_done()]
            ssg["on"] = layer == 1 and half == 1
            for m in range(8):
                b = 4 + m % 3
                tk = gemm_cols(down, half * 8 + m, [(hk(gH), hk(gL), bank[b], g_tok)], free[b])
                add_x(m, b, tk, None if scale is None else scale(m), gtok, half == 1)
            ffn_free["g"] = [tk]
            ssg["on"] = False
            if half == 1:
                U["pool"] = False
            if half == 0 and spare:
                mod_flush()
        if spare:
            mod_flush()
        return [tk, ffn_free["sg"][0], ffn_free["sg"][1], [xready[m] for m in range(8)]]

    TAPS1 = ((0, 2), (1, 1), (2, 0))
    TAPS2 = ((0, 1), (1, 0), (-1, 2))

    def attn_load_bias(h, slot_i, row, need):
        return SP.dma(lambda e: e.dma_start(tm[slot_i][:], toep_src(row)), d_tm[slot_i], t_toep, need)

    top[0] = mark2
    qT = sb("qT", [128, 8, S])
    kT = sb("kT", [128, 8, S])
    vR = sb("vR", [128, 4, D])
    kiT = Pr[2]
    wiR = sb("wiR", [128, 4, 16])
    sco = [None] + [sb(f"sco{i}", [128, 128 * (i + 1)]) for i in range(1, 4)]
    m8 = sb("m8", [128, 8])
    rl = Pr
    bz = sq
    qiT = sb("qiT", [128, 8, S], at=PT_at)

    def att_gain(name):
        return lambda k: M(name, k, k + 1)

    hw = norm_split(lambda k: XT[:, k, :], S, lambda k: xready[k], att_gain("attn0"), hk(hH), hk(hL), None,
                    gtok=t_sm)
    t_toep = tables()
    tk = gemm_cols("we", 0, [(hk(hH), hk(hL), bank[0], hw)], free[0])
    c0 = copy(V, kiT[:], bank[0], tk)
    free[0] = [c0]
    wit = Sp[0]
    tk = gemm_cols("wi", 0, [(hk(hH), hk(hL), bank[1][0:16, :], hw)], free[1])
    c1 = copy(A, turned(wit[0:16, :]), in_blocks(bank[1][0:16, :]), tk, scale=0.25)
    free[1] = [c1]

    def index_keys():
        a = sumsq(kiT[:], S, C("blk"), 6, [c0])
        r, a = rsqrt_of(rs[:], bank[6], 64, a, rs_free[0])
        free[6] = [a]
        k_ = stt(kiT[:], kiT[:], M("idxk"), rs[:], ALU.mult, ALU.mult, r, c0)
        rs_free[0] = [k_]
        for i in range(4):
            x = PE.put(lambda e, i=i: e.transpose(bank[5][:, i * 16:i * 16 + 16], wit[0:16, i * 128:i * 128 + 128],
                                                  C("ident", 0, 16)[0:16, :]), c1, t_cn, inc=int(i == 3))
        w_ = copy(V, wiR[:].rearrange("p a b -> p (a b)"), bank[5][:, 0:64], x)
        free[5] = [w_]
        return k_, w_

    t_qi = []
    for c in range(8):
        b = c % 4
        tk = gemm_cols("we", 1 + c, [(hk(hH), hk(hL), bank[b], hw)], free[b])
        if c == 0:
            t_ki, t_wi = index_keys()
        a = copy((V, A)[c % 2], turned(qiT[:, c, :]), in_blocks(bank[b]), tk)
        free[b] = [a]
        t_qi.append(a)
    t_sco = {}
    sc_free = [[], []]
    n = 0
    for i in range(1, 4):
        W = 128 * (i + 1)
        prev = None
        for h in range(16):
            b, z = 4 + n % 3, n % 2
            p0 = 64 * (h % 2)
            tk = mm(bank[b][:, :W], qiT[p0:p0 + 64, h // 2, i * 128:i * 128 + 128], kiT[p0:p0 + 64, :W], True, True,
                    t_ki, t_qi[h // 2], free[b], inc=1)
            a = act(rl[z][:, :W], bank[b][:, :W], ACT.Relu, tk, sc_free[z], scale=0.125)
            free[b] = [a]
            w_ = wiR[:, i, h:h + 1]
            if h == 0:
                prev = ts(V, sco[i][:], rl[z][:, :W], w_, None, ALU.mult, None, a, t_wi)
            else:
                prev = stt(sco[i][:], rl[z][:, :W], w_, sco[i][:], ALU.mult, ALU.add, a, prev, t_wi)
            sc_free[z] = [prev]
            n += 1
        prev = tt(V, sco[i][:, W - 128:W], sco[i][:, W - 128:W], C("causal"), ALU.add, prev, t_cn)
        t_sco[i] = prev
    topk_prog = []

    def topk_steps():
        for i in range(1, 4):
            src = sco[i]
            prev = t_sco[i]
            for r_ in range(KEEP // 8):
                a = V.put(lambda e, i=i: e.max(m8[:], sco[i][:]), prev)
                prev = V.put(lambda e, i=i: e.match_replace(sco[i][:], m8[:], sco[i][:], LOW), a)
                if r_ % 4 == 3:
                    yield None
            t_sco[i] = ts(V, sco[i][:], sco[i][:], -2e38, BIG, ALU.is_gt, ALU.mult, prev)
            yield None

    def v_unit(name, c, b, dst, key, *w):
        tk = gemm_cols(name, c, [(hk(hH), hk(hL), bank[b], hw)], free[b])
        j = c % 2
        a = copy(A, sq[j][:], bank[b], tk, sq_free[j])
        free[b] = [a]
        flush_later()

        def turn():
            z = 4 + j
            for i in range(4):
                x = PE.put(lambda e, o=bank[z][:, i * 128:i * 128 + 128], i_=sq[j][:, i * 128:i * 128 + 128]:
                           e.transpose(o, i_, ident), a, t_cn, free[z], inc=int(i == 3))
            sq_free[j] = [x]
            free[z] = [copy(A, dst, in_blocks(bank[z]), x, *w)]
            t_qk[key] = free[z][0]

        later.append(turn)

    tki = topk_steps()
    t_qk = {}
    for c in range(24):
        b = c % 4
        kind, cc = (c % 12) // 4, c % 4
        g = c // 12
        if kind < 2:
            tk = gemm_cols("we", 9 + c, [(hk(hH), hk(hL), bank[b], hw)], free[b])
            flush_later()
            dst = (qT, kT)[kind][:, g * 4 + cc, :]
            a = copy(A, turned(dst) if kind == 0 else in_blocks(dst), in_blocks(bank[b]), tk,
                     scale=(-0.125, 1.0)[kind])
            free[b] = [a]
            t_qk[(g, kind, cc)] = a
        else:
            o = g * 512 + cc * 128
            v_unit("we", 9 + c, b, vR[:, :, o:o + 128], (g, kind, cc))
        next(tki, None)
    flush_later()
    for _ in tki:
        pass
    h_done[0] = [pe_done()]

    def run_attn(heads, row0, masked):
        tmt = {}
        st = {"n": 0}

        def need(h):
            if h in tmt or h not in heads:
                return
            k = st["n"] % 4
            st["n"] += 1
            tmt[h] = (k, attn_load_bias(h, k, row0 + h, tm_free[k]))

        for h in heads[:4]:
            need(h)

        def qk(h, i):
            p0 = 64 * (h % 2)
            c = h // 2
            W = 128 * (i + 1)
            tok = [t_qk[(c // 4, 0, c % 4)], t_qk[(c // 4, 1, c % 4)]]
            return [(qT[p0:p0 + 64, c, i * 128:i * 128 + 128], kT[p0:p0 + 64, c, :W], 0, W, tok)]

        def bias(h, i):
            k, tok = tmt[h]
            bap = tm[k][:, 384 - 128 * i:512]
            if masked and i > 0:
                z = st["z"] = (st.get("z", 0) + 1) % 2
                W = 128 * (i + 1)
                a = tt(P, bz[z][:, :W], bap, sco[i][:], ALU.add, tok, t_sco[i], bz_free[z])
                st["bz"] = (z, a)
                st["tm", h] = a
                return bz[z][:, :W], [a]
            st["bz"] = None
            return bap, [tok]

        def fill(h, i, m):
            if st["bz"] is not None:
                bz_free[st["bz"][0]] = [m]
            if i == (3, 0)[h % 2]:
                k, _ = tmt[h]
                tm_free[k] = [m, st.get(("tm", h))]
                later = [x for x in heads if x not in tmt]
                if later:
                    need(later[0])

        def vpair(h, b):
            c = h // 2
            return vR[:, b, c * 128:c * 128 + 128], [t_qk[(c // 4, 2, c % 4)]]

        def finish(h, ob, tok):
            p0, c = 64 * (h % 2), h // 2
            x = turned(bank[ob][p0:p0 + 64, :])
            H, L = in_blocks(hH[p0:p0 + 64, c, :]), in_blocks(hL[p0:p0 + 64, c, :])
            a = copy(A, H, x, tok, h_done[0])
            free_ = []

            def low():
                d = tt(V, L, x, H.bitcast(F), ALU.subtract, a, h_done[0])
                free_.append(d)
                mt[c] += [a, d]

            return free_, low

        items = [(h + u, (i, 3 - i)[u]) for h in heads[::2] for i in range(4) for u in range(2)]
        return attention(items, False, 0, qk, bias,
                         lambda h, i: list(range(i + 1)), vpair, lambda h: BIG, finish, fill)

    bz_free = sq_free
    mt = [[] for _ in range(8)]
    t_mix = run_attn(list(range(8)), 0, False)
    t_mix = run_attn(list(range(8, 16)), 0, True)

    def mix_out(wo):
        for m in range(8):
            b = 4 + m % 3
            tk = gemm_cols(wo, m, [(hk(hH), hk(hL), bank[b], mt)], free[b])
            add_x(m, b, tk)
        h_done[0] = [tk]
        return tk

    tk = mix_out("wo0")
    start = [tk, t_mix]
    fin = ffn(0, "up0", "dn0", att_gain("ffn0"), TAPS1, "cw0", "cb0", True, start)

    hw = norm_split(lambda k: XT[:, k, :], S, lambda k: xready[k], att_gain("attn1"), hk(hH), hk(hL), h_done[0])
    for c in range(24):
        b = c % 4
        kind, cc = c // 8, c % 8
        if kind < 2:
            tk = gemm_cols("wq1", c, [(hk(hH), hk(hL), bank[b], hw)], free[b])
            dst = (qT, kT)[kind][:, cc, :]
            a = copy(A, turned(dst) if kind == 0 else in_blocks(dst), in_blocks(bank[b]), tk, fin,
                     scale=(-0.125, 1.0)[kind])
            free[b] = [a]
            t_qk[(cc // 4, kind, cc % 4)] = a
        else:
            v_unit("wq1", c, b, vR[:, :, cc * 128:cc * 128 + 128], (cc // 4, kind, cc % 4), fin)
    flush_later()
    h_done[0] = [pe_done()]
    for f_ in (tm_free, Sp_free, Pr_free, PT_free):
        f_[:] = [y + flat([fin]) for y in f_]
    mt = [[] for _ in range(8)]
    t_mix = run_attn(list(range(16)), 16, False)
    tk = mix_out("wo1")
    fin = ffn(1, "up1", "dn1", att_gain("ffn1"), TAPS1, "cw1", "cb1", True, [tk, t_mix])

    tmod = mod_state["tok"]
    gm = sc1[:, 8:16]
    gc = sc1[:, 16:24]
    gf = sc1[:, 24:32]
    g1 = stt(gm, modT[:, 8:16, 0], 1.0, M("mix2"), ALU.add, ALU.mult, tmod, t_sm)
    g2 = stt(gc, modT[:, 8:16, 1], 1.0, M("mix2"), ALU.add, ALU.mult, tmod, t_sm)
    g3 = stt(gf, modT[:, 32:40, 0], 1.0, M("ffn2"), ALU.add, ALU.mult, tmod, t_sm)
    qn8 = ts(V, sc1[:, 32:33], M("qn"), -0.125, None, ALU.mult, None, t_sm)
    g4 = tt(V, sc1[:, 48:56], gm, M("final"), ALU.mult, g1)
    nsk = ts(V, sc1[:, 40:48], M("sink"), -1.0, None, ALU.mult, None, t_sm)
    smalls2 = [g1, g2, g3, g4, qn8, nsk]
    f0 = fence()
    join(f0, V, A, P, PE)

    top[0] = mark1
    hcH = sb("hcH", [128, KD, CTX], R)
    hcL = sb("hcL", [128, KD, CTX], R)
    mixed2 = sb("mixed2", [128, 8, S])
    yc_at = top[0]
    yc = sb("yc", [128, 4, S])
    mark3 = top[0]
    Sp = [sb(f"Sq{i}", [128, 641]) for i in range(2)]
    Pr = [sb(f"Pq{i}", [128, 768]) for i in range(3)]
    PT = [sb("PU", [128, 6, S])]
    aqT = sb("aqT", [128, 4, S])
    bqT = sb("bqT", [128, 4, S])
    akT, bkT = sb("akT", [128, 768], at=yc_at), sb("bkT", [128, 768])
    avR, bvR = [[sb(f"{x}{i}", [128, 3, 128], at=tails[2 * (x == "bvR") + i]) for i in range(2)]
                for x in ("avR", "bvR")]
    ropes = sb("ropes", [128, 2, S], at=yc_at + 3072)
    band = sb("band", [128, 1152])
    d_b2 = [slot(f"d_b2{i}") for i in range(5)]
    ctxT = mixed2[:, :, :].rearrange("p a b -> p (a b)")[:, 0:2048].rearrange("p (k n) -> p k n", k=8)
    qtmp = [mixed2[:, 4 + i, :] for i in range(4)]
    qt_free = [[] for _ in range(4)]
    t_ctx = SP.dma(lambda e: e.dma_start(ctxT, t["ctxT"]), d_b2[0], f0)
    t_rope = SP.dma(lambda e: e.dma_start(ropes[:], t["ropes"]), d_b2[1], f0)
    t_band = SP.dma(lambda e: e.dma_start(band[:], t["band"]), d_b2[2], f0)
    for z in (Sp_free, Pr_free, PT_free):
        z[:] = [[] for _ in z]

    r1 = norm_scale(S)
    tg = mm(bank[6], C("ones"), ssum_g[:], True, True, ssg["tok"], free[6], inc=1)
    hf_free[1] = [tg]
    rr = ssum
    a = tt(V, rr[:], bank[6], rs[:], ALU.mult, tg, r1, ss["free"])
    free[6] = [a]
    a = tt(V, rr[:], rr[:], rs[:], ALU.mult, a)
    a, _ = rsqrt_of(rr[:], rr[:], D, a)
    r12 = tt(V, rr[:], rr[:], rs[:], ALU.mult, a)
    hw = norm_split(lambda k: XT[:, k, :], S, lambda k: xready[k], lambda k: sc1[:, 48 + k:49 + k], hk(hH),
                    hk(hL), h_done[0], shift=lambda k: modT[:, k, 0:1], gtok=smalls2, scale=(rr[:], [r12]))
    for k in range(KD):
        a = stt(XT[:, k, :], XT[:, k, :], M("final", k, k + 1), rs[:], ALU.mult, ALU.mult, r1, xready[k])
        xready[k] = [a]
    rs_free[0] = [a]
    ss["free"] = [a]
    hcl = []
    for k in range(KD):
        add_square(ctxT[:, k, :], k, t_ctx)

    def norm_context():
        hcl.extend(norm_split(lambda k: ctxT[:, k, :], CTX, lambda k: [t_ctx], lambda k: gc[:, k:k + 1],
                              hk(hcH), hk(hcL), None, shift=lambda k: modT[:, k, 1:2], gtok=smalls2))

    def both(b0, b1):
        return [(hk(hH), hk(hL), bank[b0], hw), (hk(hcH), hk(hcL), bank[b1][:, :CTX], hcl)]

    def b128(b, c):
        return bank[b][:, c * 128:c * 128 + 128]

    def b3(x, n):
        return x.rearrange("p (i d) -> p i d", i=n)

    def head_norm(x, n, gain, w, b=7):
        a = sumsq(x, n, C("blk"), b, w)
        r, a1 = rsqrt_of(rs[:, :n], bank[b][:, :n], 64, a, rs_free[0])
        free[b] = [a1]
        a = stt(x, x, gain, rs[:, :n], ALU.mult, ALU.mult, r, w)
        rs_free[0] = [a]
        return a

    def turn6(dst, src, b0, b1, *w):
        for c in range(6):
            o = b128((b0, b1)[c // 3], c % 3)
            x = PE.put(lambda e, o=o, i_=src[:, c * 128:c * 128 + 128]: e.transpose(o, i_, ident), list(w), t_cn,
                       free[b0], free[b1], inc=int(c == 5))
        a = copy(V, dst[0], b3(bank[b0][:, 0:384], 3), x)
        c = copy(V, dst[1], b3(bank[b1][:, 0:384], 3), x)
        free[b0], free[b1] = [a], [c]
        return [a, c]

    rope_n = [0]

    def rope(dst, x, w):
        b = 4 + rope_n[0] % 2
        j = rope_n[0] % 2
        rope_n[0] += 1
        a = mm(bank[b], C("rot"), x, True, True, w, t_cn, free[b], inc=1)
        u = tt(V, hf[j][:], bank[b], ropes[:, 1, :], ALU.mult, a, t_rope, hf_free[j])
        free[b] = [u]
        c = tt(P, dst, x, ropes[:, 0, :], ALU.mult, w, t_rope)
        d = tt(P, dst, dst, hf[j][:], ALU.add, c, u)
        hf_free[j] = [d]
        return a, d

    t_k2, t_v2, t_q2 = {}, {}, {}
    jobs = []

    def step_jobs():
        for j_ in list(jobs):
            if next(j_, "end") == "end":
                jobs.remove(j_)

    def start_job(j_):
        step_jobs()
        next(j_)
        jobs.append(j_)

    def k_job(g, tk):
        kT2, z = (akT, bkT)[g], g
        a = copy(A, qtmp[z], bank[0], tk, qt_free[z])
        c = copy(A, kT2[:, S:], bank[1][:, :CTX], tk)
        free[0], free[1] = [a], [c]
        yield
        if g == 1:
            a = head_norm(qtmp[z], S, M("kn"), [a])
            c = head_norm(kT2[:, S:], CTX, M("kn"), [c])
            yield
        x1, x2 = rope(kT2[:, 0:S], qtmp[z], [a])
        qt_free[z] = [x1, x2]
        t_k2[g] = [x2, c]

    def v_job(g, tk):
        a = copy(A, Pr[g][:, 0:S], bank[2], tk)
        c = copy(A, Pr[g][:, S:768], bank[3][:, :CTX], tk)
        free[2], free[3] = [a], [c]
        yield
        t_v2[g] = turn6([y[:, :, :] for y in (avR, bvR)[g]], Pr[g], 4, 5, a, c)

    def q_job(g, c, b, z, tk):
        a = copy(A, qtmp[z], bank[b], tk, qt_free[z], scale=(-0.125, 1.0)[g])
        free[b] = [a]
        yield
        if g == 1:
            a = head_norm(qtmp[z], S, sc1[:, 32:33], [a, qn8])
            yield
        x1, x2 = rope((aqT, bqT)[g][:, c, :], qtmp[z], [a])
        qt_free[z] = [x1, x2]
        t_q2[(g, c)] = x2

    def q_units(g):
        for c in range(4):
            tk = gemm_cols("win", (0, 6)[g] + c, [(hk(hH), hk(hL), bank[c], hw)], free[c])
            start_job(q_job(g, c, c, c, tk))
            if g == 0 and c == 1:
                norm_context()

    q_units(0)
    for g in range(2):
        tk = gemm_cols("win", (4, 10)[g], both(0, 1), free[0], free[1])
        start_job(k_job(g, tk))
        tk = gemm_cols("win", (5, 11)[g], both(2, 3), free[2], free[3])
        start_job(v_job(g, tk))
    q_units(1)
    while jobs:
        step_jobs()
    join([hcl], V, A)

    def local(i):
        return max(i - 1, 0), min(i + 1, 3)

    def qk2(h, i):
        g, h = h // 8, h % 8
        p0 = 64 * (h // 4)
        q = (aqT, bqT)[g][p0:p0 + 64, h % 4, i * 128:i * 128 + 128]
        k = (akT, bkT)[g][p0:p0 + 64, :]
        tok = [t_q2[(g, h % 4)], t_k2[g]]
        if g == 1:
            return [(q, k[:, 0:512], 0, 512, tok), (q, k[:, 512:768], 512, 256, tok)]
        lo, hi = local(i)
        out_ = [(q, k[:, 512:768], 0, 256, tok), (q, k[:, lo * 128:lo * 128 + 256], 256, 256, tok)]
        if hi - lo == 2:
            out_.append((q, k[:, hi * 128:hi * 128 + 128], 512, 128, tok))
        return out_

    def bias2(h, i):
        if h >= 8:
            return None
        lo, hi = local(i)
        n_ = 256 + 128 * (hi - lo + 1)
        return (band[:, 640:640 + n_] if i == 0 else band[:, 0:n_]), [t_band]

    def slots2(h, i):
        lo, hi = local(i)
        return list(range(6)) if h >= 8 else [0, 1] + [2 + b for b in range(lo, hi + 1)]

    def vpair2(h, b):
        g = h // 8
        blk_ = b if g else (4 + b if b < 2 else b - 2)
        return (avR, bvR)[g][blk_ // 3][:, blk_ % 3, :], [t_v2[g]]

    t_mx = {}

    def finish2(h, ob, tok):
        p0 = 64 * (h % 8 // 4)
        a = copy((V, A)[h % 2], mixed2[p0:p0 + 64, 4 * (h // 8) + h % 4, :], bank[ob][p0:p0 + 64, :], tok)
        return [a], lambda: None

    attention([(h, i) for h in range(8) for i in range(4)], True, 1, qk2, bias2, slots2, vpair2,
              lambda h: sc1[:, 40 + h:41 + h], finish2)
    join([qt_free], V, A)
    t_mx = attention([(h, i) for h in range(8, 16) for i in range(4)], True, 0, qk2, bias2, slots2, vpair2,
                     lambda h: BIG, finish2)

    f1 = fence()
    join(f1, V, A, P, PE)
    top[0] = mark3
    decR = sb("decR", [128, 2, 1024], R)
    uR = sb("uR", [128, 2, 128], R, at=tails[0])
    lmask = [sb(f"lmask{i}", [128, 8 - i, 128], U8, at=tails[1 + i]) for i in range(2)]
    zc = [sb(f"zc{i}", [128, 768]) for i in range(2)]
    vc = sb("vc", [128, 768])
    t6, lfc = sb("t6", [128, 768]), sb("lfc", [128, 768])
    lfH, lfL = sb("lfH", [128, 6, 128], R), sb("lfL", [128, 6, 128], R)
    kcc = [sb(f"kcc{i}", [128, 768]) for i in range(2)]
    kd = lfc[:, :].rearrange("p (c n) -> p c n", n=128)
    vr = sb("vr", [128, 6, 128])
    qts = [sb(f"qt{i}", [128, S]) for i in range(2)]
    E4 = sb("E4", [128, 4, 4, 128])
    Z = [in_blocks(ssum[:, :]), in_blocks(hf[1][:, :])]
    scT = in_blocks(hf[0][:, :])
    qa = [in_blocks(sq[i][:, :]) for i in range(2)]
    st8 = [sb(f"st{i}", [128, 3, 128], at=tails[3 + i]) for i in range(3)]

    def state(d, c):
        n_ = 4 * d + c
        return st8[n_ // 3][:, n_ % 3, :]

    def mask(n_):
        return lmask[n_ // 8][:, n_ % 8:n_ % 8 + 1, :].to_broadcast([128, 4, 128])

    f6 = sb("f6", [128, 2, 6])
    f6r = sb("f6r", [128, 6])
    e4f = E4[:, :, :, :].rearrange("p a b c -> p (a b c)")
    a = SP.dma(lambda e: e.dma_start(e4f, t["decay"].rearrange("p a b -> p (a b)")), d_b2[3], f1)
    t_dec = V.put(lambda e: e.tensor_copy(decR[:, :, :].rearrange("p a b -> p (a b)"), e4f), a)
    lmf = e4f[:, 0:15 * 128].rearrange("p (m n) -> p m n", m=15)
    a = SP.dma(lambda e: e.dma_start(lmf, t["lmask"]), d_b2[4], t_dec)
    t_lm = [V.put(lambda e: e.tensor_copy(lmask[0][:], lmf[:, 0:8, :]), a),
            V.put(lambda e: e.tensor_copy(lmask[1][:], lmf[:, 8:15, :]))]
    t_u0 = copy(V, uR[:, 0, :], C("uf"), t_cn)
    t_u1 = copy(V, uR[:, 1, :], C("ub"), t_cn)
    t_u = [t_u0, t_u1]
    z_fr, vc_fr, q_fr = [[], []], [[]], [[], []]
    z_tk, vc_tk, q_tk, s_tk = {}, {}, {}, {}

    def projections(h):
        def two(unit, dst, fr, key, out_):
            res = []
            yield from gemm_steps("win", unit, both(0, 1), 1, res, free[0], free[1])
            a = copy(A, dst[:, 0:S], bank[0], res[0], fr[0])
            c = copy(A, dst[:, S:768], bank[1][:, :CTX], res[0])
            free[0], free[1] = [a], [c]
            out_[key] = [a, c]

        def one(unit, b, dst, fr, out_):
            res = []
            yield from gemm_steps("win", unit, [(hk(hH), hk(hL), bank[b], hw)], 2, res, free[b])
            a = act(dst, bank[b], ACT.Silu, res[0], fr)
            free[b] = [a]
            out_[h] = a

        yield from two(16 + h, zc[0], [z_fr[0]], (h, 0), z_tk)
        yield from two(24 + h, vc, vc_fr, h, vc_tk)
        yield from one(12 + h, 0, qts[h % 2][:], q_fr[h % 2], q_tk)
        yield from two(20 + h, zc[1], [z_fr[1]], (h, 1), z_tk)
        yield from one(28 + h, 1, yc[:, h, :], None, s_tk)

    gen = None

    def tick(n_=1):
        for _ in range(n_):
            next(gen, None)

    lf_fr, kd_fr, kc_fr, vr_fr, qa_fr, st_fr, sc_fr2 = [], [], [[], []], [], [[], []], [[], []], []
    t6_fr, e_free, z_f = [], [t_lm], [[], []]
    sc_t = None
    fg = {}

    def forget_a(h, d):
        x = act(t6[:], zc[d][:], ACT.Abs, z_tk[(h, d)], t6_fr)
        x = act(t6[:], t6[:], ACT.Exp, x, scale=-1.0)
        fg["ln"] = act(t6[:], t6[:], ACT.Ln, x, bias=1.0)

    def forget_b(h, d):
        lf_t = stt(lfc[:], zc[d][:], 0.0, t6[:], ALU.min, ALU.subtract, fg["ln"], z_tk[(h, d)], lf_fr, kd_fr)
        x = tt(V, t6[:], lfc[:], zc[d][:], ALU.subtract, lf_t)
        z_fr[d] = [x]
        k_ = act(kcc[d][:], t6[:], ACT.Exp, x, kc_fr[d])
        x = V.put(lambda e: e.tensor_reduce(f6r[:], lfc[:, :].rearrange("p (c n) -> p c n", n=128), AX.X,
                                            ALU.add), lf_t, fg.get("f6"))
        fg["f6"] = act(f6[:, d, :], f6r[:], ACT.Exp, x, st_fr[d])
        fg[(h, d)] = (lf_t, k_, fg["f6"])

    def tail(h, x):
        sq_free[0] = [x]
        a = sumsq(bank[2], S, C("ones"), 3, x)
        qa_fr[0] = [a]
        r, a1 = rsqrt_of(rs[:], bank[3], 128, a, rs_free[0])
        free[3] = [a1]
        y = stt(rs[:], bank[2], M("gn"), rs[:], ALU.mult, ALU.mult, r, x)
        free[2] = [y]
        y = tt(P, yc[:, h, :], yc[:, h, :], rs[:], ALU.mult, y, s_tk[h])
        rs_free[0] = [y]
        return y

    gen = projections(0)
    tick(9)
    forget_a(0, 0)
    tick(8)
    forget_b(0, 0)
    for _ in gen:
        pass
    ends = []
    for h in range(4):
        gen = projections(h + 1) if h < 3 else iter(())
        qt = in_blocks(qts[h % 2][:, :])
        qa_t, st_t, kc_t = {}, {}, {}
        for d in range(2):
            lf_t, kc_t[d], f6_t = fg[(h, d)]
            tick(4 if d == 0 else 2)
            for c in range(6):
                o = b128(4 + c // 4, c % 4)
                x = PE.put(lambda e, o=o, i_=lfc[:, c * 128:c * 128 + 128]: e.transpose(o, i_, ident), lf_t,
                           free[4], free[5], inc=int(c == 5))
            lf_fr = [x]
            a1 = copy(A, lfH[:, 0:4, :], b3(bank[4], 4), x)
            a2 = copy(A, lfH[:, 4:6, :], b3(bank[5][:, :CTX], 2), x)
            b1 = tt(V, lfL[:, 0:4, :], b3(bank[4], 4), lfH[:, 0:4, :].bitcast(F), ALU.subtract, a1)
            b2 = tt(V, lfL[:, 4:6, :], b3(bank[5][:, :CTX], 2), lfH[:, 4:6, :].bitcast(F), ALU.subtract, a2)
            free[4], free[5] = [b1], [b2]
            lr_t = [a1, a2, b1, b2]
            if d == 0:
                v_t = turn6([vr[:, 0:3, :], vr[:, 3:6, :]], vc, 6, 7, vc_tk[h], vr_fr)
                vc_fr[0] = v_t
            if ends:
                tail(*ends)
                ends = []
            tick(2)
            for c in range(6):
                o = b128(6 + c // 4, c % 4)
                xk = PE.put(lambda e, o=o, i_=kcc[d][:, c * 128:c * 128 + 128]: e.transpose(o, i_, ident), kc_t[d],
                            free[6], free[7], inc=int(c == 5))
            mm(bank[4], uR[:, d, :], lfH[:, 0:4, :], True, False, lr_t, free[4], t_u)
            mm(bank[4], uR[:, d, :], lfL[:, 0:4, :], False, True)
            mm(bank[5][:, :CTX], uR[:, d, :], lfH[:, 4:6, :], True, False, free[5])
            x = mm(bank[5][:, :CTX], uR[:, d, :], lfL[:, 4:6, :], False, True, inc=1)
            e1 = act(t6[:, 0:S], bank[4], ACT.Exp, x, kc_t[d])
            e2 = act(t6[:, S:768], bank[5][:, :CTX], ACT.Exp, x)
            free[4], free[5] = [e1], [e2]
            k1 = tt(V, kd[:, 0:4, :], b3(bank[6], 4), in_blocks(t6[:, 0:S]), ALU.mult, e1, xk, kd_fr)
            k2 = tt(V, kd[:, 4:6, :], b3(bank[7][:, :CTX], 2), in_blocks(t6[:, S:768]), ALU.mult, e2, xk, kd_fr)
            free[6], free[7] = [k1], [k2]
            t6_fr = [k1, k2]

            def decays(grp):
                et_ = []
                for c in range(4):
                    b = 4 + c
                    mm(bank[b], lfH[:, c, :], decR[:, d, grp * 512:grp * 512 + 512], True, False, t_dec, lr_t,
                       free[b])
                    x = mm(bank[b], lfL[:, c, :], decR[:, d, grp * 512:grp * 512 + 512], False, True, inc=1)
                    x = act(E4[:, c, :, :], b3(bank[b], 4), ACT.Exp, x, e_free)
                    free[b] = [x]
                    et_.append(x)
                return et_

            et = decays(0)
            e_free = []
            for c in range(6):
                o = b128(2, c) if c < 4 else b128(3, c - 4)
                x = mm(o, kd[:, c, :], vr[:, c, :], True, True, k1, k2, v_t, free[2], free[3], inc=int(c == 5))
            kd_fr = [x]
            tick(1)
            first, second = ((4, 5), (5, 4))[d]
            s0 = (0, 3)[d]
            prev = copy(V, state(d, s0), b128(3, first - 4), x, st_fr[d])
            prev = stt(state(d, s0), state(d, s0), f6[:, d, second:second + 1], b128(3, second - 4),
                       ALU.mult, ALU.add, prev, f6_t)
            free[3] = [prev]
            for c in ((0, 1, 2), (3, 2, 1))[d]:
                to = c + (1, -1)[d]
                prev = stt(state(d, to), state(d, c), f6[:, d, c:c + 1], b128(2, c), ALU.mult, ALU.add,
                           prev)
            free[2] = [prev]
            st_t[d] = prev
            if d == 1:
                zi_tok = tt(P, Z[0], in_blocks(kcc[0][:, 0:S]), in_blocks(kcc[1][:, 0:S]), ALU.add, kc_t[0],
                            kc_t[1], z_f[0])
                for c in range(4):
                    y = mm(b128(3, c), Z[0][:, c, :], qt[:, c, :], True, True, zi_tok, q_tk[h], free[3],
                           inc=int(c == 3))
                z_f[0] = [y]
                sc_t = V.put(lambda e: e.copy_predicated(scT, mask(14), b3(bank[3], 4)), y, sc_t, t_lm)
                free[3] = [sc_t]
                kc_fr[0] = kc_fr[0] + [zi_tok]
            kv_ = in_blocks(kcc[d][:, 0:S])
            qa_t[d] = tt(V, qa[d], qt, E4[:, :, 0, :], ALU.mult, et, q_tk[h], qa_fr[d])
            e_free.append(qa_t[d])
            made = {}

            def produce(mat):
                b_, z_ = LEVELS[mat - 1], mat % 2

                def view(y_):
                    return y_.rearrange("p c (n u b) -> p c n u b", u=2, b=b_)

                uq = (1, 0)[d]
                Ev, Zv, Qv, Kv = view(E4[:, :, mat % 4, :]), view(Z[z_]), view(qt), view(kv_)
                w1 = pair_mult(V, Zv, Ev, Qv, uq, et, z_f[z_], q_tk[h])
                w2 = pair_mult(P, Zv, Ev, Kv, 1 - uq, et, z_f[z_], kc_t[d])
                made[mat] = [w1, w2]
                e_free.extend([w1, w2])

            def consume(mat):
                z_, pb = mat % 2, 2 + mat % 2
                for c in range(4):
                    x = mm(b128(pb, c), Z[z_][:, c, :], Z[z_][:, c, :], True, True, made[mat], free[pb],
                           inc=int(c == 3))
                z_f[z_] = [x]
                mk = mask(2 * (mat - 1) + d)
                t_ = V.put(lambda e: e.copy_predicated(scT, mk, b3(bank[pb], 4)), x, sc_t, t_lm, sc_fr2)
                free[pb] = [t_]
                return t_

            produce(1)
            produce(2)
            tick()
            sc_t = consume(1)
            produce(3)
            tick()
            sc_t = consume(2)
            et = decays(1)
            e_free = []
            tick(2)
            sc_t = consume(3)
            produce(4)
            produce(5)
            tick(2)
            nxt = (h, 1) if d == 0 else (h + 1, 0)
            if nxt[0] < 4:
                forget_a(*nxt)
            sc_t = consume(4)
            produce(6)
            tick()
            sc_t = consume(5)
            produce(7)
            kc_fr[d] = made[7]
            if nxt[0] < 4:
                forget_b(*nxt)
            tick()
            sc_t = consume(6)
            sc_t = consume(7)
        for _ in gen:
            pass
        for c in range(4):
            mm(b128(2, c), vr[:, c, :], scT[:, c, :], True, False, v_t, sc_t, free[2])
            mm(b128(2, c), state(0, c), qa[0][:, c, :], False, False, st_t[0], qa_t[0])
            x = mm(b128(2, c), state(1, c), qa[1][:, c, :], False, True, st_t[1], qa_t[1], inc=1)
        vr_fr, sc_fr2 = [x], [x]
        qa_fr, st_fr = [[x], [x]], [[x], [x]]
        q_fr[h % 2] = [x]
        ends = [h, x]
    y = tail(*ends)

    f2 = fence()
    join(f2, V, A, P, PE)
    top[0] = mark3
    yH, yL = sb("yH", [128, 12, S], R), sb("yL", [128, 12, S], R)
    acc = [rs, sb("acc1", [128, S])]
    gt, tmp = sq, hf
    top[0] = mark1
    mH, mL = sb("mH", [128, KD, S], R), sb("mL", [128, KD, S], R)
    ty = []
    for c in range(12):
        src = mixed2[:, c, :] if c < 8 else yc[:, c - 8, :]
        a = copy(A, yH[:, c, :], src)
        b = tt((V, P)[c % 2], yL[:, c, :], src, yH[:, c, :].bitcast(F), ALU.subtract, a)
        ty.append([a, b])
    acc_f, gt_f, tmp_f = [rs_free[0], []], sq_free, hf_free
    tm_ = []
    n = 0
    for m in range(8):
        j = m % 2
        for br in range(3):
            z = n % 2
            n += 1
            tk = gemm_cols("win", 32 + 8 * br + m, [(hk(hH), hk(hL), bank[z], hw)], free[z])
            g_ = act(gt[z][:], bank[z], ACT.Sigmoid, tk, gt_f[z])
            free[z] = [g_]
            tk = gemm_cols("wbr", 8 * br + m, [(lambda k, br=br: yH[:, 4 * br + k, :],
                                                lambda k, br=br: yL[:, 4 * br + k, :], bank[2 + z],
                                                ty[4 * br:4 * br + 4])], free[2 + z])
            if br == 0:
                a = tt(V, acc[j][:], bank[2 + z], gt[z][:], ALU.mult, tk, g_, acc_f[j])
                free[2 + z], gt_f[z] = [a], [a]
                prev = a
            else:
                a = tt(V, tmp[z][:], bank[2 + z], gt[z][:], ALU.mult, tk, g_, tmp_f[z])
                free[2 + z], gt_f[z] = [a], [a]
                prev = tt(P, acc[j][:], acc[j][:], tmp[z][:], ALU.add, a, prev)
                tmp_f[z] = [prev]
        a = copy(A, mH[:, m, :], acc[j][:], prev)
        b = tt(P, mL[:, m, :], acc[j][:], mH[:, m, :].bitcast(F), ALU.subtract, a, prev)
        acc_f[j] = [a, b]
        tm_.append([a, b])
    rs_free[0] = acc_f[0]
    h_done[0] = [tk]
    for m in range(8):
        b = 4 + m % 3
        tk = gemm_cols("wout", m, [(hk(mH), hk(mL), bank[b], tm_)], free[b])
        add_x(m, b, tk, modT[:, 16 + m, 0:1], tmod)
    f3 = fence()
    ffn(2, "up2", "dn2", lambda k: gf[:, k:k + 1], TAPS2, "dw2", "db2", False, f3,
        shift=lambda k: modT[:, 24 + k, 0:1], gtok=smalls2, scale=lambda m: modT[:, 40 + m, 0:1])

    r = norm_scale(S)
    g = "final2"
    d_out = slot("d_out")
    for k in range(KD):
        a = stt(XT[:, k, :], XT[:, k, :], M(g, k, k + 1), rs[:], ALU.mult, ALU.mult, r, xready[k])
        tk = SP.dma(lambda e, k=k: e.dma_start(out[:, k, :], XT[:, k, :]), d_out, a)
    SP.items.append(([tk], lambda e: None, None, 0))
    SP.items.append(([t_toep], lambda e: None, None, 0))

    blk = ctx.enter_context(nc.Block())

    @blk.sync
    def _(e):
        SP.run(e)

    @blk.tensor
    def _(e):
        PE.run(e)

    @blk.vector
    def _(e):
        V.run(e)

    @blk.scalar
    def _(e):
        A.run(e)

    @blk.gpsimd
    def _(e):
        P.run(e)


def constants():
    c = np.zeros((128, N_CN), np.float32)

    def put(name, v):
        c[:, CN[name][0]:CN[name][1]] = v

    i = np.arange(128)
    put("ident", np.eye(128))
    put("ones", 1.0)
    put("blk", (i[:, None] // 64 == i[None, :] // 64))
    put("causal", np.where(i[None, :] <= 127 - i[:, None], 0.0, -BIG))
    rot = np.zeros((128, 128), np.float32)
    for a in range(64):
        rot[2 * a + 1, 2 * a] = -1.0
        rot[2 * a, 2 * a + 1] = 1.0
    put("rot", rot)
    s, tt_ = i[:, None], i[None, :]
    put("uf", s > tt_)
    put("ub", s < tt_)
    mf, mb = [s <= tt_], [s >= tt_]
    masks = []
    for b in LEVELS:
        mid = tt_ // (2 * b) * (2 * b) + b
        up = tt_ >= mid
        mf.append(np.where(up, (s >= mid) & (s <= tt_), (s > tt_) & (s < mid)))
        mb.append(np.where(up, (s >= mid) & (s < tt_), (s >= tt_) & (s < mid)))
        same = s // (2 * b) == tt_ // (2 * b)
        masks.append(same & (s < mid) & (tt_ >= mid))
        masks.append(same & (s >= mid) & (tt_ < mid))
    masks.append(np.eye(128))
    msk = np.stack(masks, 1).astype(np.float32)
    w = np.arange(TOEP)
    d = 511 - w
    n = np.maximum(d, 0)
    nf = np.maximum(n, 16).astype(np.float32)
    large = 16 + (np.log(nf / np.float32(16)) / np.float32(math.log(128 / 16)) * np.float32(16)).astype(np.int32)
    bucket = np.where(n < 16, n, np.minimum(large, 31))
    oh = np.zeros((32, TOEP), np.float32)
    oh[bucket, w] = -1.0
    mr = np.zeros((32, TOEP), np.float32)
    mr[:, d < 0] = BIG
    cnt = ((d >= 0) & (d <= 128)).astype(int) + ((d >= 0) & (d % 4 == 0)) + ((d >= 0) & (d % 16 == 0))
    mr[16:, :] = np.where(cnt > 0, -np.log(np.maximum(cnt, 1)), BIG)
    tpos = np.arange(S)
    inv = (np.float32(10000.0) ** (-np.arange(0, 32, 2, dtype=np.float32) / np.float32(32))).astype(np.float32)
    ang = np.concatenate([(tpos // 64).astype(np.float32)[:, None] * inv, (tpos % 64).astype(np.float32)[:, None] * inv], 1)
    cs = np.stack([np.cos(ang), np.sin(ang)], 0).astype(np.float32)
    cs = np.repeat(cs, 2, axis=2).transpose(2, 0, 1)
    cs = np.concatenate([cs, cs], 0)
    j = np.arange(384)
    near = np.where(np.abs(j[None, :] - 128 - i[:, None]) <= 128, 0.0, BIG)
    band = np.zeros((128, 1152), np.float32)
    band[:, 256:640] = near
    band[:, 896:] = near[:, 128:]
    return {"consts": c, "decay": np.stack([np.concatenate(mf, 1), np.concatenate(mb, 1)], 1).astype(np.float32), "lmask": msk, "onehot": oh, "maskrow": mr, "ropes": np.ascontiguousarray(cs), "band": band}


def pack(w, kt=None):
    K, N = w.shape
    return np.ascontiguousarray(w.reshape(K // 128, 128, N // 128, 128).transpose(2, 1, 0, 3)).reshape(
        N // 128, 128, K)


def cols(v):
    return v.reshape(-1, 128).T


def lay(i):
    o = constants()
    g = {k: np.asarray(v) for k, v in i.items()}
    sm = np.zeros((128, N_SM), np.float32)

    def put(name, v):
        sm[:, SM[name][0]:SM[name][1]] = v

    for l in range(2):
        put(f"attn{l}", cols(g["attn_norm"][l]))
        put(f"ffn{l}", cols(g["ffn_norm"][l]))
        put(f"cw{l}", cols(g["conv_w"][l]))
        put(f"cb{l}", cols(g["conv_b"][l]))
    put("final", cols(g["final_norm"]))
    put("mix2", cols(g["norm_mix_2"]))
    put("ffn2", cols(g["norm_ffn_2"]))
    put("final2", cols(g["norm_final_2"]))
    put("dw2", cols(g["w_dw_2"]))
    put("db2", cols(g["b_dw_2"]))
    put("bmod", cols(g["b_mod_2"]))
    put("idxk", np.tile(g["idx_k_norm"].reshape(64), 2)[:, None])
    put("qn", np.tile(g["qn_b_2"].reshape(64), 2)[:, None])
    put("kn", np.tile(g["kn_b_2"].reshape(64), 2)[:, None])
    put("gn", g["gn_c_2"].reshape(128, 1))
    put("sink", np.broadcast_to(g["sink_a_2"].reshape(1, 8), (128, 8)))
    put("c", cols(g["c_2"]))
    put("cctx", cols(g["c_ctx_2"]))
    o["smalls"] = sm
    o["xT"] = np.ascontiguousarray(g["x"][0].T.reshape(8, 128, S).transpose(1, 0, 2))
    o["ctxT"] = np.ascontiguousarray(g["ctx_2"][0].T.reshape(8, 128, CTX).transpose(1, 0, 2))
    o["rel"] = np.concatenate([g["rel_bias"], g["rel_bias"]], 1)
    we = g["w_in_even"][0]
    o["we"] = np.concatenate([pack(np.concatenate([we[:, 4096:4160], we[:, 4096:4160]], 1)), pack(we[:, 3072:4096]),
                              pack(we[:, :3072])], 0)
    o["wi"] = np.ascontiguousarray(we[:, 4160:4176].reshape(8, 128, 16).transpose(1, 0, 2)).reshape(1, 128, 128)
    o["wq1"] = pack(g["w_in_odd"][0])
    for l in range(2):
        o[f"wo{l}"] = pack(g["w_o"][l])
        o[f"up{l}"] = pack(g["w_up"][l])
        o[f"dn{l}"] = np.concatenate([pack(g["w_down"][l][:1408]), pack(g["w_down"][l][1408:])], 0)
    o["wmod"] = pack(g["w_mod_2"][0])
    wi = g["w_in_2"][0]
    perm = np.concatenate([np.arange(h * 64, h * 64 + 64) for c in range(4) for h in (c, c + 4)])
    aq, bq = wi[:, :512][:, perm], wi[:, 768:1280][:, perm]
    o["win"] = pack(np.concatenate([aq, wi[:, 512:768], bq, wi[:, 1280:]], 1))
    wb = g["w_branch_2"][0]
    o["wbr"] = np.concatenate([pack(wb[0][perm]), pack(wb[1][perm]), pack(wb[2])], 0)
    o["wout"] = pack(g["w_out_2"][0])
    o["up2"] = pack(g["w_up_2"][0])
    o["dn2"] = np.concatenate([pack(g["w_down_2"][0][:1408]), pack(g["w_down_2"][0][1408:])], 0)
    return o


def kernel(**inputs):
    import concourse.bacc as _bacc
    from concourse.bass_utils import run_bass_kernel_spmd as _run

    nc = _bacc.Bacc("TRN2", target_bir_lowering=False, num_devices=1)
    arrays = lay(inputs)
    t = {k: nc.dram_tensor(f"in_{k}", v.shape, mybir.dt.from_np(v.dtype), kind="ExternalInput").ap()
         for k, v in arrays.items()}
    t["toep"] = nc.dram_tensor("toep", (32, TOEP), F, kind="Internal").ap()
    out = nc.dram_tensor("out_y", (128, KD, S), F, kind="ExternalOutput").ap()
    build(nc, t, out)
    r = _run(nc, [{f"in_{k}": v for k, v in arrays.items()}], core_ids=[0])
    y = r.results[0]["out_y"]
    return np.ascontiguousarray(y.transpose(2, 1, 0)).reshape(1, S, D)
```
